# Optimizing a Trainium2 kernel written in Bass

```python
import jax
import jax.numpy as jnp
from jax import lax
import numpy as np

D_MODEL = 1024
BATCH = 1
SEQ = 1024
DEPTH = 1
DEC_BATCH = 8
DEC_SEQ = 8
PAST_LEN = 1024
PAGE_SIZE = 128

HEAD_DIM = 64
NSA_HEADS = 8
NSA_KV_HEADS = 2
NSA_GROUP = NSA_HEADS // NSA_KV_HEADS
NSA_W = NSA_HEADS * HEAD_DIM
NSA_KV_W = NSA_KV_HEADS * HEAD_DIM
CMP_LEN = 32
CMP_STRIDE = 16
CMP_HID = 128
SLC_BLOCK = 64
SLC_TOPK = 16
WINDOW = 512
RET_HEADS = 4
RET_W = RET_HEADS * HEAD_DIM
RET_CHUNK = 64
MEM_HEADS = 4
MEM_W = MEM_HEADS * HEAD_DIM
N_MEM = 256
MIX_W = NSA_W + RET_W + MEM_W
IN_SIZES = (NSA_W, 2 * NSA_KV_W, 2 * NSA_KV_W, 2 * NSA_KV_W, 3 * NSA_HEADS, NSA_W, RET_W, RET_W, RET_W, RET_W, MEM_W, MEM_W)
IN_W = 2 * NSA_W + 6 * NSA_KV_W + 3 * NSA_HEADS + 4 * RET_W + 2 * MEM_W
Q_BLOCK = 128
ROPE_BASE = 10000.0
EPS = 1e-6
NEG_INF = -1e30
SCALE = HEAD_DIM ** -0.5

kernel_name = 'hymba_nsa_retention_decoder_step'

def rmsnorm(x, g):
    xf = x.astype(jnp.float32)
    y = xf * lax.rsqrt(jnp.mean(xf * xf, axis=-1, keepdims=True) + EPS)
    return (y * g.astype(jnp.float32)).astype(x.dtype)

def masked_softmax(s, mask):
    s = jnp.where(mask, s.astype(jnp.float32), NEG_INF)
    m = jnp.max(s, axis=-1, keepdims=True)
    e = jnp.where(mask, jnp.exp(s - m), 0.0)
    return e / jnp.maximum(jnp.sum(e, axis=-1, keepdims=True), 1e-30)

def rope(x, pos):
    half = HEAD_DIM // 2
    inv = ROPE_BASE ** (-jnp.arange(half, dtype=jnp.float32) / half)
    ang = pos.astype(jnp.float32)[:, None] * inv[None, :]
    cos = jnp.cos(ang)[None, :, None, :]
    sin = jnp.sin(ang)[None, :, None, :]
    xf = x.astype(jnp.float32)
    x1, x2 = xf[..., :half], xf[..., half:]
    return jnp.concatenate([x1 * cos - x2 * sin, x1 * sin + x2 * cos], axis=-1).astype(x.dtype)

def split_cols(h):
    cuts = np.cumsum(np.array(IN_SIZES))[:-1].tolist()
    return jnp.split(h, cuts, axis=-1)

def mixer_inputs(x, ln_g, w_in):
    B, T = x.shape[:2]
    h = rmsnorm(x, ln_g) @ w_in
    q_n, kv_c, kv_s, kv_w, g_n, z_n, q_r, k_r, v_r, z_r, q_m, z_m = split_cols(h)
    kvs = lambda a: a.reshape(B, T, 2, NSA_KV_HEADS, HEAD_DIM)
    heads = lambda a, n: a.reshape(B, T, n, HEAD_DIM)
    gates = jax.nn.sigmoid(g_n.astype(jnp.float32)).reshape(B, T, 3, NSA_KV_HEADS, NSA_GROUP, 1)
    return (heads(q_n, NSA_HEADS), kvs(kv_c), kvs(kv_s), kvs(kv_w), gates, z_n,
            heads(q_r, RET_HEADS), heads(k_r, RET_HEADS), heads(v_r, RET_HEADS), z_r,
            heads(q_m, MEM_HEADS), z_m)

def nsa_compress(kv, comp):
    pe, w1, b1, w2 = comp
    B, L = kv.shape[:2]
    nch = L // CMP_STRIDE
    ch = kv[:, :nch * CMP_STRIDE].reshape(B, nch, CMP_STRIDE, 2, NSA_KV_HEADS, HEAD_DIM)
    pe_r = pe.reshape(2, 2, CMP_STRIDE, HEAD_DIM)
    w1_r = w1.reshape(2, 2, CMP_STRIDE, HEAD_DIM, CMP_HID)
    pe_lo = pe_r[:, 0].transpose(1, 0, 2)[:, :, None, :]
    pe_hi = pe_r[:, 1].transpose(1, 0, 2)[:, :, None, :]
    lo = jnp.einsum('bcpvkd,vpdh->bcvkh', ch[:, :-1] + pe_lo, w1_r[:, 0])
    hi = jnp.einsum('bcpvkd,vpdh->bcvkh', ch[:, 1:] + pe_hi, w1_r[:, 1])
    h = jax.nn.gelu(lo + hi + b1[None, None, :, None, :])
    return jnp.einsum('bcvkh,vhd->bcvkd', h, w2)

def nsa_cmp_attend(q, t, kc, vc):
    nc = kc.shape[1]
    end = jnp.arange(nc) * CMP_STRIDE + CMP_LEN - 1
    s = jnp.einsum('bqkgd,bckd->bkgqc', q, kc) * SCALE
    p = masked_softmax(s, end[None, :] <= t[:, None])
    o = jnp.einsum('bkgqc,bckd->bqkgd', p.astype(vc.dtype), vc)
    return o, p.sum(axis=2)

def slc_importance(imp, nb):
    r = SLC_BLOCK // CMP_STRIDE
    need = r * nb + 1
    lead = [(0, 0)] * (imp.ndim - 1)
    pp = jnp.pad(imp, lead + [(1, 0)])
    cur = pp.shape[-1]
    if cur >= need:
        pp = pp[..., :need]
    else:
        pp = jnp.pad(pp, lead + [(0, need - cur)])
    return pp[..., :r * nb].reshape(pp.shape[:-1] + (nb, r)).sum(-1) + pp[..., r::r]

def gathered_attend(qb, kg, vg, mask):
    s = jnp.einsum('bqkgd,bkqsd->bkgqs', qb, kg) * SCALE
    p = masked_softmax(s, mask[:, :, None])
    return jnp.einsum('bkgqs,bkqsd->bqkgd', p.astype(vg.dtype), vg)

def window_attend(qb, t, kw, vw, kpos):
    s = jnp.einsum('bqkgd,bskd->bkgqs', qb, kw) * SCALE
    mask = (kpos[None, :] <= t[:, None]) & (kpos[None, :] > t[:, None] - WINDOW) & (kpos[None, :] >= 0)
    p = masked_softmax(s, mask)
    return jnp.einsum('bkgqs,bskd->bqkgd', p.astype(vw.dtype), vw)

def nsa_prompt(q, kv_c, kv_s, kv_w, gates, comp):
    B, T = q.shape[:2]
    nb = T // SLC_BLOCK
    k_top = min(SLC_TOPK, nb)
    kvc = nsa_compress(kv_c, comp)
    kc, vc = kvc[:, :, 0], kvc[:, :, 1]
    sel = kv_s.reshape(B, nb, SLC_BLOCK, 2, NSA_KV_HEADS, HEAD_DIM).transpose(3, 0, 4, 1, 2, 5)
    ks, vs = sel[0], sel[1]
    kw = jnp.pad(kv_w, ((0, 0), (WINDOW, 0), (0, 0), (0, 0), (0, 0)))
    qg = q.reshape(B, T, NSA_KV_HEADS, NSA_GROUP, HEAD_DIM)
    blk = jnp.arange(nb)
    bi = jnp.arange(B)[:, None, None]
    hi = jnp.arange(NSA_KV_HEADS)[None, :, None]

    def query_block(q0):
        qb = lax.dynamic_slice_in_dim(qg, q0, Q_BLOCK, axis=1)
        gb = lax.dynamic_slice_in_dim(gates, q0, Q_BLOCK, axis=1)
        t = q0 + jnp.arange(Q_BLOCK)
        o_c, imp = nsa_cmp_attend(qb, t, kc, vc)
        score = slc_importance(imp, nb)
        cur = (t // SLC_BLOCK)[:, None]
        forced = (blk[None, :] == 0) | (blk[None, :] == cur) | (blk[None, :] == cur - 1)
        valid = blk[None, :] * SLC_BLOCK <= t[:, None]
        score = jnp.where(forced, jnp.inf, jnp.where(valid, score, -jnp.inf))
        top_s, idx = lax.top_k(score, k_top)
        flat = idx.reshape(B, NSA_KV_HEADS, Q_BLOCK * k_top)
        kg = ks[bi, hi, flat].reshape(B, NSA_KV_HEADS, Q_BLOCK, k_top * SLC_BLOCK, HEAD_DIM)
        vg = vs[bi, hi, flat].reshape(B, NSA_KV_HEADS, Q_BLOCK, k_top * SLC_BLOCK, HEAD_DIM)
        kpos = (idx[..., None] * SLC_BLOCK + jnp.arange(SLC_BLOCK)).reshape(B, NSA_KV_HEADS, Q_BLOCK, k_top * SLC_BLOCK)
        ok = jnp.broadcast_to((top_s > -jnp.inf)[..., None], idx.shape + (SLC_BLOCK,)).reshape(kpos.shape)
        o_s = gathered_attend(qb, kg, vg, (kpos <= t[None, None, :, None]) & ok)
        wb = lax.dynamic_slice_in_dim(kw, q0, WINDOW + Q_BLOCK, axis=1)
        kpos_w = q0 - WINDOW + jnp.arange(WINDOW + Q_BLOCK)
        o_w = window_attend(qb, t, wb[:, :, 0], wb[:, :, 1], kpos_w)
        return gb[:, :, 0] * o_c + gb[:, :, 1] * o_s + gb[:, :, 2] * o_w

    o = lax.map(query_block, jnp.arange(0, T, Q_BLOCK))
    return o.transpose(1, 0, 2, 3, 4, 5).reshape(B, T, NSA_W)

def nsa_sample(q, kv_c, kv_s, kv_w, gates, comp, pool_cmp, pool_slc, win_buf, page_table):
    DB, S = q.shape[:2]
    t = PAST_LEN + jnp.arange(S)
    qg = q.reshape(DB, S, NSA_KV_HEADS, NSA_GROUP, HEAD_DIM)
    past_c = pool_cmp[page_table].reshape(DB, PAST_LEN, 2, NSA_KV_HEADS, HEAD_DIM)
    kvc = nsa_compress(jnp.concatenate([past_c, kv_c], axis=1), comp)
    o_c, imp = nsa_cmp_attend(qg, t, kvc[:, :, 0], kvc[:, :, 1])
    nbp = PAST_LEN // SLC_BLOCK
    score = slc_importance(imp, nbp)
    blk = jnp.arange(nbp)
    score = jnp.where((blk == 0) | (blk == nbp - 1), jnp.inf, score)
    k_top = min(SLC_TOPK - 1, nbp)
    _, idx = lax.top_k(score, k_top)
    bpp = PAGE_SIZE // SLC_BLOCK
    phys = page_table[jnp.arange(DB)[:, None, None, None], idx // bpp]
    rows = (idx % bpp)[..., None] * SLC_BLOCK + jnp.arange(SLC_BLOCK)
    hidx = jnp.arange(NSA_KV_HEADS)[None, :, None, None, None]
    g = pool_slc[phys[..., None], rows, :, hidx]
    nk = k_top * SLC_BLOCK
    kg = g[..., 0, :].reshape(DB, NSA_KV_HEADS, S, nk, HEAD_DIM)
    vg = g[..., 1, :].reshape(DB, NSA_KV_HEADS, S, nk, HEAD_DIM)
    k_new, v_new = kv_s[:, :, 0], kv_s[:, :, 1]
    s_past = jnp.einsum('bqkgd,bkqsd->bkgqs', qg, kg)
    s_new = jnp.einsum('bqkgd,bjkd->bkgqj', qg, k_new)
    s = jnp.concatenate([s_past, s_new], axis=-1) * SCALE
    causal = jnp.arange(S)[None, :] <= jnp.arange(S)[:, None]
    mask = jnp.concatenate([jnp.ones((S, nk), dtype=bool), causal], axis=-1)
    p = masked_softmax(s, mask)
    o_s = (jnp.einsum('bkgqs,bkqsd->bqkgd', p[..., :nk].astype(vg.dtype), vg)
           + jnp.einsum('bkgqj,bjkd->bqkgd', p[..., nk:].astype(v_new.dtype), v_new))
    buf = jnp.concatenate([win_buf, kv_w], axis=1)
    wb = win_buf.shape[1]
    kpos_w = PAST_LEN - wb + jnp.arange(wb + S)
    o_w = window_attend(qg, t, buf[:, :, 0], buf[:, :, 1], kpos_w)
    o = gates[:, :, 0] * o_c + gates[:, :, 1] * o_s + gates[:, :, 2] * o_w
    return o.reshape(DB, S, NSA_W), buf[:, S:]

def ret_log_decay():
    return jnp.log1p(-jnp.exp2(-5.0 - jnp.arange(RET_HEADS, dtype=jnp.float32)))

def retention_chunk(state, q, k, v, log_g):
    C = q.shape[1]
    n = jnp.arange(C, dtype=jnp.float32)
    diff = n[:, None] - n[None, :]
    dmat = jnp.where(diff >= 0, jnp.exp(log_g[:, None, None] * jnp.maximum(diff, 0.0)), 0.0)
    q = q * SCALE
    s = jnp.einsum('bnhd,bmhd->bhnm', q, k) * dmat[None]
    inner = jnp.einsum('bhnm,bmhe->bnhe', s, v)
    xi = jnp.exp(log_g[None, :] * (n[:, None] + 1.0))
    cross = jnp.einsum('bnhd,bhde->bnhe', q * xi[None, :, :, None], state)
    zeta = jnp.exp(log_g[None, :] * (C - 1.0 - n[:, None]))
    new_state = (jnp.exp(log_g * C)[None, :, None, None] * state
                 + jnp.einsum('bmhd,bmhe->bhde', k * zeta[None, :, :, None], v))
    return inner + cross, new_state

def head_groupnorm(o, g):
    mu = jnp.mean(o, axis=-1, keepdims=True)
    var = jnp.mean(jnp.square(o - mu), axis=-1, keepdims=True)
    y = (o - mu) * lax.rsqrt(var + EPS)
    return y.reshape(o.shape[:2] + (RET_W,)) * g.astype(jnp.float32)

def retention_prompt(q, k, v, pos, gn):
    B, T = q.shape[:2]
    q, k = rope(q, pos), rope(k, pos)
    log_g = ret_log_decay()
    nch = T // RET_CHUNK
    to_chunks = lambda a: a.astype(jnp.float32).reshape(B, nch, RET_CHUNK, RET_HEADS, HEAD_DIM).transpose(1, 0, 2, 3, 4)

    def step(st, qkv):
        o, st = retention_chunk(st, qkv[0], qkv[1], qkv[2], log_g)
        return st, o

    st0 = jnp.zeros((B, RET_HEADS, HEAD_DIM, HEAD_DIM), jnp.float32)
    st, o = lax.scan(step, st0, (to_chunks(q), to_chunks(k), to_chunks(v)))
    o = o.transpose(1, 0, 2, 3, 4).reshape(B, T, RET_HEADS, HEAD_DIM)
    return head_groupnorm(o, gn), st

def retention_sample(q, k, v, pos, state, gn):
    q, k = rope(q, pos), rope(k, pos)
    o, st = retention_chunk(state.astype(jnp.float32), q.astype(jnp.float32), k.astype(jnp.float32),
                            v.astype(jnp.float32), ret_log_decay())
    return head_groupnorm(o, gn), st

def mem_kv(mem, g, w):
    B = mem.shape[0]
    return (rmsnorm(mem, g) @ w).reshape(B, N_MEM, 2, MEM_HEADS, HEAD_DIM)

def mem_attend(q, mkv):
    s = jnp.einsum('bqhd,bmhd->bhqm', q, mkv[:, :, 0]) * SCALE
    p = jax.nn.softmax(s.astype(jnp.float32), axis=-1)
    return jnp.einsum('bhqm,bmhd->bqhd', p.astype(mkv.dtype), mkv[:, :, 1])

def finish(x, o_n, z_n, o_r, z_r, o_m, z_m, w_out):
    B, T = x.shape[:2]
    f32 = jnp.float32
    mix = jnp.concatenate([
        o_n.astype(f32) * jax.nn.silu(z_n.astype(f32)),
        o_r.astype(f32) * jax.nn.silu(z_r.astype(f32)),
        o_m.reshape(B, T, MEM_W).astype(f32) * jax.nn.silu(z_m.astype(f32)),
    ], axis=-1).astype(x.dtype)
    return x + mix @ w_out

def setup_inputs(seed: int = 0) -> dict:
    key = jax.random.key(seed)
    ks = jax.random.split(key, 24)
    f32 = jnp.float32
    nrm = lambda k, s, sc: jax.random.normal(k, s, f32) * sc
    n_pages = PAST_LEN // PAGE_SIZE
    n_used = DEC_BATCH * n_pages
    n_pool = n_used + n_used // 4
    wb = min(WINDOW, PAST_LEN)
    page_table = jax.random.permutation(ks[8], n_pool)[:n_used].reshape(DEC_BATCH, n_pages).astype(jnp.int32)
    return {
        'x_prompt': nrm(ks[0], (BATCH, SEQ, D_MODEL), 1.0),
        'mem_prompt': nrm(ks[1], (BATCH, N_MEM, D_MODEL), 1.0),
        'x_sample': nrm(ks[2], (DEC_BATCH, DEC_SEQ, D_MODEL), 1.0),
        'cache_nsa_cmp': nrm(ks[3], (DEPTH, n_pool, PAGE_SIZE, 2, NSA_KV_HEADS, HEAD_DIM), 1.0),
        'cache_nsa_slc': nrm(ks[4], (DEPTH, n_pool, PAGE_SIZE, 2, NSA_KV_HEADS, HEAD_DIM), 1.0),
        'cache_nsa_win': nrm(ks[5], (DEPTH, DEC_BATCH, wb, 2, NSA_KV_HEADS, HEAD_DIM), 1.0),
        'state_ret': nrm(ks[6], (DEPTH, DEC_BATCH, RET_HEADS, HEAD_DIM, HEAD_DIM), 1.0),
        'cache_mem': nrm(ks[7], (DEPTH, DEC_BATCH, N_MEM, 2, MEM_HEADS, HEAD_DIM), 1.0),
        'page_table': page_table,
        'ln_mix': 1.0 + nrm(ks[9], (DEPTH, D_MODEL), 0.05),
        'w_in': nrm(ks[10], (DEPTH, D_MODEL, IN_W), D_MODEL ** -0.5),
        'cmp_pe': nrm(ks[11], (DEPTH, 2, CMP_LEN, HEAD_DIM), 0.1),
        'cmp_w1': nrm(ks[12], (DEPTH, 2, CMP_LEN * HEAD_DIM, CMP_HID), (CMP_LEN * HEAD_DIM) ** -0.5),
        'cmp_b1': nrm(ks[13], (DEPTH, 2, CMP_HID), 0.02),
        'cmp_w2': nrm(ks[14], (DEPTH, 2, CMP_HID, HEAD_DIM), CMP_HID ** -0.5),
        'ret_gn': 1.0 + nrm(ks[15], (DEPTH, RET_W), 0.05),
        'ln_mem': 1.0 + nrm(ks[16], (DEPTH, D_MODEL), 0.05),
        'w_mem_kv': nrm(ks[17], (DEPTH, D_MODEL, 2 * MEM_W), D_MODEL ** -0.5),
        'w_out': nrm(ks[18], (DEPTH, MIX_W, D_MODEL), MIX_W ** -0.5),
        'ln_final': 1.0 + nrm(ks[19], (D_MODEL,), 0.05),
    }

def reference(x_prompt, mem_prompt, x_sample, cache_nsa_cmp, cache_nsa_slc, cache_nsa_win, state_ret, cache_mem,
              page_table, ln_mix, w_in, cmp_pe, cmp_w1, cmp_b1, cmp_w2, ret_gn, ln_mem, w_mem_kv, w_out, ln_final):
    xp, xs = x_prompt, x_sample
    T = xp.shape[1]
    S = xs.shape[1]
    pos_p = jnp.arange(T)
    pos_s = PAST_LEN + jnp.arange(S)
    cmp_p, cmp_s, slc_p, slc_s, win_p, win_s, ret_p, ret_s, mem_p = [], [], [], [], [], [], [], [], []
    for l in range(DEPTH):
        comp = (cmp_pe[l], cmp_w1[l], cmp_b1[l], cmp_w2[l])
        q_n, kv_c, kv_s, kv_w, g_n, z_n, q_r, k_r, v_r, z_r, q_m, z_m = mixer_inputs(xp, ln_mix[l], w_in[l])
        o_n = nsa_prompt(q_n, kv_c, kv_s, kv_w, g_n, comp)
        o_r, st_r = retention_prompt(q_r, k_r, v_r, pos_p, ret_gn[l])
        mkv = mem_kv(mem_prompt, ln_mem[l], w_mem_kv[l])
        o_m = mem_attend(q_m, mkv)
        xp = finish(xp, o_n, z_n, o_r, z_r, o_m, z_m, w_out[l])
        cmp_p.append(kv_c)
        slc_p.append(kv_s)
        win_p.append(kv_w[:, T - min(WINDOW, T):])
        ret_p.append(st_r)
        mem_p.append(mkv)
        q_n, kv_c, kv_s, kv_w, g_n, z_n, q_r, k_r, v_r, z_r, q_m, z_m = mixer_inputs(xs, ln_mix[l], w_in[l])
        o_n, new_win = nsa_sample(q_n, kv_c, kv_s, kv_w, g_n, comp, cache_nsa_cmp[l], cache_nsa_slc[l],
                                  cache_nsa_win[l], page_table)
        o_r, st_r = retention_sample(q_r, k_r, v_r, pos_s, state_ret[l], ret_gn[l])
        o_m = mem_attend(q_m, cache_mem[l])
        xs = finish(xs, o_n, z_n, o_r, z_r, o_m, z_m, w_out[l])
        cmp_s.append(kv_c)
        slc_s.append(kv_s)
        win_s.append(new_win)
        ret_s.append(st_r)
    y_prompt = rmsnorm(xp, ln_final)
    y_sample = rmsnorm(xs, ln_final)
    return (y_prompt, y_sample, jnp.stack(cmp_p), jnp.stack(cmp_s), jnp.stack(slc_p), jnp.stack(slc_s),
            jnp.stack(win_p), jnp.stack(win_s), jnp.stack(ret_p), jnp.stack(ret_s), jnp.stack(mem_p))


_drawn_inputs = setup_inputs


def setup_inputs(seed=0):
    import zlib

    import numpy as np

    out = dict(_drawn_inputs(seed))
    spreads = {}
    factors = {'cache_nsa_cmp': 2.764,
     'cache_nsa_slc': 4.878,
     'cmp_pe': 5.637,
     'cmp_b1': 8.0,
     'ret_gn': 4.299,
     'cache_mem': 3.24}
    for name, (base, spread) in spreads.items():
        noise = np.random.default_rng([zlib.crc32(name.encode()), seed]).standard_normal(out[name].shape)
        drawn = base * np.exp(spread * noise) if base else spread * noise
        out[name] = jnp.asarray(drawn.astype(out[name].dtype))
    for name, factor in factors.items():
        out[name] = (out[name] * factor).astype(out[name].dtype)
    return out
```

```python
import numpy as np
import concourse.bass as bass
from concourse import mybir

F32 = mybir.dt.float32
F32R = mybir.dt.float32r
BF16 = mybir.dt.bfloat16
I32 = mybir.dt.int32
ALU = mybir.AluOpType
ACT = mybir.ActivationFunctionType
AX = mybir.AxisListType

D = 1024
T = 1024
NDB, DS = 8, 8
NS_TOK = NDB * DS
PAST, PAGE, NPOOL = 1024, 128, 80
NPG = PAST // PAGE
HD = 64
QT = T // 128
NT = QT + 1
NM = 256
WIN = 512
INW = 3352
KT = D // 128
SCALE = HD ** -0.5
EPS = 1e-6
NEG = -1e30
C_QN, C_KVC, C_KVS, C_KVW, C_G, C_ZN, C_QR, C_ZR, C_QM, C_ZM = 0, 512, 768, 1024, 1280, 1304, 1816, 2584, 2840, 3096
CHUNKS = [(0, 512), (512, 512), (1024, 280), (1304, 512), (1816, 512), (2328, 512), (2840, 512), (0, 512)]
MEMJ = 7
LOG_G = np.log1p(-np.exp2(-5.0 - np.arange(4)))


def tile_rows(n):
    return NS_TOK if n == QT else 128


def tile_col(n):
    return 128 * n if n <= QT else T + NS_TOK + 128 * (n - NT)


def constants():
    f = np.float32
    c = {}
    c["c_ident"] = np.eye(128, dtype=f)
    q, k = np.arange(128)[:, None], np.arange(128)[None, :]
    causal = np.where(k > q, NEG, 0.0)
    tail = np.where(k <= q, NEG, 0.0)
    cmpm = [np.where((16 * np.arange(64)[None, :] + 31 <= 128 * i + q) & (np.arange(64)[None, :] < 63), 0.0, NEG) for i in range(QT)]
    r = np.arange(128)
    rb, rs = r // 64, r % 8
    new = []
    for p in range(4):
        j = np.arange(64)
        new.append(np.where((j[None, :] // 8 == 2 * p + rb[:, None]) & (j[None, :] % 8 <= rs[:, None]), 0.0, NEG))
    winh = np.where(np.arange(8)[None, :] <= rs[:, None], NEG, 0.0)
    c["c_mask"] = np.concatenate([causal, tail] + cmpm + new + [winh], axis=1).astype(f)
    half = HD // 2
    inv = (10000.0 ** (-np.arange(half) / half)).astype(f)
    pos = np.concatenate([np.arange(T), np.tile(PAST + np.arange(DS), NDB)])
    n = np.concatenate([np.arange(T) % 128, np.tile(np.arange(DS), NDB)]) + 1
    ang = pos.astype(f)[:, None] * inv[None, :]
    cs, sn = np.cos(ang).astype(np.float64), np.sin(ang).astype(np.float64)
    dq = SCALE * np.exp(LOG_G[None, :] * n[:, None])
    dk = np.exp(-LOG_G[None, :] * n[:, None])
    dd = np.concatenate([dq, dk], axis=1)
    c["c_rope"] = np.concatenate([(dd[:, :, None] * cs[:, None, :]).reshape(-1, 256), (dd[:, :, None] * sn[:, None, :]).reshape(-1, 256)], axis=1).astype(f)
    m_le_n = (q <= k).astype(f)
    same_b = (q // 8 == k // 8).astype(f)
    c["c_ret"] = np.concatenate([m_le_n, (m_le_n * same_b), (q // 64 == k // 64).astype(f)], axis=1).astype(f)
    hh = np.arange(128) // 64
    dec = [np.exp(LOG_G[2 * p + hh] * s) for s in (128, DS) for p in range(2)]
    selkv = [(r % 64 // 32 == v) for v in range(2)]
    selh = [(r % 32 // 8 == v) for v in range(4)]
    selb = [(r // 8 == v) for v in range(8)]
    c["c_col"] = np.stack(dec + selkv + selh + selb, axis=1).astype(f)
    c["c_sum"] = ((r[:, None] // 32 == r[None, :] // 32) & (rs[:, None] == rs[None, :])).astype(f)
    blk = np.tile(np.arange(14, dtype=f)[None, :] + 1, (128, 1))
    c["c_blk"] = blk
    return c


M_CAUSAL, M_TAIL, M_CMP, M_NEW, M_WINH = 0, 128, 256, 256 + 64 * QT, 256 + 64 * QT + 256
M_W = M_WINH + 8


class Region:

    def __init__(self, nc, at, tag):
        self.nc, self.at, self.tag = nc, at, tag

    def __call__(self, name, shape, dt=F32):
        size = int(np.prod(shape[1:])) * (2 if dt == BF16 else 4)
        t = self.nc.alloc_sbuf_tensor_at(self.tag + name, shape, dt, offset=self.at)
        self.at += (size + 31) // 32 * 32
        return t


class Link:

    def __init__(self, eng, sem):
        self.eng, self.sem, self.n = eng, sem, 0

    def do(self, ins):
        self.n += 1
        ins.then_inc(self.sem, 1)

    def wait(self):
        self.eng.wait_ge(self.sem, self.n)

    def step(self, ins):
        self.do(ins)
        self.wait()


def build(nc, io, stop="D"):
    order = "ABCRPSD"
    on = lambda s: order.index(s) <= order.index(stop)
    BASE = (nc.sbuf_base + 63) // 64 * 64
    LIMIT = nc.sbuf_usable_end
    sem = {}

    def S(name):
        if name not in sem:
            sem[name] = nc.alloc_semaphore(name)
        return sem[name]

    hD = nc.dram_tensor("h_scratch", [T + NS_TOK, INW], F32, kind="Internal").ap()
    oD = nc.dram_tensor("o_scratch", [NDB * 64, 3 * HD], F32, kind="Internal").ap()
    omD = nc.dram_tensor("om_scratch", [NDB * 32, HD], F32, kind="Internal").ap()

    x_rows = [io["x_prompt"][0, 128 * n:128 * n + 128, :] for n in range(QT)]
    x_rows += [io["x_sample"].rearrange("b s d -> (b s) d")]
    x_rows += [io["mem_prompt"][0, 128 * n:128 * n + 128, :] for n in range(2)]
    w_src = [io["w_in"][0, :, c:c + n] for c, n in CHUNKS[:MEMJ]] + [io["w_mem_kv"][0]]
    w_src += [io["w_out"][0, :, 512 * j:512 * j + 512] for j in range(2)]
    w_src = [w.rearrange("(k p) n -> p k n", p=128) for w in w_src]
    w_n = [n for _, n in CHUNKS] + [512, 512]
    new_mem = io["new_mem"][0, 0].rearrange("m a h d -> m (a h d)")

    fix = Region(nc, BASE, "f_")
    NCOL = T + NS_TOK + 2 * 128
    xhi = fix("xhi", [128, KT, NCOL], F32R)
    xlo = fix("xlo", [128, KT, NCOL], F32R)
    ident = fix("ident", [128, 128])
    identb = fix("identb", [128, 128], BF16)
    colc = fix("colc", [128, 18])
    KCs = fix("KCs", [128, NDB, 64])
    VC = fix("VC", [64, NDB + 1, 128])
    KCp = fix("KCp", [128, 2, 64], F32R)
    OC = fix("OC", [128, NT, 256])
    small = fix("small", [128, 160])
    pt = fix("pt", [1, NDB * NPG], I32)
    arena = fix.at

    ra = Region(nc, arena, "a_")
    wraw = [ra(f"wraw{i}", [128, 4, 512]) for i in range(2)]
    whi = [ra(f"whi{i}", [128, KT, 512], F32R) for i in range(2)]
    wlo = [ra(f"wlo{i}", [128, KT, 512], F32R) for i in range(2)]
    w_end = ra.at
    HST = 3
    hst = [ra(f"hst{i}", [128, 512]) for i in range(HST)]
    xraw = [ra(f"xraw{i}", [128, D]) for i in range(2)]
    xs = [ra("xs0", [128, D])]
    gb = ra("gb", [128, 2, D])
    assert ra.at <= LIMIT, (ra.at, LIMIT)

    psum = nc.alloc_psum_tensor("psum", [128, 8 * 512], F32)
    bank = lambda b, n=512: psum[:, 512 * b:512 * b + n]

    rc = Region(nc, arena, "c_")
    w1raw = rc("w1raw", [128, 2, 2, 8, 128])
    w1hi = rc("w1hi", [128, 2, 2, 8, 128], F32R)
    w1lo = rc("w1lo", [128, 2, 2, 8, 128], F32R)
    G = nc.alloc_sbuf_tensor_at("c_G", [128, 16, 2, 2, HD], F32, offset=arena)
    G2 = rc("G2", [128, 2, 2, 16, HD])
    cthi = [rc(f"cthi{i}", [128, 8, 258], F32R) for i in range(2)]
    ctlo = [rc(f"ctlo{i}", [128, 8, 258], F32R) for i in range(2)]
    hid = [rc(f"hid{i}", [128, 4, 64]) for i in range(2)]
    w2 = rc("w2", [128, 2, HD])
    pe_raw = rc("pe_raw", [32, 128])
    pe_t = rc("pe_t", [128, 32])
    b1 = rc("b1", [128, 2])
    assert rc.at <= LIMIT, (rc.at, LIMIT)

    rg = Region(nc, arena, "r_")
    retc = rg("retc", [128, 384])
    gnb = rg("gnb", [128, 256])
    rr = [rg(f"rr{i}", [128, 768]) for i in range(2)]
    rt = [rg(f"rt{i}", [128, 512]) for i in range(2)]
    ro = [rg(f"ro{i}", [128, 512]) for i in range(2)]
    rtmp = rg("rtmp", [128, 4, 8, 32])
    RT = [rg(f"RT{i}", [128, 4, 128]) for i in range(2)]
    AT = [rg(f"AT{i}", [128, 2, 2, 128]) for i in range(2)]
    BD = rg("BD", [128, 2, 128])
    BDs = rg("BDs", [128, NDB, 2, 128])
    NSt = rg("NSt", [128, NDB, 2, 128])
    QZ = rg("QZ", [128, 2, NDB, NS_TOK])
    KZ = rg("KZ", [NS_TOK, NDB, 256])
    kvt = rg("kvt", [128, 4, 128])
    rsq = rg("rsq", [128, 256])
    assert rg.at <= LIMIT, (rg.at, LIMIT)

    rp = Region(nc, arena, "p_")
    maskb = rp("maskb", [128, M_W], BF16)
    KS = rp("KS", [128, 2, 2, T], F32R)
    V = rp("V", [128, 2, QT, 128])
    KM = rp("KM", [128, 4, NM], F32R)
    VM = rp("VM", [128, 2, 256])
    split_at = rp.at
    QA = [rp(f"QA{i}", [128, 12, 128], F32R) for i in range(2)]
    QB = [rp(f"QB{i}", [128, 12, 128], F32R) for i in range(2)]
    rk = Region(nc, split_at, "pk_")
    Ktok = rk("Ktok", [128, 2, QT, 128])
    Kmt = rk("Kmt", [128, 2, 256])
    mraw = rk("mraw", [128, M_W])
    assert rk.at <= rp.at
    qd = [rp(f"qd{i}", [128, 12, 2, HD]) for i in range(2)]
    zt = [rp(f"zt{i}", [128, D]) for i in range(2)]
    gt = [rp(f"gt{i}", [128, 24]) for i in range(2)]
    P = [rp(f"P{i}", [128, T]) for i in range(2)]
    NPT = 2
    PTs = [rp(f"PT{i}", [128, 512]) for i in range(NPT)]
    Oi = rp("Oi", [128, 28, HD])
    mx = [rp(f"mx{i}", [128, D]) for i in range(2)]
    ssum = rp("ssum", [128, 2, 28])
    gw = rp("gw", [128, 2, 28])
    nb = rp("nb", [128, 4])
    mxv = rp("mxv", [128, 4])
    rw = rp("rw", [128, 2, 7])
    assert rp.at <= LIMIT, (rp.at, LIMIT)

    ru = Region(nc, split_at - (split_at - arena) + (2 * M_W + 31) // 32 * 32, "s_")
    s_at = ru.at
    SG = [ru(f"SG{i}", [128, 2, NPG, 256]) for i in range(2)]
    WG = [ru(f"WG{i}", [128, 2, 4, 256]) for i in range(2)]
    rm = Region(nc, s_at, "m_")
    MK = [rm(f"MK{i}", [128, 4, 2, 512]) for i in range(2)]
    KTm = rm("KTm", [128, 4, 2, NM])
    QM = rm("QM", [128, 2, NDB, 128])
    assert rm.at <= ru.at
    KTs = ru("KTs", [128, 2, PAST])
    KTw = ru("KTw", [128, 2, WIN])
    KTn = ru("KTn", [128, 2, NS_TOK])
    QP = ru("QP", [128, NDB, 128])
    PC = ru("PC", [128, 64])
    PW = ru("PW", [128, WIN + 64])
    PSl = ru("PSl", [128, PAST + 64])
    PM = ru("PM", [128, NM])
    PTS = ru("PTS", [128, 15, 128])
    qs = ru("qs", [NS_TOK, 4, 2, HD])
    qms = ru("qms", [NS_TOK, 256])
    kvn = ru("kvn", [NS_TOK, 512])
    csum = ru("csum", [128, 128])
    cblk = ru("cblk", [128, 14])
    zs = ru("zs", [NS_TOK, D])
    gs = ru("gs", [NS_TOK, 24])
    ms = ru("ms", [NS_TOK, D])
    on_s = ru("on_s", [NS_TOK, 8, 3, HD])
    om_s = ru("om_s", [NS_TOK, 4, HD])
    OMs = ru("OMs", [128, 2, HD])
    OSp = [ru(f"OSp{i}", [128, 3, HD]) for i in range(2)]
    pp = ru("pp", [128, 64])
    sc = ru("sc", [128, 3, 14])
    smx, snb, ssm, rs3 = ru("smx", [128, 10]), ru("snb", [128, 8]), ru("ssm", [128, 10]), ru("rs3", [128, 3])
    assert ru.at <= LIMIT, (ru.at, LIMIT)

    rd = Region(nc, w_end, "d_")
    gf = rd("gf", [128, D])
    xr = [rd(f"xr{i}", [128, D]) for i in range(2)]
    yt = [rd(f"yt{i}", [128, D]) for i in range(1)] * 2
    yo = [rd(f"yo{i}", [128, D]) for i in range(2)]
    assert rd.at <= LIMIT, (rd.at, LIMIT)

    proj_jobs = [(j, t) for j in range(MEMJ) for t in range(NT)] + [(MEMJ, NT), (MEMJ, NT + 1)]
    ACT_CHUNKS = (2, 3, 5, 6)

    def by_act(j):
        return j in ACT_CHUNKS

    def evac_count(q, act):
        return sum(by_act(j) == act for j, _ in proj_jobs[:q + 1])

    def wait_evac(eng, q):
        act = by_act(proj_jobs[q][0])
        eng.wait_ge(S("h_evac_act") if act else S("h_evac_dve"), evac_count(q, act))

    last_job = {}
    for q, (j, t) in enumerate(proj_jobs):
        last_job[j] = q

    def load_w(sp, j):
        for half in range(2):
            m = 2 * j + half
            if m >= 2:
                sp.wait_ge(S("w_split"), m - 1)
            sp.dma_start(wraw[m % 2][:, :, 0:w_n[j]], w_src[j][:, 4 * half:4 * half + 4, :]).then_inc(S(f"w_in{m % 2}"), 16)

    def split_w_hi(act, j):
        for half in range(2):
            m = 2 * j + half
            act.wait_ge(S(f"w_in{m % 2}"), 16 * (m // 2 + 1))
            if half == 0 and j >= 2:
                act.wait_ge(S("h_mm"), last_job[j - 2] + 1)
            nc.scalar.copy(whi[j % 2][:, 4 * half:4 * half + 4, 0:w_n[j]], wraw[m % 2][:, :, 0:w_n[j]]).then_inc(S("w_hi"), 1)

    def split_w_lo(dve, j):
        for half in range(2):
            m = 2 * j + half
            dve.wait_ge(S("w_hi"), m + 1)
            ks = slice(4 * half, 4 * half + 4)
            nc.vector.tensor_tensor(wlo[j % 2][:, ks, 0:w_n[j]], wraw[m % 2][:, :, 0:w_n[j]],
                                    whi[j % 2][:, ks, 0:w_n[j]].bitcast(F32), ALU.subtract).then_inc(S("w_split"), 1)

    def wait_h(eng):
        for i in range(HST):
            eng.wait_ge(S(f"h_out{i}"), 16 * len(range(i, len(proj_jobs), HST)))

    def mm3(out, jw, k, n, col, rows, first, last):
        hi, lo = xhi[:, k, col:col + rows], xlo[:, k, col:col + rows]
        wh, wl = whi[jw][:, k, 0:n], wlo[jw][:, k, 0:n]
        nc.tensor.matmul(out, hi, wh, start=first, stop=False)
        nc.tensor.matmul(out, hi, wl, start=False, stop=False)
        return nc.tensor.matmul(out, lo, wh, start=False, stop=last)

    def x_src(n, g):
        return bank((2 * n + g) % 4).rearrange("p (k c) -> p k c", k=4)[:, :, 0:tile_rows(n)]

    NITEM = NDB // 2 + 1
    NIDX = 2 * NITEM
    irows = lambda u: 128 if u < NDB // 2 else 64

    def sp_compress(sp):
        sp.wait_ge(S("h_mm"), len(proj_jobs))
        sp.dma_start(pe_raw[:], io["cmp_pe"][0].rearrange("v (l q) d -> (v l) (q d)", q=2)).then_inc(S("c_const"), 16)
        for v in range(2):
            sp.dma_start(b1[:, v:v + 1], io["cmp_b1"][0, v].rearrange("(h o) -> h o", o=1)).then_inc(S("c_const"), 16)
        sp.dma_start(w2[:], io["cmp_w2"][0].rearrange("v h d -> h v d")).then_inc(S("c_const"), 16)
        for v in range(2):
            sp.dma_start(w1raw[:, v], io["cmp_w1"][0, v].rearrange("(l k q) h -> q l k h", l=2, k=8)).then_inc(S("c_w1"), 16)
        sp.wait_ge(S("c_w1lo"), 4)
        sp.wait_ge(S("c_pe"), 2)
        for u in range(NITEM):
            if u >= 1:
                sp.wait_ge(S("c_regroup"), 4 * u)
            if u < NDB // 2:
                for j in range(2 * NPG):
                    page = sp.value_load(pt[0:1, 2 * NPG * u + j:2 * NPG * u + j + 1], min_val=0, max_val=NPOOL - 1)
                    sp.dma_start(G[8 * j:8 * j + 8].rearrange("c p a k d -> c (p a k d)"),
                                 io["cache_nsa_cmp"][0, bass.ds(page, 1)].rearrange("o (c p) a k d -> (o c) (p a k d)", p=16)).then_inc(S("g_in"), 16)
            else:
                sp.dma_start(G[0:64].rearrange("c p a k d -> c p (a k d)"),
                             hD[0:T, C_KVC:C_KVC + 256].rearrange("(c p) n -> c p n", p=16)).then_inc(S("g_in"), 16)

    def pool_compress(pool):
        wait_h(pool)
        pool.wait_ge(S("h_mm"), len(proj_jobs))
        for h in range(2):
            pool.memset(hid[h][:], 0.0).then_inc(S("c_zero"), 1)
            pool.memset(cthi[h][:, :, 256:258].bitcast(F32), 0.0).then_inc(S("c_zero"), 1)
            pool.memset(ctlo[h][:, :, 256:258].bitcast(F32), 0.0).then_inc(S("c_zero"), 1)
        for u in range(NITEM):
            r = irows(u)
            pool.wait_ge(S("g_in"), 16 * (2 * NPG * (u + 1) if u < NDB // 2 else NDB * NPG + 1))
            for v in range(2):
                if u >= 1:
                    pool.wait_ge(S("c_tr"), 4 * (2 * (u - 1) + v + 1))
                for k in range(2):
                    pool.tensor_copy(G2[0:r, v, k], G[0:r, :, v, k, :]).then_inc(S("c_regroup"), 1)

    def pe_compress(pe):
        pe.wait_ge(S("h_evac_act"), evac_count(len(proj_jobs) - 1, True))
        pe.wait_ge(S("h_evac_dve"), evac_count(len(proj_jobs) - 1, False))
        pe.wait_ge(S("c_const"), 16 * 4)
        nc.tensor.transpose(bank(7, 32), pe_raw[:], ident[0:32, 0:32]).then_inc(S("c_pe"), 1)
        pe.wait_ge(S("c_pet"), 1)
        pe.wait_ge(S("c_w1"), 32)
        for v in range(2):
            for i in range(16):
                l = nc.tensor.matmul(psum[:, 512 * 7 + 64 + v:512 * 7 + 65 + v], w1raw[:, v, i // 8, i % 8], pe_t[:, 16 * v + i:16 * v + i + 1],
                                     start=i == 0, stop=i == 15)
        l.then_inc(S("c_pe"), 1)

        def tr(idx):
            u, v = idx // 2, idx % 2
            r = irows(u)
            pe.wait_ge(S("c_regroup"), 4 * u + 2 * v + 2)
            for g in range(4):
                if idx >= 1:
                    pe.wait_ge(S("c_lo"), 4 * (idx - 1) + g + 1)
                for j in range(4):
                    kk, kv = 2 * g + j // 2, j % 2
                    l = nc.tensor.transpose(bank(g)[:, 128 * j:128 * j + r], G2[0:r, v, kv, 2 * kk:2 * kk + 2, :], ident[0:r, 0:r])
                l.then_inc(S("c_tr"), 1)

        def hidden(idx):
            u, v = idx // 2, idx % 2
            n = 2 * irows(u)
            if idx == 0:
                pe.wait_ge(S("c_w1lo"), 4)
                pe.wait_ge(S("c_zero"), 6)
            pe.wait_ge(S("c_lo"), 4 * idx + 4)
            if idx >= 2:
                pe.wait_ge(S("c_gelu"), idx - 1)
            out = bank(4 + idx % 2, n)
            ch, cl = cthi[idx % 2], ctlo[idx % 2]
            for l in range(2):
                for kk in range(8):
                    first, last = l == 0 and kk == 0, l == 1 and kk == 7
                    wh, wl = w1hi[:, v, l, kk], w1lo[:, v, l, kk]
                    nc.tensor.matmul(out, wh, ch[:, kk, l:l + n], start=first, stop=False)
                    nc.tensor.matmul(out, wh, cl[:, kk, l:l + n], start=False, stop=False)
                    i = nc.tensor.matmul(out, wl, ch[:, kk, l:l + n], start=False, stop=last)
            i.then_inc(S("c_mm"), 1)

        def second(idx):
            u, v = idx // 2, idx % 2
            pe.wait_ge(S("c_gelu"), idx + 1)
            if idx >= 2:
                pe.wait_ge(S("c_kv"), idx - 1)
            h = hid[idx % 2]
            nb = 2 if u < NDB // 2 else 1
            if idx == 1:
                pe.wait_ge(S("c_bias"), 2)
            if v == 0:
                for kv in range(2):
                    i = nc.tensor.matmul(psum[64 * kv:64 * kv + 64, 512 * 6:512 * 6 + 64 * nb], w2[:, 0], h[:, nb * kv:nb * kv + nb], start=True, stop=True)
            else:
                for kv in range(2):
                    for b in range(nb):
                        o = 512 * 7 + 128 * b + 64 * kv
                        i = nc.tensor.matmul(psum[0:64, o:o + 64], h[:, nb * kv + b], w2[:, 1], start=True, stop=True)
            i.then_inc(S("c_l2"), 1)

        tr(0)
        for idx in range(NIDX):
            if idx + 1 < NIDX:
                tr(idx + 1)
            hidden(idx)
            if idx >= 1:
                second(idx - 1)
        second(NIDX - 1)

    def ct_views(idx, g, dst):
        r = irows(idx // 2)
        return (dst[idx % 2][:, 2 * g:2 * g + 2, 0:2 * r].rearrange("p k (v c) -> p k v c", v=2),
                bank(g).rearrange("p (k v c) -> p k v c", k=2, v=2)[:, :, :, 0:r])

    def act_compress(act):
        act.wait_ge(S("c_w1"), 32)
        for i in range(4):
            nc.scalar.copy(w1hi[:, i // 2, i % 2], w1raw[:, i // 2, i % 2]).then_inc(S("c_w1hi"), 1)

        def hi(idx):
            if idx >= 2:
                act.wait_ge(S("c_mm"), idx - 1)
            for g in range(4):
                act.wait_ge(S("c_tr"), 4 * idx + g + 1)
                dst, src = ct_views(idx, g, cthi)
                nc.scalar.copy(dst, src).then_inc(S("c_hi"), 1)

        def gelu(idx):
            n = irows(idx // 2) // 32
            act.wait_ge(S("c_mm"), idx + 1)
            if idx >= 2:
                act.wait_ge(S("c_l2"), idx - 1)
            nc.scalar.activation(hid[idx % 2][:, 0:n, 0:63], bank(4 + idx % 2, 64 * n).rearrange("p (g c) -> p g c", c=64)[:, :, 0:63],
                                 ACT.Gelu_apprx_tanh, bias=small[:, 64 + idx % 2:65 + idx % 2]).then_inc(S("c_gelu"), 1)

        hi(0)
        act.wait_ge(S("c_bias"), 2)
        act.wait_ge(S("c_zero"), 6)
        for idx in range(NIDX):
            if idx + 1 < NIDX:
                hi(idx + 1)
            gelu(idx)
        act.wait_ge(S("c_l2"), NIDX - 1)
        for kv in range(2):
            rows = slice(64 * kv, 64 * kv + 64)
            nc.scalar.copy(KCp[rows, kv, :], psum[rows, 512 * 6:512 * 6 + 64]).then_inc(S("c_kcp_hi"), 1)

    def dve_compress(dve):
        dve.wait_ge(S("c_pe"), 1)
        nc.vector.tensor_copy(pe_t[:], bank(7, 32)).then_inc(S("c_pet"), 1)
        for i in range(4):
            dve.wait_ge(S("c_w1hi"), i + 1)
            nc.vector.tensor_tensor(w1lo[:, i // 2, i % 2], w1raw[:, i // 2, i % 2], w1hi[:, i // 2, i % 2].bitcast(F32), ALU.subtract).then_inc(S("c_w1lo"), 1)
        dve.wait_ge(S("c_pe"), 2)
        for v in range(2):
            nc.vector.tensor_tensor(small[:, 64 + v:65 + v], psum[:, 512 * 7 + 64 + v:512 * 7 + 65 + v], b1[:, v:v + 1], ALU.add).then_inc(S("c_bias"), 1)

        def lo(idx):
            for g in range(4):
                dve.wait_ge(S("c_hi"), 4 * idx + g + 1)
                dst, src = ct_views(idx, g, ctlo)
                hv, _ = ct_views(idx, g, cthi)
                nc.vector.tensor_tensor(dst, src, hv.bitcast(F32), ALU.subtract).then_inc(S("c_lo"), 1)

        def keep(idx):
            u, v = idx // 2, idx % 2
            dve.wait_ge(S("c_l2"), idx + 1)
            if u < NDB // 2:
                if v == 0:
                    i = nc.vector.tensor_copy(KCs[:, 2 * u:2 * u + 2, :], bank(6, 128))
                else:
                    i = nc.vector.tensor_copy(VC[:, 2 * u:2 * u + 2, :], psum[0:64, 512 * 7:512 * 7 + 256])
            elif v == 1:
                i = nc.vector.tensor_copy(VC[:, NDB, :], psum[0:64, 512 * 7:512 * 7 + 128])
            else:
                return
            i.then_inc(S("c_kv"), 1)

        lo(0)
        for idx in range(NIDX):
            if idx + 1 < NIDX:
                lo(idx + 1)
            if idx >= 1:
                keep(idx - 1)
        keep(NIDX - 1)
        dve.wait_ge(S("c_kcp_hi"), 2)
        for kv in range(2):
            rows, other = slice(64 * kv, 64 * kv + 64), slice(64 - 64 * kv, 128 - 64 * kv)
            nc.vector.tensor_tensor(KCp[other, kv, :], psum[rows, 512 * 6:512 * 6 + 64], KCp[rows, kv, :].bitcast(F32), ALU.subtract).then_inc(S("c_kv"), 1)

    N_CKV = NIDX - 1 + 2

    def sp_retention(sp):
        sp.wait_ge(S("c_kv"), N_CKV)
        sp.dma_start(retc[:], io["c_ret"]).then_inc(S("r_const"), 16)
        sp.dma_start(gnb[:], io["ret_gn"].to_broadcast([128, 256])).then_inc(S("r_const"), 16)
        for n in range(NT):
            if n >= 2:
                sp.wait_ge(S("r_use"), n - 1)
                sp.wait_ge(S("r_rope"), n - 1)
            r = tile_rows(n)
            sp.dma_start(rr[n % 2][0:r], hD[128 * n:128 * n + r, C_QR:C_QR + 768]).then_inc(S(f"r_in{n % 2}"), 16)
            sp.dma_start(rt[n % 2][0:r], io["c_rope"][128 * n:128 * n + r, :]).then_inc(S(f"r_in{n % 2}"), 16)
            if n == 1:
                sp.wait_ge(S("r_zero"), 2)
                for i in range(4):
                    pr, par = i // 2, i % 2
                    q = slice(64 * par, 64 * par + 64)
                    sp.dma_start(BDs[q, :, pr, q], io["state_ret"][0, :, 2 * pr + par].rearrange("b d e -> d b e")).then_inc(S("r_state"), 16)
        sp.wait_ge(S("r_bd"), QT)
        for par in range(2):
            q = slice(64 * par, 64 * par + 64)
            sp.dma_start(io["new_ret_p"][0, 0, par::2].rearrange("h d e -> d h e"), BD[q, :, q]).then_inc(S("out_done"), 16)
        sp.wait_ge(S("r_ns"), 4)
        for i in range(4):
            pr, par = i // 2, i % 2
            q = slice(64 * par, 64 * par + 64)
            sp.dma_start(io["new_ret_s"][0, :, 2 * pr + par].rearrange("b d e -> d b e"), NSt[q, :, pr, q]).then_inc(S("out_done"), 16)

    def pool_retention(pool):
        ch = Link(pool, S("r_pool"))
        pool.wait_ge(S("c_kv"), N_CKV)
        pool.memset(BDs[:], 0.0).then_inc(S("r_zero"), 1)
        pool.memset(QZ[:], 0.0).then_inc(S("r_zero"), 1)
        for n in range(NT):
            r = tile_rows(n)
            pool.wait_ge(S(f"r_in{n % 2}"), 32 * (n // 2 + 1))
            if n >= 2:
                pool.wait_ge(S("r_use"), n - 1)
            v = rr[n % 2][0:r, 0:512].rearrange("p (h t e) -> p h t e", h=8, t=2)
            o = ro[n % 2][0:r].rearrange("p (h t e) -> p h t e", h=8, t=2)
            cs = rt[n % 2][0:r, 0:256].rearrange("p (h e) -> p h e", h=8)
            sn = rt[n % 2][0:r, 256:512].rearrange("p (h e) -> p h e", h=8)
            if n >= 1:
                pool.wait_ge(S("r_rope"), n)
            for i, (x, w) in enumerate(((0, cs), (1, sn), (0, sn), (1, cs))):
                ch.do(pool.tensor_tensor(rtmp[0:r, i], v[:, :, x], w, ALU.mult))
            ch.wait()
            ch.do(pool.tensor_tensor(o[:, :, 0], rtmp[0:r, 0], rtmp[0:r, 1], ALU.subtract))
            pool.tensor_tensor(o[:, :, 1], rtmp[0:r, 2], rtmp[0:r, 3], ALU.add).then_inc(S("r_rope"), 1)
        pool.wait_ge(S("r_rt"), NT)
        for pr in range(2):
            for b in range(NDB):
                i = pool.tensor_copy(QZ[:, pr, b, DS * b:DS * b + DS], RT[QT % 2][:, pr, DS * b:DS * b + DS])
        i.then_inc(S("r_qz"), 1)
        pool.wait_ge(S("r_rope"), NT)
        for b in range(NDB):
            i = pool.tensor_scalar(KZ[:, b], ro[QT % 2][0:NS_TOK, 256:512], colc[0:NS_TOK, 10 + b:11 + b], None, ALU.mult)
        i.then_inc(S("r_qz"), 1)

    def pe_retention(pe):
        pe.wait_ge(S("c_kv"), N_CKV)

        def tr(n):
            r = tile_rows(n)
            pe.wait_ge(S("r_rope"), n + 1)
            if n >= 1:
                pe.wait_ge(S("r_rt"), n)
            for i in range(4):
                l = nc.tensor.transpose(bank(0)[:, 128 * i:128 * i + r], ro[n % 2][0:r, 128 * i:128 * i + 128], ident[0:r, 0:r])
            l.then_inc(S("r_tr"), 1)

        def scores(n):
            r = tile_rows(n)
            pe.wait_ge(S("r_rt"), n + 1)
            if n >= 1:
                pe.wait_ge(S("r_at"), 2 * n)
            for h in range(4):
                q = slice(64 * (h % 2), 64 * (h % 2) + 64)
                o = 512 * (1 + h % 2) + 128 * (h // 2)
                l = nc.tensor.matmul(psum[0:r, o:o + r], RT[n % 2][q, 2 + h // 2, 0:r], RT[n % 2][q, h // 2, 0:r], start=True, stop=True)
            l.then_inc(S("r_sc"), 1)

        def output(n):
            r = tile_rows(n)
            v = rr[n % 2]
            pe.wait_ge(S("r_at"), 2 * n + 2)
            if n >= 2:
                pe.wait_ge(S("r_o"), n - 1)
            o = 512 * (3 + n % 2)
            if n < QT:
                pe.wait_ge(S("r_bd"), n) if n else pe.wait_ge(S("r_bd0"), 1)
                for pr in range(2):
                    nc.tensor.matmul(psum[0:r, o + 128 * pr:o + 128 * pr + 128], RT[n % 2][:, pr, 0:r], BD[:, pr, :], start=pr == 0, stop=False, skip_group_check=True)
            else:
                pe.wait_ge(S("r_state"), 64)
                pe.wait_ge(S("r_qz"), 1)
                for pr in range(2):
                    for b in range(NDB):
                        nc.tensor.matmul(psum[0:r, o + 128 * pr:o + 128 * pr + 128], QZ[:, pr, b, :], BDs[:, b, pr, :], start=pr == 0 and b == 0, stop=False, skip_group_check=True)
            for h in range(4):
                l = nc.tensor.matmul(psum[0:r, o + 64 * h:o + 64 * h + 64], AT[n % 2][0:r, h % 2, h // 2, 0:r], v[0:r, 512 + 64 * h:576 + 64 * h], start=False, stop=True, skip_group_check=True)
            if n < QT:
                l.then_inc(S("r_out"), 1)
                if n >= 1:
                    pe.wait_ge(S("r_kvr"), n)
                for pr in range(2):
                    l = nc.tensor.matmul(psum[:, 512 * 5 + 128 * pr:512 * 5 + 128 * pr + 128], ro[n % 2][:, 256 + 128 * pr:384 + 128 * pr], v[:, 512 + 128 * pr:640 + 128 * pr], start=True, stop=True)
                l.then_inc(S("r_use"), 1)
            else:
                l.then_inc(S("r_out"), 1)
                pe.wait_ge(S("r_qz"), 2)
                pe.wait_ge(S("r_kvr"), QT)
                pe.wait_ge(S("r_at"), 2 * NT)
                for b in range(NDB):
                    for pr in range(2):
                        o2 = 512 * (1, 2, 5, 6)[b // 2] + 256 * (b % 2) + 128 * pr
                        l = nc.tensor.matmul(psum[:, o2:o2 + 128], KZ[:, b, 128 * pr:128 * pr + 128], v[0:r, 512 + 128 * pr:640 + 128 * pr], start=True, stop=True)
                l.then_inc(S("r_use"), 1)

        tr(0)
        scores(0)
        for n in range(NT):
            if n + 1 < NT:
                tr(n + 1)
            output(n)
            if n + 1 < NT:
                scores(n + 1)

    def act_retention(act):
        for n in range(NT):
            r = tile_rows(n)
            act.wait_ge(S("r_tr"), n + 1)
            if n >= 2:
                act.wait_ge(S("r_use"), n - 1)
            nc.scalar.copy(RT[n % 2][:, :, 0:r], bank(0).rearrange("p (i c) -> p i c", i=4)[:, :, 0:r]).then_inc(S("r_rt"), 1)
        act.wait_ge(S("r_ve"), 1)
        nc.scalar.activation(small[:, 116:152], small[:, 80:116], ACT.Sqrt).then_inc(S("r_sd"), 1)

    def dve_retention(dve):
        ch = Link(dve, S("r_dve"))
        ch.step(nc.vector.memset(small[:, 80:116], 1.0))
        nc.vector.memset(BD[:], 0.0).then_inc(S("r_bd0"), 1)
        dve.wait_ge(S("r_bd0"), 1)
        dve.wait_ge(S("r_const"), 32)

        def scores(n):
            r = tile_rows(n)
            mask = retc[0:r, (0 if n < QT else 128):(0 if n < QT else 128) + r]
            dve.wait_ge(S("r_sc"), n + 1)
            if n >= 2:
                dve.wait_ge(S("r_use"), n - 1)
            for par in range(2):
                for pr in range(2):
                    o = 512 * (1 + par) + 128 * pr
                    l = nc.vector.tensor_tensor(AT[n % 2][0:r, par, pr, 0:r], psum[0:r, o:o + r], mask, ALU.mult)
                l.then_inc(S("r_at"), 1)

        def norm(n):
            r = tile_rows(n)
            dve.wait_ge(S("r_out"), n + 1)
            o = psum[0:r, 512 * (3 + n % 2):512 * (3 + n % 2) + 256].rearrange("p (h e) -> p h e", h=4)
            oc = OC[0:r, n].rearrange("p (h e) -> p h e", h=4)
            mu, var = small[0:r, 152:156], small[0:r, 80 + 4 * n:84 + 4 * n]
            ch.step(nc.vector.tensor_reduce(out=mu, in_=o, op=ALU.add, axis=AX.X))
            ch.step(nc.vector.tensor_scalar(mu, mu, 1.0 / HD, None, ALU.mult))
            nc.vector.tensor_tensor(oc, o, mu.rearrange("p (h o) -> p h o", o=1).to_broadcast([r, 4, HD]), ALU.subtract).then_inc(S("r_o"), 1)
            dve.wait_ge(S("r_o"), n + 1)
            ch.step(nc.vector.tensor_tensor(rsq[0:r], OC[0:r, n], OC[0:r, n], ALU.mult))
            ch.step(nc.vector.tensor_reduce(out=var, in_=rsq[0:r].rearrange("p (h e) -> p h e", h=4), op=ALU.add, axis=AX.X))

        bdm = retc[:, 256:384]
        scores(0)
        for n in range(NT):
            norm(n)
            dve.wait_ge(S("r_use"), n + 1)
            if n < QT:
                for pr in range(2):
                    o = 512 * 5 + 128 * pr
                    l = nc.vector.tensor_tensor(kvt[:, pr], psum[:, o:o + 128], bdm, ALU.mult)
                l.then_inc(S("r_kvr"), 1)
                dve.wait_ge(S("r_kvr"), n + 1)
                ch.step(nc.vector.tensor_tensor(kvt[:, 0:2], kvt[:, 0:2], BD[:], ALU.add))
                nc.vector.tensor_scalar(BD[:, 0], kvt[:, 0], colc[:, 0:1], None, ALU.mult)
                nc.vector.tensor_scalar(BD[:, 1], kvt[:, 1], colc[:, 1:2], None, ALU.mult).then_inc(S("r_bd"), 1)
                dve.wait_ge(S("r_bd"), n + 1)
            else:
                for g in range(4):
                    o = 512 * (1, 2, 5, 6)[g]
                    for i in range(4):
                        ch.do(nc.vector.tensor_tensor(kvt[:, i], psum[:, o + 128 * i:o + 128 * i + 128], bdm, ALU.mult))
                    ch.wait()
                    ch.step(nc.vector.tensor_tensor(kvt[:], kvt[:], BDs[:, 2 * g:2 * g + 2].rearrange("p b r e -> p (b r) e"), ALU.add))
                    for pr in range(2):
                        l = nc.vector.tensor_scalar(NSt[:, 2 * g:2 * g + 2, pr], kvt[:].rearrange("p (b r) e -> p b r e", b=2)[:, :, pr], colc[:, 2 + pr:3 + pr], None, ALU.mult)
                    l.then_inc(S("r_ns"), 1)
                    dve.wait_ge(S("r_ns"), g + 1)
            if n + 1 < NT:
                scores(n + 1)
        v, sd, rs = small[:, 80:116], small[:, 116:152], small[:, 116:152]
        nc.vector.tensor_scalar(v, v, 1.0 / HD, EPS, ALU.mult, ALU.add).then_inc(S("r_ve"), 1)
        dve.wait_ge(S("r_sd"), 1)
        ch.step(nc.vector.reciprocal(rs, sd))
        rsqrt_polish(dve, ch, rs, v, small[:, 0:36])
        for n in range(NT):
            r = tile_rows(n)
            oc = OC[0:r, n].rearrange("p (h e) -> p h e", h=4)
            ch.step(nc.vector.tensor_tensor(oc, oc, rs[0:r, 4 * n:4 * n + 4].rearrange("p (h o) -> p h o", o=1).to_broadcast([r, 4, HD]), ALU.mult))
            nc.vector.tensor_tensor(OC[0:r, n], OC[0:r, n], gnb[0:r], ALU.mult).then_inc(S("r_done"), 1)

    def rsqrt_polish(dve, ch, y, v, tmp):
        ch.step(nc.vector.tensor_tensor(tmp, y, y, ALU.mult))
        ch.step(nc.vector.tensor_tensor(tmp, tmp, v, ALU.mult))
        ch.step(nc.vector.tensor_scalar(tmp, tmp, -0.5, 1.5, ALU.mult, ALU.add))
        ch.step(nc.vector.tensor_tensor(y, y, tmp, ALU.mult))

    UN = 28
    GRP = 7

    def unit(u):
        i, l = u // UN, u % UN
        if l >= 24:
            return i, l - 24, 3, 0, NM
        h, b = l // 3, l % 3
        if b == 2:
            return i, h, b, 0, 64
        k0 = 0 if b == 0 else max(0, i - WIN // 128)
        return i, h, b, k0, 128 * (i + 1 - k0)

    def prompt_schedule():
        chunks, steps, waiting = [], [], []

        def add(c):
            chunks.append(c)
            steps.append(("t", len(chunks) - 1))

        def pv():
            c = waiting.pop()
            steps.append(("pv", c))
            _, u, first, n = chunks[c]
            nk = (unit(u)[4] + 127) // 128
            if first + n == nk and u % GRP == GRP - 1:
                steps.append(("norm", u // GRP))

        for part in range(3):
            add(("q", 0, part))
        steps.append(("qk", 0))
        for u in range(UN * QT):
            i, l = u // UN, u % UN
            if u + 1 < UN * QT:
                steps.append(("qk", u + 1))
            nk = (unit(u)[4] + 127) // 128
            for first in range(0, nk, 4):
                add(("p", u, first, min(4, nk - first)))
                if waiting:
                    pv()
                waiting.append(len(chunks) - 1)
            if i >= 1 and l in (8, 10):
                add(("x", i - 1, (l - 8) // 2))
            if i + 1 < QT and l in (14, 17, 20):
                add(("q", i + 1, (l - 14) // 3))
        pv()
        for part in range(2):
            add(("x", QT - 1, part))
        return chunks, steps

    p_chunks, p_steps = prompt_schedule()

    def chunk_act(c):
        return p_chunks[c][0] == "p" and c % 2 == 0

    def chunks_before(c, test):
        return sum(test(k) for k in range(c))

    def wait_chunk_read(eng, c):
        if chunk_act(c):
            eng.wait_ge(S("pt_act"), chunks_before(c + 1, chunk_act))
        else:
            eng.wait_ge(S("pt_dve"), c + 1 - chunks_before(c + 1, chunk_act))

    p_index = [k for k, c in enumerate(p_chunks) if c[0] == "p"]
    p_rank = {c: n for n, c in enumerate(p_index)}
    last_chunk = {p_chunks[c][1]: c for c in p_index}
    q_last = {c[1]: k for k, c in enumerate(p_chunks) if c[0] == "q"}
    x_last = {c[1]: k for k, c in enumerate(p_chunks) if c[0] == "x"}
    split_rank = {c: n for n, c in enumerate([k for k, c in enumerate(p_chunks) if c[0] != "p"])}

    def s_view(u, t):
        n = unit(u)[4]
        base = 1024 * (u % 2)
        if n <= 512:
            return t[:, base:base + n]
        return t[:, base:base + 1024].rearrange("p (a b) -> p a b", a=2)[:, :, 0:n // 2]

    def sp_prompt(sp):
        sp.wait_ge(S("r_done"), NT)
        sp.wait_ge(S("out_done"), 16 * (7 + 2 + 4))
        sp.dma_start(mraw[:], io["c_mask"]).then_inc(S("p_const"), 16)
        for br, c in enumerate((C_KVS, C_KVW)):
            sp.dma_start(Ktok[:, br], hD[0:T, c:c + 128].rearrange("(t p) n -> p t n", p=128)).then_inc(S("p_const"), 16)
            sp.dma_start(V[:, br], hD[0:T, c + 128:c + 256].rearrange("(t p) n -> p t n", p=128)).then_inc(S("p_const"), 16)
        sp.dma_start(Kmt[:], new_mem[:, 0:256].rearrange("(t p) n -> p t n", p=128)).then_inc(S("p_const"), 16)
        sp.dma_start(VM[:], new_mem[:, 256:512].rearrange("(t p) n -> p t n", p=128)).then_inc(S("p_const"), 16)
        for i in range(QT):
            rows = slice(128 * i, 128 * i + 128)
            if i >= 2:
                sp.wait_ge(S("p_tr"), q_last[i - 2] + 1)
            for j in range(2):
                sp.dma_start(qd[i % 2][:, 0:8, j, :], hD[rows, 0:512].rearrange("p (h d) -> p h d", d=HD)).then_inc(S(f"p_q{i % 2}"), 16)
                sp.dma_start(qd[i % 2][:, 8:12, j, :], hD[rows, C_QM:C_QM + 256].rearrange("p (h d) -> p h d", d=HD)).then_inc(S(f"p_q{i % 2}"), 16)
            if i >= 2:
                sp.wait_ge(S("p_norm"), 4 * (i - 1))
                sp.wait_ge(S("p_mix"), i - 1)
            sp.dma_start(gt[i % 2][:], hD[rows, C_G:C_G + 24]).then_inc(S(f"p_g{i % 2}"), 16)
            for o, c, n in ((0, C_ZN, 512), (512, C_ZR, 256), (768, C_ZM, 256)):
                sp.dma_start(zt[i % 2][:, o:o + n], hD[rows, c:c + n]).then_inc(S(f"p_z{i % 2}"), 16)

    def pe_prompt(pe):
        pe.wait_ge(S("r_done"), NT)
        pe.wait_ge(S("p_const"), 16 * 7)
        for br in range(2):
            for half in range(2):
                for j in range(4):
                    l = nc.tensor.transpose(bank(2 * br + half)[:, 128 * j:128 * j + 128], Ktok[:, br, 4 * half + j, :], ident[:])
                l.then_inc(S("p_ktr"), 1)
        for pr in range(2):
            for mt in range(2):
                l = nc.tensor.transpose(bank(4)[:, 256 * pr + 128 * mt:256 * pr + 128 * mt + 128], Kmt[:, mt, 128 * pr:128 * pr + 128], ident[:])
        l.then_inc(S("p_ktr"), 1)
        pe.wait_ge(S("p_klo"), 10)
        pe.wait_ge(S("p_maskb"), 1)

        def qk(u):
            i, h, b, k0, n = unit(u)
            if u % UN == 0:
                pe.wait_ge(S("pt_dve"), chunks_final_dve(q_last[i]))
            if u >= 2:
                pe.wait_ge(S("p_exp"), u - 1)
            hq = h if b < 3 else 8 + h
            base = 1024 * (u % 2)
            halves = 1 if n <= 512 else 2
            w = n // halves
            for a in range(halves):
                o = psum[:, base + 512 * a:base + 512 * a + w]
                keys = slice(128 * k0 + w * a, 128 * k0 + w * a + w)
                k = KM[:, h, keys] if b == 3 else KCp[:, h // 4, :] if b == 2 else KS[:, b, h // 4, keys]
                masks = []
                if b == 2:
                    masks.append((o, M_CMP + 64 * i))
                if b == 1 and i >= WIN // 128 and a == 0:
                    masks.append((o[:, 0:128], M_TAIL))
                if b < 2 and a == halves - 1:
                    masks.append((o[:, w - 128:w], M_CAUSAL))
                nc.tensor.matmul(o, QA[i % 2][:, hq, :], k, start=True, stop=False)
                l = nc.tensor.matmul(o, QB[i % 2][:, hq, :], k, start=False, stop=not masks)
                for n_m, (om, at) in enumerate(masks):
                    l = nc.tensor.matmul(om, identb[:], maskb[:, at:at + om.shape[1]], start=False, stop=n_m == len(masks) - 1)
            l.then_inc(S("p_qk"), 1)

        def transposes(c):
            kind = p_chunks[c]
            if c >= 2:
                wait_chunk_read(pe, c - 2)
            o = bank(4 + c % 2)
            if kind[0] == "p":
                _, u, first, n = kind
                pe.wait_ge(S("p_exp"), u + 1)
                w = min(128, unit(u)[4])
                for j in range(n):
                    l = nc.tensor.transpose(o[0:w, 128 * j:128 * j + 128], P[u % 2][:, 128 * (first + j):128 * (first + j) + w], ident[:])
            elif kind[0] == "q":
                _, i, part = kind
                pe.wait_ge(S(f"p_q{i % 2}"), 64 * (i // 2 + 1))
                for j in range(4):
                    l = nc.tensor.transpose(o[:, 128 * j:128 * j + 128], qd[i % 2][:, 4 * part + j], ident[:])
            else:
                _, i, part = kind
                pe.wait_ge(S("p_mix"), i + 1)
                for j in range(4):
                    l = nc.tensor.transpose(o[:, 128 * j:128 * j + 128], mx[i % 2][:, 512 * part + 128 * j:512 * part + 128 * j + 128], ident[:])
            l.then_inc(S("p_tr"), 1)

        def pv(c):
            _, u, first, n = p_chunks[c]
            i, h, b, k0, keys = unit(u)
            wait_chunk_read(pe, c)
            if first == 0 and u % GRP == 0 and u >= 2 * GRP:
                pe.wait_ge(S("p_norm"), u // GRP - 1)
            nk = (keys + 127) // 128
            o = psum[:, 512 * (6 + u // GRP % 2) + HD * (u % GRP):512 * (6 + u // GRP % 2) + HD * (u % GRP) + HD]
            for j in range(n):
                k = first + j
                if b == 3:
                    v = VM[:, k, HD * h:HD * h + HD]
                elif b == 2:
                    v = VC[:, NDB, HD * (h // 4):HD * (h // 4) + HD]
                else:
                    v = V[:, b, k0 + k, HD * (h // 4):HD * (h // 4) + HD]
                w = min(128, keys)
                l = nc.tensor.matmul(o, PTs[p_rank[c] % NPT][0:w, 128 * j:128 * j + 128], v, start=k == 0, stop=k == nk - 1)
            l.then_inc(S("p_pv"), 1)

        for what, n in p_steps:
            if what == "qk":
                qk(n)
            elif what == "t":
                transposes(n)
            elif what == "pv":
                pv(n)

    def chunks_final_dve(c):
        return c + 1 - chunks_before(c + 1, chunk_act)

    def pt_copy(eng, copy, c, sem):
        _, u, _, n = p_chunks[c]
        w = min(128, unit(u)[4])
        r = p_rank[c]
        eng.wait_ge(S("p_tr"), c + 1)
        if r >= NPT:
            eng.wait_ge(S("p_pv"), r - NPT + 1)
        copy(PTs[r % NPT][0:w, 0:128 * n], bank(4 + c % 2)[0:w, 0:128 * n]).then_inc(sem, 1)

    def split_dst(c, lo):
        kind, i, part = p_chunks[c]
        if kind == "q":
            return (QB if lo else QA)[i % 2][:, 4 * part:4 * part + 4, :]
        return (xlo if lo else xhi)[:, 4 * part:4 * part + 4, tile_col(i):tile_col(i) + 128]

    def act_prompt(act):
        for n in range(4):
            br, half = n // 2, n % 2
            act.wait_ge(S("p_ktr"), n + 1)
            for kv in range(2):
                rows = slice(64 * kv, 64 * kv + 64)
                nc.scalar.copy(KS[rows, br, kv, 512 * half:512 * half + 512], psum[rows, 512 * n:512 * n + 512]).then_inc(S("p_khi"), 1)
        act.wait_ge(S("p_ktr"), 5)
        for par in range(2):
            rows = slice(64 * par, 64 * par + 64)
            nc.scalar.copy(KM[rows, par::2, :], psum[rows, 2048:2560].rearrange("p (h m) -> p h m", h=2)).then_inc(S("p_khi"), 1)
        for what, n in p_steps:
            if what == "qk":
                u, i = n, n // UN
                act.wait_ge(S("p_nb"), u + 1)
                if u >= 2:
                    act.wait_ge(S("p_tr"), last_chunk[u - 2] + 1)
                if u % UN == 0 and i >= 2:
                    act.wait_ge(S("p_norm"), 4 * (i - 1))
                keys = unit(u)[4]
                dst = P[u % 2][:, 0:keys]
                if keys > 512:
                    dst = dst.rearrange("p (a b) -> p a b", a=2)
                nc.scalar.activation(dst, s_view(u, psum), ACT.Exp, bias=nb[:, u % 4:u % 4 + 1], scale=SCALE,
                                     accum_out=ssum[:, i % 2, u % UN:u % UN + 1]).then_inc(S("p_exp"), 1)
            elif what == "t":
                if p_chunks[n][0] != "p":
                    kind, i, part = p_chunks[n]
                    act.wait_ge(S("p_tr"), n + 1)
                    if kind == "q" and i >= 2:
                        act.wait_ge(S("p_qk"), UN * (i - 1))
                    nc.scalar.copy(split_dst(n, False), bank(4 + n % 2).rearrange("p (j c) -> p j c", j=4)).then_inc(S("p_shi"), 1)
                elif chunk_act(n):
                    pt_copy(act, nc.scalar.copy, n, S("pt_act"))

    def dve_prompt(dve):
        ch = Link(dve, S("p_dve"))
        for n in range(4):
            br, half = n // 2, n % 2
            for kv in range(2):
                rows, other = slice(64 * kv, 64 * kv + 64), slice(64 - 64 * kv, 128 - 64 * kv)
                ks = slice(512 * half, 512 * half + 512)
                dve.wait_ge(S("p_khi"), 2 * n + kv + 1)
                nc.vector.tensor_tensor(KS[other, br, kv, ks], psum[rows, 512 * n:512 * n + 512], KS[rows, br, kv, ks].bitcast(F32), ALU.subtract).then_inc(S("p_klo"), 1)
        for par in range(2):
            rows, other = slice(64 * par, 64 * par + 64), slice(64 - 64 * par, 128 - 64 * par)
            dve.wait_ge(S("p_khi"), 9 + par)
            nc.vector.tensor_tensor(KM[other, par::2, :], psum[rows, 2048:2560].rearrange("p (h m) -> p h m", h=2), KM[rows, par::2, :].bitcast(F32), ALU.subtract).then_inc(S("p_klo"), 1)
        nc.vector.tensor_copy(maskb[:], mraw[:]).then_inc(S("p_maskb"), 1)
        ch.step(nc.vector.memset(gw[:, :, 24:28], 1.0))
        for what, n in p_steps:
            if what == "qk":
                u, i = n, n // UN
                if u % UN == 0:
                    dve.wait_ge(S(f"p_g{i % 2}"), 16 * (i // 2 + 1))
                    g = gt[i % 2][:].rearrange("p (b h) -> p h b", b=3)
                    w = gw[:, i % 2, 0:24].rearrange("p (h b) -> p h b", b=3)
                    ch.do(nc.vector.tensor_copy(w[:, :, 0:2], g[:, :, 1:3]))
                    ch.do(nc.vector.tensor_copy(w[:, :, 2], g[:, :, 0]))
                    ch.wait()
                dve.wait_ge(S("p_qk"), u + 1)
                sv = s_view(u, psum)
                if u >= 4:
                    dve.wait_ge(S("p_nb"), u - 3)
                ch.step(nc.vector.tensor_reduce(out=mxv[:, u % 4:u % 4 + 1], in_=sv, op=ALU.max, axis=AX.X if unit(u)[4] <= 512 else AX.XY))
                if u >= 4:
                    dve.wait_ge(S("p_exp"), u - 3)
                nc.vector.tensor_scalar(nb[:, u % 4:u % 4 + 1], mxv[:, u % 4:u % 4 + 1], NEG / 10, -SCALE, ALU.max, ALU.mult).then_inc(S("p_nb"), 1)
            elif what == "t":
                if p_chunks[n][0] != "p":
                    dve.wait_ge(S("p_shi"), split_rank[n] + 1)
                    nc.vector.tensor_tensor(split_dst(n, True), bank(4 + n % 2).rearrange("p (j c) -> p j c", j=4), split_dst(n, False).bitcast(F32), ALU.subtract).then_inc(S("pt_dve"), 1)
                elif not chunk_act(n):
                    pt_copy(dve, nc.vector.tensor_copy, n, S("pt_dve"))
            elif what == "norm":
                i, g = n // 4, n % 4
                us = slice(GRP * g, GRP * g + GRP)
                w = rw[:, n % 2]
                if n >= 2:
                    dve.wait_ge(S("p_norm"), n - 1)
                ch.step(nc.vector.tensor_scalar(w, ssum[:, i % 2, us], 1e-30, None, ALU.max))
                ch.step(nc.vector.reciprocal(w, w))
                ch.step(nc.vector.tensor_tensor(w, w, gw[:, i % 2, us], ALU.mult))
                dve.wait_ge(S("p_pv"), p_rank[last_chunk[GRP * n + GRP - 1]] + 1)
                if g == 0 and i >= 1:
                    dve.wait_ge(S("p_mix"), i)
                nc.vector.tensor_tensor(Oi[:, us, :], bank(6 + n % 2, GRP * HD).rearrange("p (u d) -> p u d", d=HD),
                                        w.rearrange("p (u o) -> p u o", o=1).to_broadcast([128, GRP, HD]), ALU.mult).then_inc(S("p_norm"), 1)

    def pool_mix(pool, ch, r, on, om, oc, z, m, done):
        mn = m[0:r, 0:512].rearrange("p (h d) -> p h d", d=HD)
        ch.do(pool.tensor_tensor(m[0:r, 512:768], oc, z[0:r, 512:768], ALU.mult))
        ch.do(pool.tensor_tensor(m[0:r, 768:1024].rearrange("p (h d) -> p h d", d=HD), om, z[0:r, 768:1024].rearrange("p (h d) -> p h d", d=HD), ALU.mult))
        ch.step(pool.tensor_tensor(mn, on[:, :, 0], on[:, :, 1], ALU.add))
        ch.step(pool.tensor_tensor(mn, mn, on[:, :, 2], ALU.add))
        pool.tensor_tensor(m[0:r, 0:512], m[0:r, 0:512], z[0:r, 0:512], ALU.mult).then_inc(S(done), 1)

    def pool_prompt(pool):
        ch = Link(pool, S("p_pool"))
        for i in range(QT):
            pool.wait_ge(S("p_norm"), 4 * (i + 1))
            pool.wait_ge(S(f"p_z{i % 2}"), 48 * (i // 2 + 1))
            if i >= 2:
                pool.wait_ge(S("p_tr"), x_last[i - 2] + 1)
            pool_mix(pool, ch, 128, Oi[:, 0:24].rearrange("p (h b) d -> p h b d", b=3), Oi[:, 24:28], OC[:, i], zt[i % 2], mx[i % 2], "p_mix")

    NPAIR = NDB // 2
    T_NEWS, T_NEWW, T_CMP = 12, 13, 14
    S_CHUNKS = [[(0, 128), (1, 128), (2, 128), (3, 128)], [(4, 128), (5, 128), (6, 128), (7, 128)],
                [(8, 128), (9, 128), (10, 128), (11, 128)], [(T_NEWS, 64), (T_NEWW, 64), (T_CMP, 63)]]
    NSC = len(S_CHUNKS)
    P_DONE = UN * QT // GRP

    def sp_sample(sp):
        sp.wait_ge(S("p_mix"), QT)
        sp.wait_ge(S("p_tr"), len(p_chunks))
        sp.wait_ge(S("p_pv"), len(p_index))
        sp.wait_ge(S("p_norm"), P_DONE)
        rows = hD[T:T + NS_TOK, :]
        for kv in range(2):
            sp.dma_start(qs[:, :, kv, :], rows[:, 256 * kv:256 * kv + 256].rearrange("p (g d) -> p g d", g=4)).then_inc(S("s_const"), 16)
        sp.dma_start(qms[:], rows[:, C_QM:C_QM + 256]).then_inc(S("s_const"), 16)
        sp.dma_start(kvn[:], rows[:, C_KVS:C_KVS + 512]).then_inc(S("s_const"), 16)
        sp.dma_start(csum[:], io["c_sum"]).then_inc(S("s_const"), 16)
        sp.dma_start(cblk[:], io["c_blk"]).then_inc(S("s_const"), 16)
        for b in range(NDB):
            sp.dma_start(MK[b // 4][:, b % 4], io["cache_mem"][0, b].rearrange("(t p) a h d -> p t (a h d)", p=128)).then_inc(S(f"m_in{b // 4}"), 16)
        for n, (o, c, w) in enumerate(((0, C_ZN, 512), (512, C_ZR, 256), (768, C_ZM, 256))):
            sp.dma_start(zs[:, o:o + w], rows[:, c:c + w]).then_inc(S("s_z"), 16)
        sp.dma_start(gs[:], rows[:, C_G:C_G + 24]).then_inc(S("s_z"), 16)
        for p in range(NPAIR):
            if p < 2:
                sp.wait_ge(S("m_pv"), 2)
            else:
                sp.wait_ge(S("s_pv"), p - 1)
            for j in range(2 * NPG):
                page = sp.value_load(pt[0:1, 2 * NPG * p + j:2 * NPG * p + j + 1], min_val=0, max_val=NPOOL - 1)
                sp.dma_start(SG[p % 2][:, j // NPG, j % NPG, :], io["cache_nsa_slc"][0, bass.ds(page, 1)].rearrange("o t a k d -> (o t) (a k d)")).then_inc(S(f"s_in{p % 2}"), 16)
            for b in range(2):
                sp.dma_start(WG[p % 2][:, b], io["cache_nsa_win"][0, 2 * p + b].rearrange("(t p) a k d -> p t (a k d)", p=128)).then_inc(S(f"s_in{p % 2}"), 16)
            if p >= 1:
                store_pair(sp, p - 1)
            if p == 1:
                for g in range(2):
                    sp.wait_ge(S("m_o"), g + 1)
                    sp.dma_start(omD[128 * g:128 * g + 128, :], OMs[:, g, :]).then_inc(S("o_out"), 16)
        store_pair(sp, NPAIR - 1)
        sp.wait_ge(S("o_out"), 16 * (NPAIR + 2))
        for b in range(NDB):
            sp.dma_start(on_s[DS * b:DS * b + DS], oD[64 * b:64 * b + 64, :].rearrange("(h s) (r d) -> s h r d", s=DS, d=HD)).then_inc(S("on_in"), 16)
            sp.dma_start(om_s[DS * b:DS * b + DS], omD[32 * b:32 * b + 32, :].rearrange("(h s) d -> s h d", s=DS)).then_inc(S("on_in"), 16)

    def store_pair(sp, p):
        sp.wait_ge(S("s_o"), p + 1)
        sp.dma_start(oD[128 * p:128 * p + 128, :], OSp[p % 2][:].rearrange("p r d -> p (r d)")).then_inc(S("o_out"), 16)

    def pool_sample(pool):
        ch = Link(pool, S("s_pool"))
        pool.wait_ge(S("p_tr"), len(p_chunks))
        pool.wait_ge(S("p_pv"), len(p_index))
        pool.wait_ge(S("p_norm"), P_DONE)
        pool.wait_ge(S("p_mix"), QT)
        pool.memset(QP[:], 0.0).then_inc(S("s_zero"), 1)
        pool.memset(QM[:], 0.0).then_inc(S("s_zero"), 1)
        pool.memset(pp[:], 0.0).then_inc(S("s_zero"), 1)
        pool.memset(rs3[:], 1.0).then_inc(S("s_zero"), 1)
        pool.wait_ge(S("on_in"), 16 * 2 * NDB)
        pool.wait_ge(S("s_z"), 64)
        g = gs[:].rearrange("p (r h o) -> p h r o", r=3, o=1).to_broadcast([NS_TOK, 8, 3, HD])
        ch.step(pool.tensor_tensor(on_s[:], on_s[:], g, ALU.mult))
        pool_mix(pool, ch, NS_TOK, on_s, om_s[:], OC[0:NS_TOK, QT], zs, ms, "s_mix")

    def pe_sample(pe):
        pe.wait_ge(S("s_const"), 96)
        pe.wait_ge(S("pt_dve"), chunks_final_dve(len(p_chunks) - 1))
        pe.wait_ge(S("pt_act"), chunks_before(len(p_chunks), chunk_act))
        pe.wait_ge(S("p_exp"), UN * QT)
        pe.wait_ge(S("p_norm"), P_DONE)
        for g in range(4):
            l = nc.tensor.transpose(bank(0)[:, 64 * g:64 * g + 64], qs[:, g], ident[0:64, 0:64])
        for pr in range(2):
            l = nc.tensor.transpose(bank(1)[:, 64 * pr:64 * pr + 64], qms[:, 128 * pr:128 * pr + 128], ident[0:64, 0:64])
        for br in range(2):
            l = nc.tensor.transpose(bank(1)[:, 128 + 64 * br:192 + 64 * br], kvn[:, 256 * br:256 * br + 128], ident[0:64, 0:64])
        l.then_inc(S("s_qtr"), 1)

        def m_keys(b):
            pe.wait_ge(S(f"m_in{b // 4}"), 64)
            if b >= 2:
                pe.wait_ge(S("m_kt"), b - 1)
            for pr in range(2):
                for mt in range(2):
                    l = nc.tensor.transpose(bank(2 + b % 2)[:, 256 * pr + 128 * mt:256 * pr + 128 * mt + 128], MK[b // 4][:, b % 4, mt, 128 * pr:128 * pr + 128], ident[:])
            l.then_inc(S("m_ktr"), 1)

        for g in range(2):
            for b in range(4 * g, 4 * g + 4):
                m_keys(b)
            pe.wait_ge(S("s_q"), 1)
            pe.wait_ge(S("m_kt"), 4 * g + 4)
            for b in range(4 * g, 4 * g + 4):
                for pr in range(2):
                    l = nc.tensor.matmul(bank(4 + g, 256), QM[:, pr, b, :], KTm[:, b % 4, pr, :], start=b == 4 * g and pr == 0, stop=b == 4 * g + 3 and pr == 1)
            l.then_inc(S("m_qk"), 1)
            pe.wait_ge(S("m_exp"), g + 1)
            for mt in range(2):
                l = nc.tensor.transpose(bank(6)[:, 128 * mt:128 * mt + 128], PM[:, 128 * mt:128 * mt + 128], ident[:])
            l.then_inc(S("m_tr"), 1)
            pe.wait_ge(S("m_pt"), g + 1)
            if g == 1:
                pe.wait_ge(S("m_o"), 1)
            for b in range(4):
                for mt in range(2):
                    l = nc.tensor.matmul(psum[32 * b:32 * b + 32, 512 * 7:512 * 7 + 256], PTS[:, mt, 32 * b:32 * b + 32], MK[g][:, b, mt, 256:512], start=mt == 0, stop=mt == 1)
            l.then_inc(S("m_pv"), 1)
        pe.wait_ge(S("m_o"), 2)

        for p in range(NPAIR):
            pair = (2 * p, 2 * p + 1)
            if p >= 1:
                pe.wait_ge(S("s_o"), p)
                pe.wait_ge(S("s_exp"), 3 * p)
            c_out = psum[:, 512 * 7 + 384:512 * 7 + 447]
            for b in pair:
                l = nc.tensor.matmul(c_out, QP[:, b, :], KCs[:, b, 0:63], start=b == pair[0], stop=b == pair[1])
            l.then_inc(S("s_qk"), 1)
            pe.wait_ge(S(f"s_in{p % 2}"), 16 * (2 * NPG + 2) * (p // 2 + 1))
            for c in range(6):
                i = (6 + NSC) * p + c
                wait_ring(pe, i - 2)
                for j in range(4):
                    src = SG[p % 2][:, c // 2, 4 * (c % 2) + j, 0:128] if c < 4 else WG[p % 2][:, c - 4, j, 0:128]
                    l = nc.tensor.transpose(bank(5 + i % 2)[:, 128 * j:128 * j + 128], src, ident[:])
                l.then_inc(S("s_tr"), 1)
            wait_ring(pe, (6 + NSC) * p + 4)
            wait_ring(pe, (6 + NSC) * p + 5)
            for b in pair:
                nc.tensor.matmul(bank(3), QP[:, b, :], KTw[:, b % 2, :], start=b == pair[0], stop=False)
            nc.tensor.matmul(bank(3, 8), identb[:], maskb[:, M_WINH:M_WINH + 8], start=False, stop=True)
            for b in pair:
                nc.tensor.matmul(bank(4, 64), QP[:, b, :], KTn[:, 1, :], start=b == pair[0], stop=False)
            nc.tensor.matmul(bank(4, 64), identb[:], maskb[:, M_NEW + 64 * p:M_NEW + 64 * p + 64], start=False, stop=True).then_inc(S("s_qk"), 1)
            pe.wait_ge(S("s_pcn"), p + 1)
            nc.tensor.matmul(psum[:, 512 * 7 + 448:512 * 7 + 511], csum[:], PC[:, 0:63], start=True, stop=True).then_inc(S("s_imp"), 1)
            for a in range(2):
                for b in pair:
                    nc.tensor.matmul(bank(a), QP[:, b, :], KTs[:, b % 2, 512 * a:512 * a + 512], start=b == pair[0], stop=b == pair[1])
            for b in pair:
                nc.tensor.matmul(bank(2, 64), QP[:, b, :], KTn[:, 0, :], start=b == pair[0], stop=False)
            nc.tensor.matmul(bank(2, 64), identb[:], maskb[:, M_NEW + 64 * p:M_NEW + 64 * p + 64], start=False, stop=True).then_inc(S("s_qk"), 1)
            for n, c in enumerate((2, 3, 0, 1)):
                i = (6 + NSC) * p + 6 + n
                wait_ring(pe, i - 2)
                pe.wait_ge(S("s_exp"), 3 * p + (2 if n == 0 else 3))
                for j, (k, w) in enumerate(S_CHUNKS[c]):
                    l = nc.tensor.transpose(bank(5 + i % 2)[0:w, 128 * j:128 * j + 128], s_prob(k, w), ident[:])
                l.then_inc(S("s_tr"), 1)
            wait_ring(pe, (6 + NSC) * p + 8)
            wait_ring(pe, (6 + NSC) * p + 9)
            pe.wait_ge(S("s_sel"), p + 1)
            for b in range(2):
                rows = slice(64 * b, 64 * b + 64)
                o = lambda br: psum[rows, 512 * 7 + 128 * br:512 * 7 + 128 * br + 128]
                q = lambda k, w=128: PTS[0:w, k, rows]
                nc.tensor.matmul(o(0), q(T_CMP, 63), VC[0:63, pair[b], :], start=True, stop=True)
                for k in range(NPG):
                    nc.tensor.matmul(o(1), q(k), SG[p % 2][:, b, k, 128:256], start=k == 0, stop=False)
                nc.tensor.matmul(o(1), q(T_NEWS, 64), kvn[:, 128:256], start=False, stop=True)
                for k in range(4):
                    nc.tensor.matmul(o(2), q(8 + k), WG[p % 2][:, b, k, 128:256], start=k == 0, stop=False)
                l = nc.tensor.matmul(o(2), q(T_NEWW, 64), kvn[:, 384:512], start=False, stop=True)
            l.then_inc(S("s_pv"), 1)
        pe.wait_ge(S("s_mix"), 1)
        for g in range(2):
            for k in range(4):
                l = nc.tensor.transpose(bank(g)[:, 64 * k:64 * k + 64], ms[:, 128 * (4 * g + k):128 * (4 * g + k) + 128], ident[0:64, 0:64])
            l.then_inc(S("s_xtr"), 1)

    def wait_ring(eng, i):
        if i >= 0:
            eng.wait_ge(S("s_ring_dve") if i % 2 else S("s_ring_act"), i // 2 + 1)

    def s_prob(k, w):
        if k < 8:
            return PSl[:, 128 * k:128 * k + w]
        if k < 12:
            return PW[:, 128 * (k - 8):128 * (k - 8) + w]
        return {T_NEWS: PSl[:, 1024:1088], T_NEWW: PW[:, 512:576], T_CMP: PC[:, 0:63]}[k]

    def ring_copy(eng, copy, i, sem):
        p, c = i // (6 + NSC), i % (6 + NSC)
        eng.wait_ge(S("s_tr"), i + 1)
        src = bank(5 + i % 2)
        if c < 6:
            if p >= 1:
                eng.wait_ge(S("s_qk"), 3 * p)
            dst = KTs[:, c // 2, 512 * (c % 2):512 * (c % 2) + 512] if c < 4 else KTw[:, c - 4, :]
            copy(dst, src).then_inc(sem, 1)
            return
        if p >= 1:
            eng.wait_ge(S("s_pv"), p)
        part = S_CHUNKS[(2, 3, 0, 1)[c - 6]]
        w = part[-1][1] if part[-1][1] == 128 else 64
        if w == 128:
            copy(PTS[:, part[0][0]:part[0][0] + 4, :], src.rearrange("p (j c) -> p j c", j=4)).then_inc(sem, 1)
        else:
            i1 = copy(PTS[0:64, T_NEWS:T_NEWS + 2, :], src[0:64, 0:256].rearrange("p (j c) -> p j c", j=2))
            i1.then_inc(S("s_part"), 1)
            copy(PTS[0:63, T_CMP, :], src[0:63, 256:384]).then_inc(sem, 1)

    def s_scores(j):
        return [psum[:, 512 * 7 + 384:512 * 7 + 447], psum[:, 512 * 3:512 * 3 + 576], psum[:, 0:1088]][j]

    def act_sample(act):
        act.wait_ge(S("s_qtr"), 1)
        act.wait_ge(S("s_zero"), 4)
        for kv in range(2):
            rows = slice(64 * kv, 64 * kv + 64)
            for par in range(2):
                c0 = 64 * par + 32 * kv
                nc.scalar.copy(QP[rows, par::2, c0:c0 + 32].rearrange("p b (g s) -> p b g s", g=4),
                               psum[rows, 0:256].rearrange("p (g b s) -> p b g s", g=4, b=NDB)[:, par::2]).then_inc(S("s_qpart"), 1)
        for r in range(2):
            rows = slice(64 * r, 64 * r + 64)
            for pr in range(2):
                for c in range(4):
                    c0 = 32 * c + 8 * (2 * pr + r)
                    nc.scalar.copy(QM[rows, pr, c::4, c0:c0 + 8],
                                   psum[rows, 512 + 64 * pr:576 + 64 * pr].rearrange("p (b s) -> p b s", b=NDB)[:, c::4]).then_inc(S("s_qpart"), 1)
        nc.scalar.copy(KTn[:], psum[:, 640:768].rearrange("p (r c) -> p r c", r=2)).then_inc(S("s_q"), 1)
        for g in range(2):
            act.wait_ge(S("m_nb"), g + 1)
            if g == 1:
                act.wait_ge(S("m_tr"), 1)
            nc.scalar.activation(PM[:], bank(4 + g, 256), ACT.Exp, bias=snb[:, g:g + 1], scale=SCALE, accum_out=ssm[:, g:g + 1]).then_inc(S("m_exp"), 1)
            act.wait_ge(S("m_tr"), g + 1)
            if g == 1:
                act.wait_ge(S("m_pv"), 1)
            nc.scalar.copy(PTS[:, 0:2, :], bank(6, 256).rearrange("p (j c) -> p j c", j=2)).then_inc(S("m_pt"), 1)
        for p in range(NPAIR):
            base = (6 + NSC) * p

            def exp(j):
                act.wait_ge(S("s_nb"), 3 * p + j + 1)
                if p >= 1:
                    act.wait_ge(S("s_pv"), p)
                dst = (PC[:, 0:63], PW[:], PSl[:])[j]
                nc.scalar.activation(dst, s_scores(j), ACT.Exp, bias=snb[:, 4 + j:5 + j], scale=SCALE, accum_out=ssm[:, 4 + j:5 + j]).then_inc(S("s_exp"), 1)

            exp(0)
            for c in range(0, 6, 2):
                ring_copy(act, nc.scalar.copy, base + c, S("s_ring_act"))
            exp(1)
            exp(2)
            for c in range(6, 6 + NSC, 2):
                ring_copy(act, nc.scalar.copy, base + c, S("s_ring_act"))
        for g in range(2):
            act.wait_ge(S("s_xtr"), g + 1)
            nc.scalar.copy(xhi[:, 4 * g:4 * g + 4, T:T + NS_TOK], bank(g, 256).rearrange("p (k c) -> p k c", k=4)).then_inc(S("s_xhi"), 1)

    def dve_sample(dve):
        ch = Link(dve, S("s_dve"))
        dve.wait_ge(S("s_zero"), 4)
        for g in range(2):
            for b in range(4 * g, 4 * g + 4):
                dve.wait_ge(S("m_ktr"), b + 1)
                if g == 1:
                    dve.wait_ge(S("m_qk"), 1)
                nc.vector.tensor_copy(KTm[:, b % 4], bank(2 + b % 2).rearrange("p (r m) -> p r m", r=2)).then_inc(S("m_kt"), 1)
            dve.wait_ge(S("m_qk"), g + 1)
            ch.step(nc.vector.tensor_reduce(out=smx[:, g:g + 1], in_=bank(4 + g, 256), op=ALU.max, axis=AX.X))
            nc.vector.tensor_scalar(snb[:, g:g + 1], smx[:, g:g + 1], -SCALE, None, ALU.mult).then_inc(S("m_nb"), 1)
            dve.wait_ge(S("m_pv"), g + 1)
            ch.step(nc.vector.reciprocal(ssm[:, 2 + g:3 + g], ssm[:, g:g + 1]))
            o = bank(7, 256).rearrange("p (h d) -> p h d", h=4)
            t = OMs[:, g, :]
            ch.step(nc.vector.tensor_scalar(t, o[:, 0], colc[:, 6:7], None, ALU.mult))
            for h in range(1, 4):
                ch.step(nc.vector.scalar_tensor_tensor(out=t, in0=o[:, h], scalar=colc[:, 6 + h:7 + h], in1=t, op0=ALU.mult, op1=ALU.add))
            nc.vector.tensor_scalar(t, t, ssm[:, 2 + g:3 + g], None, ALU.mult).then_inc(S("m_o"), 1)
        for p in range(NPAIR):
            base = (6 + NSC) * p

            def top(j):
                dve.wait_ge(S("s_qk"), 3 * p + j + 1)
                ch.step(nc.vector.tensor_reduce(out=smx[:, 4 + j:5 + j], in_=s_scores(j), op=ALU.max, axis=AX.X))
                if p >= 1:
                    dve.wait_ge(S("s_exp"), 3 * p)
                nc.vector.tensor_scalar(snb[:, 4 + j:5 + j], smx[:, 4 + j:5 + j], -SCALE, None, ALU.mult).then_inc(S("s_nb"), 1)
                dve.wait_ge(S("s_nb"), 3 * p + j + 1)

            top(0)
            for c in range(1, 6, 2):
                ring_copy(dve, nc.vector.tensor_copy, base + c, S("s_ring_dve"))
            dve.wait_ge(S("s_exp"), 3 * p + 1)
            ch.step(nc.vector.reciprocal(ssm[:, 8:9], ssm[:, 4:5]))
            nc.vector.tensor_scalar(PC[:, 0:63], PC[:, 0:63], ssm[:, 8:9], None, ALU.mult).then_inc(S("s_pcn"), 1)
            top(1)
            dve.wait_ge(S("s_imp"), p + 1)
            ch.step(nc.vector.tensor_copy(pp[:, 1:64], psum[:, 512 * 7 + 448:512 * 7 + 511]))
            ch.step(nc.vector.tensor_reduce(out=sc[:, 0], in_=pp[:, 4:60].rearrange("p (n r) -> p n r", r=4), op=ALU.add, axis=AX.X))
            ch.step(nc.vector.tensor_tensor(sc[:, 0], sc[:, 0], pp[:, 8:64].rearrange("p (n r) -> p n r", r=4)[:, :, 0], ALU.add))
            ch.step(nc.vector.tensor_reduce(out=smx[:, 8:9], in_=sc[:, 0], op=ALU.min, axis=AX.X))
            ch.step(nc.vector.tensor_scalar(sc[:, 1], sc[:, 0], smx[:, 8:9], None, ALU.is_equal))
            ch.step(nc.vector.tensor_tensor(sc[:, 1], sc[:, 1], cblk[:], ALU.mult))
            ch.step(nc.vector.tensor_reduce(out=smx[:, 9:10], in_=sc[:, 1], op=ALU.max, axis=AX.X))
            nc.vector.tensor_scalar(sc[:, 2], cblk[:], smx[:, 9:10], NEG, ALU.is_equal, ALU.mult).then_inc(S("s_sel"), 1)
            dve.wait_ge(S("s_sel"), p + 1)
            dve.wait_ge(S("s_qk"), 3 * p + 3)
            blocks = psum[:, 64:960].rearrange("p (n c) -> p n c", c=64)
            ch.step(nc.vector.tensor_tensor(blocks, blocks, sc[:, 2].rearrange("p (n o) -> p n o", o=1).to_broadcast([128, 14, 64]), ALU.add))
            top(2)
            for c in range(7, 6 + NSC, 2):
                ring_copy(dve, nc.vector.tensor_copy, base + c, S("s_ring_dve"))
            dve.wait_ge(S("s_exp"), 3 * p + 3)
            ch.do(nc.vector.reciprocal(rs3[:, 1:2], ssm[:, 6:7]))
            ch.do(nc.vector.reciprocal(rs3[:, 2:3], ssm[:, 5:6]))
            ch.wait()
            dve.wait_ge(S("s_pv"), p + 1)
            if p >= 2:
                dve.wait_ge(S("o_out"), 16 * (p - 1) + 32)
            o = bank(7, 384).rearrange("p (r k d) -> p r k d", r=3, k=2)
            t = OSp[p % 2]
            ch.step(nc.vector.tensor_scalar(t[:], o[:, :, 0], colc[:, 4:5], None, ALU.mult))
            ch.step(nc.vector.scalar_tensor_tensor(out=t[:], in0=o[:, :, 1], scalar=colc[:, 5:6], in1=t[:], op0=ALU.mult, op1=ALU.add))
            nc.vector.tensor_tensor(t[:], t[:], rs3[:].rearrange("p (r o) -> p r o", o=1).to_broadcast([128, 3, HD]), ALU.mult).then_inc(S("s_o"), 1)
            dve.wait_ge(S("s_o"), p + 1)
        for g in range(2):
            dve.wait_ge(S("s_xhi"), g + 1)
            dst = (slice(None), slice(4 * g, 4 * g + 4), slice(T, T + NS_TOK))
            nc.vector.tensor_tensor(xlo[dst], bank(g, 256).rearrange("p (k c) -> p k c", k=4), xhi[dst].bitcast(F32), ALU.subtract).then_inc(S("s_xlo"), 1)

    OUT_W = (MEMJ + 1, MEMJ + 2)

    def sp_out(sp):
        sp.wait_ge(S("s_mix"), 1)
        sp.wait_ge(S("s_xlo"), 2)
        sp.dma_start(gf[:], io["ln_final"].rearrange("(o n) -> o n", o=1).to_broadcast([128, D])).then_inc(S("d_const"), 16)
        load_w(sp, OUT_W[0])
        for t in range(2):
            sp.dma_start(xr[t][0:tile_rows(t)], x_rows[t]).then_inc(S(f"d_x{t}"), 16)
        load_w(sp, OUT_W[1])
        for t in range(NT):
            r = tile_rows(t)
            sp.wait_ge(S("d_y"), t + 1)
            dst = io["y_prompt"][0, 128 * t:128 * t + 128, :] if t < QT else io["y_sample"].rearrange("b s d -> (b s) d")
            sp.dma_start(dst, yo[t % 2][0:r]).then_inc(S(f"y_out{t % 2}"), 16)
            if t + 2 < NT:
                sp.dma_start(xr[t % 2][0:tile_rows(t + 2)], x_rows[t + 2]).then_inc(S(f"d_x{t % 2}"), 16)
        for i in range(2):
            sp.wait_ge(S(f"y_out{i}"), 16 * len(range(i, NT, 2)))

    def pe_out(pe):
        pe.wait_ge(S("s_xlo"), 2)
        for jj, w in enumerate(OUT_W):
            pe.wait_ge(S("w_split"), 2 * w + 2)
        for t in range(NT):
            r = tile_rows(t)
            if t >= 4:
                pe.wait_ge(S("d_sum"), t - 3)
            for jj, w in enumerate(OUT_W):
                o = 512 * (2 * (t % 4) + jj)
                for k in range(KT):
                    l = mm3(psum[0:r, o:o + 512], w % 2, k, 512, tile_col(t), r, k == 0, k == KT - 1)
            l.then_inc(S("d_mm"), 1)

    def act_out(act):
        for w in OUT_W:
            split_w_hi(act, w)
        for t in range(NT):
            r = tile_rows(t)
            act.wait_ge(S("d_sum"), t + 1)
            if t >= 2:
                act.wait_ge(S(f"y_out{t % 2}"), 16 * (t // 2))
            nc.scalar.activation(yo[t % 2][0:r], yt[t % 2][0:r], ACT.Square, accum_out=small[0:r, t:t + 1]).then_inc(S("d_ss"), 1)
            act.wait_ge(S("d_ms"), t + 1)
            nc.scalar.activation(small[0:r, 32 + t:33 + t], small[0:r, 16 + t:17 + t], ACT.Sqrt).then_inc(S("d_sd"), 1)

    def dve_out(dve):
        ch = Link(dve, S("d_dve"))
        for w in OUT_W:
            split_w_lo(dve, w)
        dve.wait_ge(S("d_const"), 16)
        for t in range(NT):
            r = tile_rows(t)
            dve.wait_ge(S("d_mm"), t + 1)
            dve.wait_ge(S(f"d_x{t % 2}"), 16 * (t // 2 + 1))
            o = 1024 * (t % 4)
            nc.vector.tensor_tensor(yt[t % 2][0:r], psum[0:r, o:o + 1024], xr[t % 2][0:r], ALU.add).then_inc(S("d_sum"), 1)
            dve.wait_ge(S("d_ss"), t + 1)
            v = small[0:r, 16 + t:17 + t]
            nc.vector.tensor_scalar(v, small[0:r, t:t + 1], 1.0 / D, EPS, ALU.mult, ALU.add).then_inc(S("d_ms"), 1)
            dve.wait_ge(S("d_sd"), t + 1)
            y = small[0:r, 48 + t:49 + t]
            ch.step(nc.vector.reciprocal(y, small[0:r, 32 + t:33 + t]))
            rsqrt_polish(dve, ch, y, v, small[0:r, 64 + t:65 + t])
            nc.vector.scalar_tensor_tensor(out=yo[t % 2][0:r], in0=yt[t % 2][0:r], scalar=y, in1=gf[0:r], op0=ALU.mult, op1=ALU.mult).then_inc(S("d_y"), 1)
            dve.wait_ge(S("d_y"), t + 1)

    with nc.Block() as block:

        @block.sync
        def _(sp):
            n_c = 0
            for dst, src in ((ident[:], io["c_ident"]), (colc[:], io["c_col"]), (pt[:], io["page_table"].rearrange("b p -> (b p)").rearrange("(a n) -> a n", a=1)),
                             (gb[:, 0, :], io["ln_mix"].to_broadcast([128, D])), (gb[:, 1, :], io["ln_mem"].to_broadcast([128, D]))):
                sp.dma_start(dst, src).then_inc(S("const_in"), 16)
            load_w(sp, 0)
            for n in range(NT + 2):
                if n >= 2:
                    sp.wait_ge(S("x_scaled"), n - 1)
                sp.dma_start(xraw[n % 2][0:tile_rows(n), :], x_rows[n]).then_inc(S(f"x_in{n % 2}"), 16)
            if on("B"):
                for j in range(1, MEMJ + 1):
                    load_w(sp, j)
                sp.dma_start(io["new_win_s"][0, :, 0:WIN - DS].rearrange("b t a k d -> b (t a k d)"),
                             io["cache_nsa_win"][0, :, DS:WIN].rearrange("b t a k d -> b (t a k d)")).then_inc(S("out_done"), 16)
                wait_h(sp)
                kv = lambda c: hD[0:T, c:c + 256]
                kvs = lambda c: hD[T:T + NS_TOK, c:c + 256]
                fl = "t a k d -> t (a k d)"
                for dst, c in ((io["new_cmp_p"], C_KVC), (io["new_slc_p"], C_KVS)):
                    sp.dma_start(dst[0, 0].rearrange(fl), kv(c)).then_inc(S("out_done"), 16)
                sp.dma_start(io["new_win_p"][0, 0].rearrange(fl), kv(C_KVW)[T - WIN:T]).then_inc(S("out_done"), 16)
                for dst, c in ((io["new_cmp_s"], C_KVC), (io["new_slc_s"], C_KVS)):
                    sp.dma_start(dst[0].rearrange("b t a k d -> (b t) (a k d)"), kvs(c)).then_inc(S("out_done"), 16)
                sp.dma_start(io["new_win_s"][0, :, WIN - DS:WIN].rearrange("b t a k d -> b t (a k d)"),
                             kvs(C_KVW).rearrange("(b t) n -> b t n", b=NDB)).then_inc(S("out_done"), 16)
            n_out = 7 if on("B") else 0
            if on("C"):
                sp_compress(sp)
            if on("R"):
                sp_retention(sp)
                n_out += 2 + 4
            if on("P"):
                sp_prompt(sp)
            if on("S"):
                sp_sample(sp)
            if on("D"):
                sp_out(sp)
            sp.wait_ge(S("out_done"), 16 * n_out)

        @block.tensor
        def _(pe):
            pe.wait_ge(S("const_in"), 80)
            for n in range(NT + 2):
                r = tile_rows(n)
                pe.wait_ge(S("x_scaled"), n + 1)
                for g in range(2):
                    i = 2 * n + g
                    if i >= 4:
                        pe.wait_ge(S("x_lo"), i - 3)
                    for k in range(4):
                        l = nc.tensor.transpose(bank(i % 4)[:, 128 * k:128 * k + r], xs[0][0:r, 128 * (4 * g + k):128 * (4 * g + k) + 128], ident[0:r, 0:r])
                    l.then_inc(S("x_tr"), 1)
            if on("B"):
                pe.wait_ge(S("x_lo"), 2 * (NT + 2))
                for q, (j, t) in enumerate(proj_jobs):
                    if q == 0 or proj_jobs[q - 1][0] != j:
                        pe.wait_ge(S("w_split"), 2 * j + 2)
                    if q >= 8:
                        wait_evac(pe, q - 8)
                    r, n = tile_rows(t), w_n[j]
                    for k in range(KT):
                        l = mm3(psum[0:r, 512 * (q % 8):512 * (q % 8) + n], j % 2, k, n, tile_col(t), r, k == 0, k == KT - 1)
                    l.then_inc(S("h_mm"), 1)
            if on("C"):
                pe_compress(pe)
            if on("R"):
                pe_retention(pe)
            if on("P"):
                pe_prompt(pe)
            if on("S"):
                pe_sample(pe)
            if on("D"):
                pe_out(pe)

        @block.scalar
        def _(act):
            def hi(n):
                for g in range(2):
                    act.wait_ge(S("x_tr"), 2 * n + g + 1)
                    nc.scalar.copy(xhi[:, 4 * g:4 * g + 4, tile_col(n):tile_col(n) + tile_rows(n)], x_src(n, g)).then_inc(S("x_hi"), 1)

            split_done = 0
            for n in range(NT + 2):
                r = tile_rows(n)
                act.wait_ge(S(f"x_in{n % 2}"), 16 * (n // 2 + 1))
                if n >= 1:
                    act.wait_ge(S("x_tr"), 2 * n)
                nc.scalar.activation(xs[0][0:r, :], xraw[n % 2][0:r, :], ACT.Square, accum_out=small[0:r, n:n + 1]).then_inc(S("x_ss"), 1)
                act.wait_ge(S("x_ms"), n + 1)
                nc.scalar.activation(small[0:r, 32 + n:33 + n], small[0:r, 16 + n:17 + n], ACT.Sqrt).then_inc(S("x_sd"), 1)
                if n == 0:
                    split_w_hi(act, 0)
                if n >= 1:
                    hi(n - 1)
            hi(NT + 1)
            if on("B"):
                act.wait_ge(S("w_in0"), 16)
                split_w_hi(act, 1)
                for q, (j, t) in enumerate(proj_jobs):
                    if t == 2 and j >= 1 and j + 1 <= MEMJ:
                        split_w_hi(act, j + 1)
                    if not by_act(j):
                        continue
                    r = tile_rows(t)
                    act.wait_ge(S("h_mm"), q + 1)
                    if q >= HST:
                        act.wait_ge(S(f"h_out{q % HST}"), 16 * (q // HST))
                    src, dst = psum[0:r, 512 * (q % 8):512 * (q % 8) + 512], hst[q % HST][0:r]
                    if j == 2:
                        nc.scalar.copy(dst[:, 0:256], src[:, 0:256]).then_inc(S("h_part"), 1)
                        nc.scalar.activation(dst[:, 256:280], src[:, 256:280], ACT.Sigmoid).then_inc(S("h_evac_act"), 1)
                    elif j == 3:
                        nc.scalar.activation(dst, src, ACT.Silu).then_inc(S("h_evac_act"), 1)
                    else:
                        nc.scalar.copy(dst[:, 0:256], src[:, 0:256]).then_inc(S("h_part"), 1)
                        nc.scalar.activation(dst[:, 256:512], src[:, 256:512], ACT.Silu).then_inc(S("h_evac_act"), 1)
            if on("C"):
                act_compress(act)
            if on("R"):
                act_retention(act)
            if on("P"):
                act_prompt(act)
            if on("S"):
                act_sample(act)
            if on("D"):
                act_out(act)

        @block.vector
        def _(dve):
            def lo(n):
                for g in range(2):
                    dve.wait_ge(S("x_hi"), 2 * n + g + 1)
                    cs = slice(tile_col(n), tile_col(n) + tile_rows(n))
                    nc.vector.tensor_tensor(xlo[:, 4 * g:4 * g + 4, cs], x_src(n, g), xhi[:, 4 * g:4 * g + 4, cs].bitcast(F32), ALU.subtract).then_inc(S("x_lo"), 1)

            ch = Link(dve, S("x_dve"))
            dve.wait_ge(S("const_in"), 80)
            nc.vector.tensor_copy(identb[:], ident[:]).then_inc(S("identb"), 1)
            for n in range(NT + 2):
                r = tile_rows(n)
                dve.wait_ge(S("x_ss"), n + 1)
                nc.vector.tensor_scalar(small[0:r, 16 + n:17 + n], small[0:r, n:n + 1], 1.0 / D, EPS, ALU.mult, ALU.add).then_inc(S("x_ms"), 1)
                dve.wait_ge(S("x_sd"), n + 1)
                nc.vector.reciprocal(small[0:r, 48 + n:49 + n], small[0:r, 32 + n:33 + n]).then_inc(S("x_rs"), 1)
                dve.wait_ge(S("x_rs"), n + 1)
                rsqrt_polish(dve, ch, small[0:r, 48 + n:49 + n], small[0:r, 16 + n:17 + n], small[0:r, 64 + n:65 + n])
                nc.vector.scalar_tensor_tensor(out=xs[0][0:r, :], in0=xraw[n % 2][0:r, :], scalar=small[0:r, 48 + n:49 + n],
                                               in1=gb[0:r, int(n >= NT), :], op0=ALU.mult, op1=ALU.mult).then_inc(S("x_scaled"), 1)
                if n == 0:
                    split_w_lo(dve, 0)
                if n >= 1:
                    lo(n - 1)
            lo(NT + 1)
            if on("B"):
                split_w_lo(dve, 1)
                for q, (j, t) in enumerate(proj_jobs):
                    if t == 2 and j >= 1 and j + 1 <= MEMJ:
                        split_w_lo(dve, j + 1)
                    if by_act(j):
                        continue
                    r = tile_rows(t)
                    dve.wait_ge(S("h_mm"), q + 1)
                    if q >= HST:
                        dve.wait_ge(S(f"h_out{q % HST}"), 16 * (q // HST))
                    nc.vector.tensor_copy(hst[q % HST][0:r, :], psum[0:r, 512 * (q % 8):512 * (q % 8) + 512]).then_inc(S("h_evac_dve"), 1)
            if on("C"):
                dve_compress(dve)
            if on("R"):
                dve_retention(dve)
            if on("P"):
                dve_prompt(dve)
            if on("S"):
                dve_sample(dve)
            if on("D"):
                dve_out(dve)

        @block.gpsimd
        def _(pool):
            if on("B"):
                for q, (j, t) in enumerate(proj_jobs):
                    r, n = tile_rows(t), w_n[j]
                    wait_evac(pool, q)
                    if j == MEMJ:
                        dst = new_mem[128 * (t - NT):128 * (t - NT) + 128, :]
                    else:
                        dst = hD[128 * t:128 * t + r, CHUNKS[j][0]:CHUNKS[j][0] + n]
                    pool.dma_start(dst, hst[q % HST][0:r, 0:n]).then_inc(S(f"h_out{q % HST}"), 16)
            if on("C"):
                pool_compress(pool)
            if on("R"):
                pool_retention(pool)
            if on("P"):
                pool_prompt(pool)
            if on("S"):
                pool_sample(pool)



_OUTS = [("y_prompt", (1, T, D)), ("y_sample", (NDB, DS, D)),
         ("new_cmp_p", (1, 1, T, 2, 2, HD)), ("new_cmp_s", (1, NDB, DS, 2, 2, HD)),
         ("new_slc_p", (1, 1, T, 2, 2, HD)), ("new_slc_s", (1, NDB, DS, 2, 2, HD)),
         ("new_win_p", (1, 1, WIN, 2, 2, HD)), ("new_win_s", (1, NDB, WIN, 2, 2, HD)),
         ("new_ret_p", (1, 1, 4, HD, HD)), ("new_ret_s", (1, NDB, 4, HD, HD)),
         ("new_mem", (1, 1, NM, 2, 4, HD))]


def kernel(**inputs):
    import concourse.bacc as bacc
    from concourse.bass_utils import run_bass_kernel_spmd

    nc = bacc.Bacc("TRN2", target_bir_lowering=False, num_devices=1)
    arrays, io = {}, {}
    for name, a in {**inputs, **constants()}.items():
        a = np.ascontiguousarray(a)
        arrays[f"in_{name}"] = a
        io[name] = nc.dram_tensor(f"in_{name}", a.shape, mybir.dt.from_np(a.dtype), kind="ExternalInput").ap()
    for name, shape in _OUTS:
        io[name] = nc.dram_tensor(f"out_{name}", shape, F32, kind="ExternalOutput").ap()
    build(nc, io)
    r = run_bass_kernel_spmd(nc, [arrays], core_ids=[0])
    return tuple(r.results[0][f"out_{name}"] for name, _ in _OUTS)
```

```python
import numpy as np
import concourse.bass as bass
from concourse import mybir

F32 = mybir.dt.float32
F32R = mybir.dt.float32r
BF16 = mybir.dt.bfloat16
I32 = mybir.dt.int32
ALU = mybir.AluOpType
ACT = mybir.ActivationFunctionType
AX = mybir.AxisListType

D = 1024
T = 1024
NDB, DS = 8, 8
NS_TOK = NDB * DS
PAST, PAGE, NPOOL = 1024, 128, 80
NPG = PAST // PAGE
HD = 64
QT = T // 128
NT = QT + 1
NM = 256
WIN = 512
INW = 3352
KT = D // 128
SCALE = HD ** -0.5
EPS = 1e-6
NEG = -1e30
C_QN, C_KVC, C_KVS, C_KVW, C_G, C_ZN, C_QR, C_ZR, C_QM, C_ZM = 0, 512, 768, 1024, 1280, 1304, 1816, 2584, 2840, 3096
CHUNKS = [(0, 512), (512, 512), (1024, 280), (1304, 512), (1816, 512), (2328, 512), (2840, 512), (0, 512)]
MEMJ = 7
LOG_G = np.log1p(-np.exp2(-5.0 - np.arange(4)))


def tile_rows(n):
    return NS_TOK if n == QT else 128


def tile_col(n):
    return 128 * n if n <= QT else T + NS_TOK + 128 * (n - NT)


def constants():
    f = np.float32
    c = {}
    c["c_ident"] = np.eye(128, dtype=f)
    q, k = np.arange(128)[:, None], np.arange(128)[None, :]
    causal = np.where(k > q, NEG, 0.0)
    tail = np.where(k <= q, NEG, 0.0)
    cmpm = [np.where((16 * np.arange(64)[None, :] + 31 <= 128 * i + q) & (np.arange(64)[None, :] < 63), 0.0, NEG) for i in range(QT)]
    r = np.arange(128)
    rb, rs = r // 64, r % 8
    new = []
    for p in range(4):
        j = np.arange(64)
        new.append(np.where((j[None, :] // 8 == 2 * p + rb[:, None]) & (j[None, :] % 8 <= rs[:, None]), 0.0, NEG))
    winh = np.where(np.arange(8)[None, :] <= rs[:, None], NEG, 0.0)
    c["c_mask"] = np.concatenate([causal, tail] + cmpm + new + [winh], axis=1).astype(f)
    half = HD // 2
    inv = (10000.0 ** (-np.arange(half) / half)).astype(f)
    pos = np.concatenate([np.arange(T), np.tile(PAST + np.arange(DS), NDB)])
    n = np.concatenate([np.arange(T) % 128, np.tile(np.arange(DS), NDB)]) + 1
    ang = pos.astype(f)[:, None] * inv[None, :]
    cs, sn = np.cos(ang).astype(np.float64), np.sin(ang).astype(np.float64)
    dq = SCALE * np.exp(LOG_G[None, :] * n[:, None])
    dk = np.exp(-LOG_G[None, :] * n[:, None])
    dd = np.concatenate([dq, dk], axis=1)
    c["c_rope"] = np.concatenate([(dd[:, :, None] * cs[:, None, :]).reshape(-1, 256), (dd[:, :, None] * sn[:, None, :]).reshape(-1, 256)], axis=1).astype(f)
    m_le_n = (q <= k).astype(f)
    same_b = (q // 8 == k // 8).astype(f)
    c["c_ret"] = np.concatenate([m_le_n, (m_le_n * same_b), (q // 64 == k // 64).astype(f)], axis=1).astype(f)
    hh = np.arange(128) // 64
    dec = [np.exp(LOG_G[2 * p + hh] * s) for s in (128, DS) for p in range(2)]
    selkv = [(r % 64 // 32 == v) for v in range(2)]
    selh = [(r % 32 // 8 == v) for v in range(4)]
    selb = [(r // 8 == v) for v in range(8)]
    c["c_col"] = np.stack(dec + selkv + selh + selb, axis=1).astype(f)
    c["c_sum"] = ((r[:, None] // 32 == r[None, :] // 32) & (rs[:, None] == rs[None, :])).astype(f)
    blk = np.tile(np.arange(14, dtype=f)[None, :] + 1, (128, 1))
    c["c_blk"] = blk
    return c


M_CAUSAL, M_TAIL, M_CMP, M_NEW, M_WINH = 0, 128, 256, 256 + 64 * QT, 256 + 64 * QT + 256
M_W = M_WINH + 8


class Region:

    def __init__(self, nc, at, tag):
        self.nc, self.at, self.tag = nc, at, tag

    def __call__(self, name, shape, dt=F32):
        size = int(np.prod(shape[1:])) * (2 if dt == BF16 else 4)
        t = self.nc.alloc_sbuf_tensor_at(self.tag + name, shape, dt, offset=self.at)
        self.at += (size + 31) // 32 * 32
        return t


class Link:

    def __init__(self, eng, sem):
        self.eng, self.sem, self.n = eng, sem, 0

    def do(self, ins):
        self.n += 1
        ins.then_inc(self.sem, 1)

    def wait(self):
        self.eng.wait_ge(self.sem, self.n)

    def step(self, ins):
        self.do(ins)
        self.wait()


def build(nc, io, stop="D"):
    order = "ABCRPSD"
    on = lambda s: order.index(s) <= order.index(stop)
    BASE = (nc.sbuf_base + 63) // 64 * 64
    LIMIT = nc.sbuf_usable_end
    sem = {}

    def S(name):
        if name not in sem:
            sem[name] = nc.alloc_semaphore(name)
        return sem[name]

    hD = nc.dram_tensor("h_scratch", [T + NS_TOK, INW], F32, kind="Internal").ap()
    oD = nc.dram_tensor("o_scratch", [NDB * 64, 3 * HD], F32, kind="Internal").ap()
    omD = nc.dram_tensor("om_scratch", [NDB * 32, HD], F32, kind="Internal").ap()

    x_rows = [io["x_prompt"][0, 128 * n:128 * n + 128, :] for n in range(QT)]
    x_rows += [io["x_sample"].rearrange("b s d -> (b s) d")]
    x_rows += [io["mem_prompt"][0, 128 * n:128 * n + 128, :] for n in range(2)]
    w_src = [io["w_in"][0, :, c:c + n] for c, n in CHUNKS[:MEMJ]] + [io["w_mem_kv"][0]]
    w_src += [io["w_out"][0, :, 512 * j:512 * j + 512] for j in range(2)]
    w_src = [w.rearrange("(k p) n -> p k n", p=128) for w in w_src]
    w_n = [n for _, n in CHUNKS] + [512, 512]
    new_mem = io["new_mem"][0, 0].rearrange("m a h d -> m (a h d)")

    fix = Region(nc, BASE, "f_")
    NCOL = T + NS_TOK + 2 * 128
    xhi = fix("xhi", [128, KT, NCOL], F32R)
    xlo = fix("xlo", [128, KT, NCOL], F32R)
    ident_at = fix.at
    ident = fix("ident", [128, 128])
    identb = fix("identb", [128, 128], BF16)
    colc = fix("colc", [128, 18])
    KCs = fix("KCs", [128, NDB, 64])
    VC = fix("VC", [64, NDB + 1, 128])
    KCp = fix("KCp", [128, 2, 64], F32R)
    OC = fix("OC", [128, NT, 256])
    small = fix("small", [128, 160])
    pt = fix("pt", [1, NDB * NPG], I32)
    arena = fix.at

    ra = Region(nc, arena, "a_")
    wraw = [ra(f"wraw{i}", [128, 4, 512]) for i in range(2)]
    whi = [ra(f"whi{i}", [128, KT, 512], F32R) for i in range(2)]
    wlo = [ra(f"wlo{i}", [128, KT, 512], F32R) for i in range(2)]
    w_end = ra.at
    HST = 3
    hst = [ra(f"hst{i}", [128, 512]) for i in range(HST)]
    x_place = ra.at
    xraw = [ra(f"xraw{i}", [128, D]) for i in range(2)]
    xs = [ra("xs0", [128, D])]
    gb = ra("gb", [128, 2, D])
    assert ra.at <= LIMIT, (ra.at, LIMIT)

    psum = nc.alloc_psum_tensor("psum", [128, 8 * 512], F32)
    bank = lambda b, n=512: psum[:, 512 * b:512 * b + n]

    rc = Region(nc, arena, "c_")
    w1raw = rc("w1raw", [128, 2, 2, 8, 128])
    w1hi = rc("w1hi", [128, 2, 2, 8, 128], F32R)
    w1lo = rc("w1lo", [128, 2, 2, 8, 128], F32R)
    cthi = [rc(f"cthi{i}", [128, 8, 258], F32R) for i in range(2)]
    ctlo = [rc(f"ctlo{i}", [128, 8, 258], F32R) for i in range(2)]
    hid = [rc(f"hid{i}", [128, 4, 64]) for i in range(2)]
    w2 = rc("w2", [128, 2, HD])
    pe_raw = rc("pe_raw", [32, 128])
    pe_t = rc("pe_t", [128, 32])
    b1 = rc("b1", [128, 2])
    assert rc.at <= x_place, (rc.at, x_place)
    G = [nc.alloc_sbuf_tensor_at(f"c_G{i}", [128, 16, 2, 2, HD], F32, offset=at) for i, at in enumerate((x_place, arena))]

    rg = Region(nc, BASE, "r_")
    G2 = [rg(f"G2{i}", [128, 2, 16, HD]) for i in range(3)]
    retc = rg("retc", [128, 384])
    gnb = rg("gnb", [128, 256])
    rr = [rg(f"rr{i}", [128, 768]) for i in range(2)]
    rt = [rg(f"rt{i}", [128, 512]) for i in range(2)]
    ro = [rg(f"ro{i}", [128, 512]) for i in range(2)]
    rtmp = rg("rtmp", [128, 4, 8, 32])
    RT = [rg(f"RT{i}", [128, 4, 128]) for i in range(2)]
    AT = [rg(f"AT{i}", [128, 2, 2, 128]) for i in range(2)]
    BD = rg("BD", [128, 2, 128])
    BDs = rg("BDs", [128, NDB, 2, 128])
    QZ = rg("QZ", [128, 2, NDB, NS_TOK])
    KZ = rg("KZ", [NS_TOK, NDB, 256])
    kvt = rg("kvt", [128, 4, 128])
    rsq = rg("rsq", [128, 256])
    assert rg.at <= ident_at, (rg.at, ident_at)

    rp = Region(nc, arena, "p_")
    maskb = rp("maskb", [128, M_W], BF16)
    KS = rp("KS", [128, 2, 2, T], F32R)
    V = rp("V", [128, 2, QT, 128])
    KM = rp("KM", [128, 4, NM], F32R)
    VM = rp("VM", [128, 2, 256])
    split_at = rp.at
    QA = [rp(f"QA{i}", [128, 12, 128], F32R) for i in range(2)]
    QB = [rp(f"QB{i}", [128, 12, 128], F32R) for i in range(2)]
    rk = Region(nc, split_at, "pk_")
    Ktok = rk("Ktok", [128, 2, QT, 128])
    Kmt = rk("Kmt", [128, 2, 256])
    mraw = rk("mraw", [128, M_W])
    assert rk.at <= rp.at
    qd = [rp(f"qd{i}", [128, 12, 2, HD]) for i in range(2)]
    zt = [rp(f"zt{i}", [128, D]) for i in range(2)]
    gt = [rp(f"gt{i}", [128, 24]) for i in range(2)]
    P = [rp(f"P{i}", [128, T]) for i in range(2)]
    NPT = 3
    PTs = [rp(f"PT{i}", [128, 512]) for i in range(NPT)]
    Oi = rp("Oi", [128, 28, HD])
    mx = [rp(f"mx{i}", [128, D]) for i in range(2)]
    ssum = rp("ssum", [128, 2, 28])
    gw = rp("gw", [128, 2, 28])
    NNB = 6
    nb = rp("nb", [128, 2 * NNB])
    rw = rp("rw", [128, 2, 8])
    assert rp.at <= LIMIT, (rp.at, LIMIT)

    ru = Region(nc, split_at - (split_at - arena) + (2 * M_W + 31) // 32 * 32, "s_")
    s_at = ru.at
    SG = [ru(f"SG{i}", [128, 2, NPG, 256]) for i in range(2)]
    WG = [ru(f"WG{i}", [128, 2, 4, 256]) for i in range(2)]
    rm = Region(nc, s_at, "m_")
    MK = [rm(f"MK{i}", [128, 4, 2, 512]) for i in range(2)]
    KTm = rm("KTm", [128, 4, 2, NM])
    QM = rm("QM", [128, 2, NDB, 128])
    assert rm.at <= ru.at
    KTs = ru("KTs", [128, 2, PAST])
    KTw = ru("KTw", [128, 2, WIN])
    KTn = ru("KTn", [128, 2, NS_TOK])
    QP = ru("QP", [128, NDB, 128])
    PC = ru("PC", [128, 64])
    PW = ru("PW", [128, WIN + 64])
    PSl = ru("PSl", [128, PAST + 64])
    PM = ru("PM", [128, NM])
    PTS = ru("PTS", [128, 15, 128])
    qs = ru("qs", [NS_TOK, 4, 2, HD])
    qms = ru("qms", [NS_TOK, 256])
    kvn = ru("kvn", [NS_TOK, 512])
    csum = ru("csum", [128, 128])
    cblk = ru("cblk", [128, 14])
    zs = ru("zs", [NS_TOK, D])
    gs = ru("gs", [NS_TOK, 24])
    ms = ru("ms", [NS_TOK, D])
    on_s = ru("on_s", [NS_TOK, 8, 3, HD])
    om_s = ru("om_s", [NS_TOK, 4, HD])
    OMs = ru("OMs", [128, 2, HD])
    OSp = [ru(f"OSp{i}", [128, 3, HD]) for i in range(2)]
    pp = ru("pp", [128, 64])
    sc = ru("sc", [128, 3, 14])
    smx, snb, ssm, rs3 = ru("smx", [128, 10]), ru("snb", [128, 8]), ru("ssm", [128, 10]), ru("rs3", [128, 3])
    assert ru.at <= LIMIT, (ru.at, LIMIT)

    rd = Region(nc, w_end, "d_")
    gf = rd("gf", [128, D])
    xr = [rd(f"xr{i}", [128, D]) for i in range(2)]
    yt = [rd(f"yt{i}", [128, D]) for i in range(1)] * 2
    yo = [rd(f"yo{i}", [128, D]) for i in range(2)]
    assert rd.at <= LIMIT, (rd.at, LIMIT)

    proj_jobs = [(j, t) for j in range(MEMJ) for t in range(NT)] + [(MEMJ, NT), (MEMJ, NT + 1)]
    ACT_CHUNKS = (2, 3, 5, 6)

    def by_act(j):
        return j in ACT_CHUNKS

    def evac_count(q, act):
        return sum(by_act(j) == act for j, _ in proj_jobs[:q + 1])

    def wait_evac(eng, q):
        act = by_act(proj_jobs[q][0])
        eng.wait_ge(S("h_evac_act") if act else S("h_evac_dve"), evac_count(q, act))

    last_job = {}
    for q, (j, t) in enumerate(proj_jobs):
        last_job[j] = q

    def load_w(sp, j):
        for half in range(2):
            m = 2 * j + half
            if m >= 2:
                sp.wait_ge(S("w_split"), m - 1)
            sp.dma_start(wraw[m % 2][:, :, 0:w_n[j]], w_src[j][:, 4 * half:4 * half + 4, :]).then_inc(S(f"w_in{m % 2}"), 16)

    def split_w_hi(act, j):
        for half in range(2):
            m = 2 * j + half
            act.wait_ge(S(f"w_in{m % 2}"), 16 * (m // 2 + 1))
            if half == 0 and j >= 2:
                act.wait_ge(S("h_mm"), last_job[j - 2] + 1)
            nc.scalar.copy(whi[j % 2][:, 4 * half:4 * half + 4, 0:w_n[j]], wraw[m % 2][:, :, 0:w_n[j]]).then_inc(S("w_hi"), 1)

    def split_w_lo(dve, j):
        for half in range(2):
            m = 2 * j + half
            dve.wait_ge(S("w_hi"), m + 1)
            ks = slice(4 * half, 4 * half + 4)
            nc.vector.tensor_tensor(wlo[j % 2][:, ks, 0:w_n[j]], wraw[m % 2][:, :, 0:w_n[j]],
                                    whi[j % 2][:, ks, 0:w_n[j]].bitcast(F32), ALU.subtract).then_inc(S("w_split"), 1)

    def wait_h(eng):
        for i in range(HST):
            eng.wait_ge(S(f"h_out{i}"), 16 * len(range(i, len(proj_jobs), HST)))

    def mm3(out, jw, k, n, col, rows, first, last):
        hi, lo = xhi[:, k, col:col + rows], xlo[:, k, col:col + rows]
        wh, wl = whi[jw][:, k, 0:n], wlo[jw][:, k, 0:n]
        nc.tensor.matmul(out, hi, wh, start=first, stop=False)
        nc.tensor.matmul(out, hi, wl, start=False, stop=False)
        return nc.tensor.matmul(out, lo, wh, start=False, stop=last)

    def x_src(n, g):
        return bank((2 * n + g) % 4).rearrange("p (k c) -> p k c", k=4)[:, :, 0:tile_rows(n)]

    NITEM = NDB // 2 + 1
    NIDX = 2 * NITEM
    irows = lambda u: 128 if u < NDB // 2 else 64

    def load_gather(sp, u):
        g = G[u % 2]
        if u >= 2:
            sp.wait_ge(S("c_regroup"), 4 * (u - 1))
        if u < NDB // 2:
            for j in range(2 * NPG):
                page = sp.value_load(pt[0:1, 2 * NPG * u + j:2 * NPG * u + j + 1], min_val=0, max_val=NPOOL - 1)
                sp.dma_start(g[8 * j:8 * j + 8].rearrange("c p a k d -> c (p a k d)"),
                             io["cache_nsa_cmp"][0, bass.ds(page, 1)].rearrange("o (c p) a k d -> (o c) (p a k d)", p=16)).then_inc(S(f"g_in{u % 2}"), 16)
        else:
            sp.dma_start(g[0:64].rearrange("c p a k d -> c p (a k d)"),
                         hD[0:T, C_KVC:C_KVC + 256].rearrange("(c p) n -> c p n", p=16)).then_inc(S(f"g_in{u % 2}"), 16)

    def g_in_count(u):
        return 16 * (2 * NPG * (u // 2 + 1) if u < NDB // 2 else 2 * NPG * 2 + 1)

    def load_w1(sp):
        sp.wait_ge(S("w_split"), 2 * (MEMJ + 1))
        for v in range(2):
            sp.dma_start(w1raw[:, v], io["cmp_w1"][0, v].rearrange("(l k q) h -> q l k h", l=2, k=8)).then_inc(S("c_w1"), 16)

    def sp_compress_retention(sp):
        sp.wait_ge(S("h_mm"), len(proj_jobs))
        sp.dma_start(pe_raw[:], io["cmp_pe"][0].rearrange("v (l q) d -> (v l) (q d)", q=2)).then_inc(S("c_const"), 16)
        for v in range(2):
            sp.dma_start(b1[:, v:v + 1], io["cmp_b1"][0, v].rearrange("(h o) -> h o", o=1)).then_inc(S("c_const"), 16)
        sp.dma_start(w2[:], io["cmp_w2"][0].rearrange("v h d -> h v d")).then_inc(S("c_const"), 16)
        sp.dma_start(retc[:], io["c_ret"]).then_inc(S("r_const"), 16)
        sp.dma_start(gnb[:], io["ret_gn"].to_broadcast([128, 256])).then_inc(S("r_const"), 16)
        load_retention(sp, 0)
        load_retention(sp, 1)
        sp.wait_ge(S("c_w1lo"), 4)
        sp.wait_ge(S("c_pe"), 2)
        load_gather(sp, 1)
        sp.wait_ge(S("r_zero"), 2)
        for i in range(4):
            pr, par = i // 2, i % 2
            q = slice(64 * par, 64 * par + 64)
            sp.dma_start(BDs[q, :, pr, q], io["state_ret"][0, :, 2 * pr + par].rearrange("b d e -> d b e")).then_inc(S("r_state"), 16)
        for n in range(2, NT):
            load_retention(sp, n)
            if n % 2 == 0 and n // 2 + 1 < NITEM:
                load_gather(sp, n // 2 + 1)
        sp.wait_ge(S("r_bd"), QT)
        for par in range(2):
            q = slice(64 * par, 64 * par + 64)
            sp.dma_start(io["new_ret_p"][0, 0, par::2].rearrange("h d e -> d h e"), BD[q, :, q]).then_inc(S("out_done"), 16)
        sp.wait_ge(S("r_ns"), 4)
        for i in range(4):
            pr, par = i // 2, i % 2
            q = slice(64 * par, 64 * par + 64)
            sp.dma_start(io["new_ret_s"][0, :, 2 * pr + par].rearrange("b d e -> d b e"), BDs[q, :, pr, q]).then_inc(S("out_done"), 16)

    def load_retention(sp, n):
        if n >= 2:
            sp.wait_ge(S("r_use"), n - 1)
            sp.wait_ge(S("r_rope"), n - 1)
        r = tile_rows(n)
        sp.dma_start(rr[n % 2][0:r], hD[128 * n:128 * n + r, C_QR:C_QR + 768]).then_inc(S(f"r_in{n % 2}"), 16)
        sp.dma_start(rt[n % 2][0:r], io["c_rope"][128 * n:128 * n + r, :]).then_inc(S(f"r_in{n % 2}"), 16)

    def pool_compress_retention(pool):
        ch = Link(pool, S("r_pool"))
        wait_h(pool)
        pool.wait_ge(S("h_mm"), len(proj_jobs))
        regroup(pool, 0)
        regroup(pool, 1)
        for h in range(2):
            pool.memset(hid[h][:], 0.0).then_inc(S("c_zero"), 1)
            pool.memset(cthi[h][:, :, 256:258].bitcast(F32), 0.0).then_inc(S("c_zero"), 1)
            pool.memset(ctlo[h][:, :, 256:258].bitcast(F32), 0.0).then_inc(S("c_zero"), 1)
        pool.memset(BDs[:], 0.0).then_inc(S("r_zero"), 1)
        pool.memset(QZ[:], 0.0).then_inc(S("r_zero"), 1)
        rope(pool, ch, 0)
        rope(pool, ch, 1)
        for n in range(2, NT + 1):
            if n < NIDX:
                regroup(pool, n)
            if n < NT:
                rope(pool, ch, n)
        regroup(pool, NIDX - 1) if NIDX - 1 > NT else None
        pool.wait_ge(S("r_rt"), NT)
        for pr in range(2):
            for b in range(NDB):
                i = pool.tensor_copy(QZ[:, pr, b, DS * b:DS * b + DS], RT[QT % 2][:, pr, DS * b:DS * b + DS])
        i.then_inc(S("r_qz"), 1)
        pool.wait_ge(S("r_rope"), NT)
        for b in range(NDB):
            i = pool.tensor_scalar(KZ[:, b], ro[QT % 2][0:NS_TOK, 256:512], colc[0:NS_TOK, 10 + b:11 + b], None, ALU.mult)
        i.then_inc(S("r_qz"), 1)

    def regroup(pool, idx):
        u, v = idx // 2, idx % 2
        r = irows(u)
        pool.wait_ge(S(f"g_in{u % 2}"), g_in_count(u))
        if idx >= 3:
            pool.wait_ge(S("c_tr"), 4 * (idx - 2))
        for k in range(2):
            pool.tensor_copy(G2[idx % 3][0:r, k], G[u % 2][0:r, :, v, k, :]).then_inc(S("c_regroup"), 1)

    def rope(pool, ch, n):
        r = tile_rows(n)
        pool.wait_ge(S(f"r_in{n % 2}"), 32 * (n // 2 + 1))
        if n >= 2:
            pool.wait_ge(S("r_use"), n - 1)
        v = rr[n % 2][0:r, 0:512].rearrange("p (h t e) -> p h t e", h=8, t=2)
        o = ro[n % 2][0:r].rearrange("p (h t e) -> p h t e", h=8, t=2)
        cs = rt[n % 2][0:r, 0:256].rearrange("p (h e) -> p h e", h=8)
        sn = rt[n % 2][0:r, 256:512].rearrange("p (h e) -> p h e", h=8)
        if n >= 1:
            pool.wait_ge(S("r_rope"), n)
        for i, (x, w) in enumerate(((0, cs), (1, sn), (0, sn), (1, cs))):
            ch.do(pool.tensor_tensor(rtmp[0:r, i], v[:, :, x], w, ALU.mult))
        ch.wait()
        ch.do(pool.tensor_tensor(o[:, :, 0], rtmp[0:r, 0], rtmp[0:r, 1], ALU.subtract))
        pool.tensor_tensor(o[:, :, 1], rtmp[0:r, 2], rtmp[0:r, 3], ALU.add).then_inc(S("r_rope"), 1)

    def pe_compress_retention(pe):
        pe.wait_ge(S("h_evac_act"), evac_count(len(proj_jobs) - 1, True))
        pe.wait_ge(S("h_evac_dve"), evac_count(len(proj_jobs) - 1, False))
        pe.wait_ge(S("c_const"), 16 * 4)
        nc.tensor.transpose(bank(3, 32), pe_raw[:], ident[0:32, 0:32]).then_inc(S("c_pe"), 1)
        pe.wait_ge(S("c_pet"), 1)
        pe.wait_ge(S("c_w1"), 32)
        for v in range(2):
            for i in range(16):
                l = nc.tensor.matmul(psum[:, 512 * 3 + 64 + v:512 * 3 + 65 + v], w1raw[:, v, i // 8, i % 8], pe_t[:, 16 * v + i:16 * v + i + 1],
                                     start=i == 0, stop=i == 15)
        l.then_inc(S("c_pe"), 1)

        def tr(idx, g):
            r = irows(idx // 2)
            pe.wait_ge(S("c_regroup"), 2 * idx + 2)
            c = 4 * idx + g
            if c >= 2:
                pe.wait_ge(S("c_lo"), c - 1)
            for j in range(4):
                kk, kv = 2 * g + j // 2, j % 2
                l = nc.tensor.transpose(bank(c % 2)[:, 128 * j:128 * j + r], G2[idx % 3][0:r, kv, 2 * kk:2 * kk + 2, :], ident[0:r, 0:r])
            l.then_inc(S("c_tr"), 1)

        def hidden(idx):
            u, v = idx // 2, idx % 2
            n = 2 * irows(u)
            if idx == 0:
                pe.wait_ge(S("c_w1lo"), 4)
                pe.wait_ge(S("c_zero"), 6)
            pe.wait_ge(S("c_lo"), 4 * idx + 4)
            if idx >= 1:
                pe.wait_ge(S("c_gelu"), idx)
            out = bank(2, n)
            ch, cl = cthi[idx % 2], ctlo[idx % 2]
            for l in range(2):
                for kk in range(8):
                    first, last = l == 0 and kk == 0, l == 1 and kk == 7
                    wh, wl = w1hi[:, v, l, kk], w1lo[:, v, l, kk]
                    nc.tensor.matmul(out, wh, ch[:, kk, l:l + n], start=first, stop=False)
                    nc.tensor.matmul(out, wh, cl[:, kk, l:l + n], start=False, stop=False)
                    i = nc.tensor.matmul(out, wl, ch[:, kk, l:l + n], start=False, stop=last)
                    if last:
                        i.then_inc(S("c_mm"), 1)
                    if kk % 4 == 3 and idx + 1 < NIDX:
                        tr(idx + 1, 2 * l + kk // 4)

        def second(idx):
            u, v = idx // 2, idx % 2
            pe.wait_ge(S("c_gelu"), idx + 1)
            pe.wait_ge(S("c_kv"), idx if idx < NIDX - 1 else idx + 1) if idx else pe.wait_ge(S("c_bias"), 2)
            h = hid[idx % 2]
            nb = 2 if u < NDB // 2 else 1
            for kv in range(2):
                if v == 0:
                    i = nc.tensor.matmul(psum[64 * kv:64 * kv + 64, 512 * 3:512 * 3 + 64 * nb], w2[:, 0], h[:, nb * kv:nb * kv + nb], start=True, stop=True)
                else:
                    for b in range(nb):
                        o = 512 * 3 + 128 * b + 64 * kv
                        i = nc.tensor.matmul(psum[0:64, o:o + 64], h[:, nb * kv + b], w2[:, 1], start=True, stop=True)
            i.then_inc(S("c_l2"), 1)

        for g in range(4):
            tr(0, g)
        r_transposes(pe, 0)
        r_scores(pe, 0)
        for s in range(NIDX):
            hidden(s)
            if s >= 1:
                second(s - 1)
            if s < NT:
                if s + 1 < NT:
                    r_transposes(pe, s + 1)
                r_output(pe, s)
                if s + 1 < NT:
                    r_scores(pe, s + 1)
        second(NIDX - 1)

    def ct_views(idx, g, dst):
        r = irows(idx // 2)
        return (dst[idx % 2][:, 2 * g:2 * g + 2, 0:2 * r].rearrange("p k (v c) -> p k v c", v=2),
                bank(g % 2).rearrange("p (k v c) -> p k v c", k=2, v=2)[:, :, :, 0:r])

    def act_compress_retention(act):
        act.wait_ge(S("c_w1"), 32)
        act.wait_ge(S("h_mm"), len(proj_jobs))
        for i in range(4):
            nc.scalar.copy(w1hi[:, i // 2, i % 2], w1raw[:, i // 2, i % 2]).then_inc(S("c_w1hi"), 1)

        def hi(idx):
            if idx >= 2:
                act.wait_ge(S("c_mm"), idx - 1)
            for g in range(4):
                act.wait_ge(S("c_tr"), 4 * idx + g + 1)
                dst, src = ct_views(idx, g, cthi)
                nc.scalar.copy(dst, src).then_inc(S("c_hi"), 1)

        def gelu(idx):
            n = irows(idx // 2) // 32
            act.wait_ge(S("c_mm"), idx + 1)
            if idx >= 2:
                act.wait_ge(S("c_l2"), idx - 1)
            nc.scalar.activation(hid[idx % 2][:, 0:n, 0:63], bank(2, 64 * n).rearrange("p (g c) -> p g c", c=64)[:, :, 0:63],
                                 ACT.Gelu_apprx_tanh, bias=small[:, 64 + idx % 2:65 + idx % 2]).then_inc(S("c_gelu"), 1)

        def transposed(n):
            r = tile_rows(n)
            act.wait_ge(S("r_tr"), n + 1)
            if n >= 2:
                act.wait_ge(S("r_use"), n - 1)
            nc.scalar.copy(RT[n % 2][:, :, 0:r], bank(4).rearrange("p (i c) -> p i c", i=4)[:, :, 0:r]).then_inc(S("r_rt"), 1)

        hi(0)
        transposed(0)
        act.wait_ge(S("c_bias"), 2)
        act.wait_ge(S("c_zero"), 6)
        for s in range(NIDX):
            if s + 1 < NIDX:
                hi(s + 1)
            gelu(s)
            if s + 1 < NT:
                transposed(s + 1)
        act.wait_ge(S("c_l2"), NIDX - 1)
        for kv in range(2):
            rows = slice(64 * kv, 64 * kv + 64)
            nc.scalar.copy(KCp[rows, kv, :], psum[rows, 512 * 3:512 * 3 + 64]).then_inc(S("c_kcp_hi"), 1)
        act.wait_ge(S("r_ve"), 1)
        nc.scalar.activation(small[:, 116:152], small[:, 80:116], ACT.Sqrt).then_inc(S("r_sd"), 1)

    def dve_compress_retention(dve):
        dve.wait_ge(S("c_pe"), 1)
        nc.vector.tensor_copy(pe_t[:], bank(3, 32)).then_inc(S("c_pet"), 1)
        for i in range(4):
            dve.wait_ge(S("c_w1hi"), i + 1)
            nc.vector.tensor_tensor(w1lo[:, i // 2, i % 2], w1raw[:, i // 2, i % 2], w1hi[:, i // 2, i % 2].bitcast(F32), ALU.subtract).then_inc(S("c_w1lo"), 1)
        dve.wait_ge(S("c_pe"), 2)
        for v in range(2):
            nc.vector.tensor_tensor(small[:, 64 + v:65 + v], psum[:, 512 * 3 + 64 + v:512 * 3 + 65 + v], b1[:, v:v + 1], ALU.add).then_inc(S("c_bias"), 1)

        def lo(idx):
            for g in range(4):
                dve.wait_ge(S("c_hi"), 4 * idx + g + 1)
                dst, src = ct_views(idx, g, ctlo)
                hv, _ = ct_views(idx, g, cthi)
                nc.vector.tensor_tensor(dst, src, hv.bitcast(F32), ALU.subtract).then_inc(S("c_lo"), 1)

        def keep(idx):
            u, v = idx // 2, idx % 2
            dve.wait_ge(S("c_l2"), idx + 1)
            if u < NDB // 2:
                if v == 0:
                    i = nc.vector.tensor_copy(KCs[:, 2 * u:2 * u + 2, :], bank(3, 128))
                else:
                    i = nc.vector.tensor_copy(VC[:, 2 * u:2 * u + 2, :], psum[0:64, 512 * 3:512 * 3 + 256])
            elif v == 1:
                i = nc.vector.tensor_copy(VC[:, NDB, :], psum[0:64, 512 * 3:512 * 3 + 128])
            else:
                dve.wait_ge(S("c_kcp_hi"), 2)
                nc.vector.tensor_tensor(KCp[64:128, 0, :], psum[0:64, 512 * 3:512 * 3 + 64], KCp[0:64, 0, :].bitcast(F32), ALU.subtract).then_inc(S("c_kv"), 1)
                i = nc.vector.tensor_tensor(KCp[0:64, 1, :], psum[64:128, 512 * 3:512 * 3 + 64], KCp[64:128, 1, :].bitcast(F32), ALU.subtract)
            i.then_inc(S("c_kv"), 1)

        lo(0)
        rv = retention_dve(dve)
        rv.scores(0)
        for s in range(NIDX):
            if s + 1 < NIDX:
                lo(s + 1)
            if s >= 1:
                keep(s - 1)
            if s < NT:
                rv.norm(s)
                rv.state(s)
                if s + 1 < NT:
                    rv.scores(s + 1)
        keep(NIDX - 1)
        rv.finish()

    N_CKV = NIDX + 1

    KV_BANKS = (5, 6, 4, 5)

    def r_transposes(pe, n):
        r = tile_rows(n)
        pe.wait_ge(S("r_rope"), n + 1)
        if n >= 1:
            pe.wait_ge(S("r_kvr"), n - 1) if n > 1 else None
            pe.wait_ge(S("r_rt"), n)
        for i in range(4):
            l = nc.tensor.transpose(bank(4)[:, 128 * i:128 * i + r], ro[n % 2][0:r, 128 * i:128 * i + 128], ident[0:r, 0:r])
        l.then_inc(S("r_tr"), 1)

    def r_scores(pe, n):
        r = tile_rows(n)
        pe.wait_ge(S("r_rt"), n + 1)
        if n >= 1:
            pe.wait_ge(S("r_at"), 2 * n)
        for h in range(4):
            q = slice(64 * (h % 2), 64 * (h % 2) + 64)
            o = 512 * (5 + h % 2) + 128 * (h // 2)
            l = nc.tensor.matmul(psum[0:r, o:o + r], RT[n % 2][q, 2 + h // 2, 0:r], RT[n % 2][q, h // 2, 0:r], start=True, stop=True)
        l.then_inc(S("r_sc"), 1)

    def r_output(pe, n):
        r = tile_rows(n)
        v = rr[n % 2]
        pe.wait_ge(S("r_at"), 2 * n + 2)
        if n >= 1:
            pe.wait_ge(S("r_o"), n)
        o = 512 * 7
        if n < QT:
            pe.wait_ge(S("r_bd"), n) if n else pe.wait_ge(S("r_bd0"), 1)
            for pr in range(2):
                nc.tensor.matmul(psum[0:r, o + 128 * pr:o + 128 * pr + 128], RT[n % 2][:, pr, 0:r], BD[:, pr, :], start=pr == 0, stop=False, skip_group_check=True)
        else:
            pe.wait_ge(S("r_state"), 64)
            pe.wait_ge(S("r_qz"), 1)
            for pr in range(2):
                for b in range(NDB):
                    nc.tensor.matmul(psum[0:r, o + 128 * pr:o + 128 * pr + 128], QZ[:, pr, b, :], BDs[:, b, pr, :], start=pr == 0 and b == 0, stop=False, skip_group_check=True)
        for h in range(4):
            l = nc.tensor.matmul(psum[0:r, o + 64 * h:o + 64 * h + 64], AT[n % 2][0:r, h % 2, h // 2, 0:r], v[0:r, 512 + 64 * h:576 + 64 * h], start=False, stop=True, skip_group_check=True)
        if n < QT:
            l.then_inc(S("r_out"), 1)
            pe.wait_ge(S("r_rt"), n + 2)
            for pr in range(2):
                l = nc.tensor.matmul(psum[:, 512 * 4 + 128 * pr:512 * 4 + 128 * pr + 128], ro[n % 2][:, 256 + 128 * pr:384 + 128 * pr], v[:, 512 + 128 * pr:640 + 128 * pr], start=True, stop=True)
            l.then_inc(S("r_use"), 1)
        else:
            l.then_inc(S("r_out"), 1)
            pe.wait_ge(S("r_qz"), 2)
            pe.wait_ge(S("r_kvr"), QT)
            pe.wait_ge(S("r_at"), 2 * NT)
            for b in range(NDB):
                if b == 6:
                    l.then_inc(S("r_kvs"), 1)
                    pe.wait_ge(S("r_ns"), 1)
                for pr in range(2):
                    o2 = 512 * KV_BANKS[b // 2] + 256 * (b % 2) + 128 * pr
                    l = nc.tensor.matmul(psum[:, o2:o2 + 128], KZ[:, b, 128 * pr:128 * pr + 128], v[0:r, 512 + 128 * pr:640 + 128 * pr], start=True, stop=True)
            l.then_inc(S("r_use"), 1)

    class retention_dve:

        def __init__(self, dve):
            self.dve, self.ch = dve, Link(dve, S("r_dve"))
            self.ch.step(nc.vector.memset(small[:, 80:116], 1.0))
            nc.vector.memset(BD[:], 0.0).then_inc(S("r_bd0"), 1)
            dve.wait_ge(S("r_bd0"), 1)
            dve.wait_ge(S("r_const"), 32)


        def scores(self, n):
            dve = self.dve
            r = tile_rows(n)
            mask = retc[0:r, (0 if n < QT else 128):(0 if n < QT else 128) + r]
            dve.wait_ge(S("r_sc"), n + 1)
            if n >= 2:
                dve.wait_ge(S("r_use"), n - 1)
            for par in range(2):
                for pr in range(2):
                    o = 512 * (5 + par) + 128 * pr
                    l = nc.vector.tensor_tensor(AT[n % 2][0:r, par, pr, 0:r], psum[0:r, o:o + r], mask, ALU.mult)
                l.then_inc(S("r_at"), 1)

        def norm(self, n):
            dve, ch = self.dve, self.ch
            r = tile_rows(n)
            dve.wait_ge(S("r_out"), n + 1)
            o = psum[0:r, 512 * 7:512 * 7 + 256].rearrange("p (h e) -> p h e", h=4)
            oc = OC[0:r, n].rearrange("p (h e) -> p h e", h=4)
            mu, var = small[0:r, 152:156], small[0:r, 80 + 4 * n:84 + 4 * n]
            ch.step(nc.vector.tensor_reduce(out=mu, in_=o, op=ALU.add, axis=AX.X))
            ch.step(nc.vector.tensor_scalar(mu, mu, 1.0 / HD, None, ALU.mult))
            nc.vector.tensor_tensor(oc, o, mu.rearrange("p (h o) -> p h o", o=1).to_broadcast([r, 4, HD]), ALU.subtract).then_inc(S("r_o"), 1)
            dve.wait_ge(S("r_o"), n + 1)
            ch.step(nc.vector.tensor_tensor(rsq[0:r], OC[0:r, n], OC[0:r, n], ALU.mult))
            ch.step(nc.vector.tensor_reduce(out=var, in_=rsq[0:r].rearrange("p (h e) -> p h e", h=4), op=ALU.add, axis=AX.X))

        def state(self, n):
            dve, ch, bdm = self.dve, self.ch, retc[:, 256:384]
            dve.wait_ge(S("r_use"), n + 1) if n < QT else dve.wait_ge(S("r_kvs"), 1)
            if n < QT:
                for pr in range(2):
                    o = 512 * 4 + 128 * pr
                    l = nc.vector.tensor_tensor(kvt[:, pr], psum[:, o:o + 128], bdm, ALU.mult)
                l.then_inc(S("r_kvr"), 1)
                dve.wait_ge(S("r_kvr"), n + 1)
                ch.step(nc.vector.tensor_tensor(kvt[:, 0:2], kvt[:, 0:2], BD[:], ALU.add))
                nc.vector.tensor_scalar(BD[:, 0], kvt[:, 0], colc[:, 0:1], None, ALU.mult)
                nc.vector.tensor_scalar(BD[:, 1], kvt[:, 1], colc[:, 1:2], None, ALU.mult).then_inc(S("r_bd"), 1)
                dve.wait_ge(S("r_bd"), n + 1)
            else:
                for g in range(4):
                    if g == 3:
                        dve.wait_ge(S("r_use"), NT)
                    o = 512 * KV_BANKS[g]
                    for i in range(4):
                        ch.do(nc.vector.tensor_tensor(kvt[:, i], psum[:, o + 128 * i:o + 128 * i + 128], bdm, ALU.mult))
                    ch.wait()
                    ch.step(nc.vector.tensor_tensor(kvt[:], kvt[:], BDs[:, 2 * g:2 * g + 2].rearrange("p b r e -> p (b r) e"), ALU.add))
                    for pr in range(2):
                        l = nc.vector.tensor_scalar(BDs[:, 2 * g:2 * g + 2, pr], kvt[:].rearrange("p (b r) e -> p b r e", b=2)[:, :, pr], colc[:, 2 + pr:3 + pr], None, ALU.mult)
                    l.then_inc(S("r_ns"), 1)
                    dve.wait_ge(S("r_ns"), g + 1)

        def finish(self):
            dve, ch = self.dve, self.ch
            v, sd, rs = small[:, 80:116], small[:, 116:152], small[:, 116:152]
            nc.vector.tensor_scalar(v, v, 1.0 / HD, EPS, ALU.mult, ALU.add).then_inc(S("r_ve"), 1)
            dve.wait_ge(S("r_sd"), 1)
            ch.step(nc.vector.reciprocal(rs, sd))
            rsqrt_polish(dve, ch, rs, v, small[:, 0:36])
            for n in range(NT):
                r = tile_rows(n)
                oc = OC[0:r, n].rearrange("p (h e) -> p h e", h=4)
                ch.step(nc.vector.tensor_tensor(oc, oc, rs[0:r, 4 * n:4 * n + 4].rearrange("p (h o) -> p h o", o=1).to_broadcast([r, 4, HD]), ALU.mult))
                nc.vector.tensor_tensor(OC[0:r, n], OC[0:r, n], gnb[0:r], ALU.mult).then_inc(S("r_done"), 1)

    def rsqrt_polish(dve, ch, y, v, tmp):
        ch.step(nc.vector.tensor_tensor(tmp, y, y, ALU.mult))
        ch.step(nc.vector.tensor_tensor(tmp, tmp, v, ALU.mult))
        ch.step(nc.vector.tensor_scalar(tmp, tmp, -0.5, 1.5, ALU.mult, ALU.add))
        ch.step(nc.vector.tensor_tensor(y, y, tmp, ALU.mult))

    UN = 18
    SM = 28
    GROUPS = (0, 7, 15, 22, SM)
    NG = len(GROUPS) - 1

    def group(num):
        return sum(num >= g for g in GROUPS) - 1

    def softmaxes(v):
        i, l = v // UN, v % UN
        base = 1024 * (v % 2)
        if l >= 16:
            return [(24 + 2 * (l - 16) + r, 3, 2 * (l - 16) + r, 0, NM, [(base + 512 * r, NM)], 256 * r) for r in range(2)]
        h, k0 = l // 2, 0 if l % 2 == 0 else max(0, i - WIN // 128)
        n = 128 * (i + 1 - k0)
        halves = [(base, n)] if n <= 512 else [(base, n // 2), (base + 512, n // 2)]
        if l % 2 == 0:
            return [(3 * h, 0, h, 0, n, halves, 0)]
        return [(3 * h + 1, 1, h, k0, n, halves, 0), (3 * h + 2, 2, h, 0, 64, [(base + 512 + 448, 64)], 640)]

    def tiles_of(v):
        return [(a, k, min(128, s[4])) for a, s in enumerate(softmaxes(v)) for k in range((s[4] + 127) // 128)]

    def prompt_schedule():
        chunks, steps, waiting = [], [], []

        def add(c):
            chunks.append(c)
            steps.append(("t", len(chunks) - 1))

        def pv():
            c = waiting.pop(0)
            steps.append(("pv", c))
            _, v, tiles = chunks[c]
            for a, k, _ in tiles:
                s = softmaxes(v)[a]
                if 128 * (k + 1) >= s[4] and s[0] + 1 in GROUPS:
                    steps.append(("norm", NG * (v // UN) + group(s[0])))

        for part in range(3):
            add(("q", 0, part))
        for v in range(2):
            steps.extend([("qk", v), ("sm", v)])
        for v in range(UN * QT):
            i, l = v // UN, v % UN
            if v + 2 < UN * QT:
                steps.append(("qk", v + 2))
            tiles = tiles_of(v)
            for first in range(0, len(tiles), 4):
                add(("p", v, tiles[first:first + 4]))
                if len(waiting) == 2:
                    pv()
                waiting.append(len(chunks) - 1)
            if v + 2 < UN * QT:
                steps.append(("sm", v + 2))
            if i >= 1 and l in (5, 7):
                add(("x", i - 1, (l - 5) // 2))
            if i + 1 < QT and l in (9, 11, 13):
                add(("q", i + 1, (l - 9) // 2))
        while waiting:
            pv()
        for part in range(2):
            add(("x", QT - 1, part))
        return chunks, steps

    p_chunks, p_steps = prompt_schedule()

    def chunk_act(c):
        return p_chunks[c][0] == "p" and c % 2 == 0

    def chunks_before(c, test):
        return sum(test(k) for k in range(c))

    def wait_chunk_read(eng, c):
        if chunk_act(c):
            eng.wait_ge(S("pt_act"), chunks_before(c + 1, chunk_act))
        else:
            eng.wait_ge(S("pt_dve"), c + 1 - chunks_before(c + 1, chunk_act))

    p_index = [k for k, c in enumerate(p_chunks) if c[0] == "p"]
    p_rank = {c: n for n, c in enumerate(p_index)}
    last_chunk = {p_chunks[c][1]: c for c in p_index}
    q_last = {c[1]: k for k, c in enumerate(p_chunks) if c[0] == "q"}
    x_last = {c[1]: k for k, c in enumerate(p_chunks) if c[0] == "x"}
    split_rank = {c: n for n, c in enumerate([k for k, c in enumerate(p_chunks) if c[0] != "p"])}

    pv_done, n_pv = {}, 0
    for what, n in p_steps:
        if what == "pv":
            n_pv += 1
        elif what == "norm":
            pv_done[n] = n_pv

    def s_view(s):
        at, n = s[5][0]
        if len(s[5]) == 1:
            return psum[:, at:at + n]
        return psum[:, at:at + 1024].rearrange("p (a b) -> p a b", a=2)[:, :, 0:n]

    def sp_prompt(sp):
        sp.wait_ge(S("r_done"), NT)
        sp.wait_ge(S("out_done"), 16 * (7 + 2 + 4))
        sp.dma_start(mraw[:], io["c_mask"]).then_inc(S("p_const"), 16)
        for br, c in enumerate((C_KVS, C_KVW)):
            sp.dma_start(Ktok[:, br], hD[0:T, c:c + 128].rearrange("(t p) n -> p t n", p=128)).then_inc(S("p_const"), 16)
            sp.dma_start(V[:, br], hD[0:T, c + 128:c + 256].rearrange("(t p) n -> p t n", p=128)).then_inc(S("p_const"), 16)
        sp.dma_start(Kmt[:], new_mem[:, 0:256].rearrange("(t p) n -> p t n", p=128)).then_inc(S("p_const"), 16)
        sp.dma_start(VM[:], new_mem[:, 256:512].rearrange("(t p) n -> p t n", p=128)).then_inc(S("p_const"), 16)
        for i in range(QT):
            rows = slice(128 * i, 128 * i + 128)
            if i >= 2:
                sp.wait_ge(S("p_tr"), q_last[i - 2] + 1)
            for j in range(2):
                sp.dma_start(qd[i % 2][:, 0:8, j, :], hD[rows, 0:512].rearrange("p (h d) -> p h d", d=HD)).then_inc(S(f"p_q{i % 2}"), 16)
                sp.dma_start(qd[i % 2][:, 8:12, j, :], hD[rows, C_QM:C_QM + 256].rearrange("p (h d) -> p h d", d=HD)).then_inc(S(f"p_q{i % 2}"), 16)
            if i >= 2:
                sp.wait_ge(S("p_norm"), NG * (i - 1))
                sp.wait_ge(S("p_mix"), i - 1)
            sp.dma_start(gt[i % 2][:], hD[rows, C_G:C_G + 24]).then_inc(S(f"p_g{i % 2}"), 16)
            for o, c, n in ((0, C_ZN, 512), (512, C_ZR, 256), (768, C_ZM, 256)):
                sp.dma_start(zt[i % 2][:, o:o + n], hD[rows, c:c + n]).then_inc(S(f"p_z{i % 2}"), 16)

    def pe_prompt(pe):
        pe.wait_ge(S("r_done"), NT)
        pe.wait_ge(S("p_const"), 16 * 7)
        for br in range(2):
            for half in range(2):
                for j in range(4):
                    l = nc.tensor.transpose(bank(2 * br + half)[:, 128 * j:128 * j + 128], Ktok[:, br, 4 * half + j, :], ident[:])
                l.then_inc(S("p_ktr"), 1)
        for pr in range(2):
            for mt in range(2):
                l = nc.tensor.transpose(bank(4)[:, 256 * pr + 128 * mt:256 * pr + 128 * mt + 128], Kmt[:, mt, 128 * pr:128 * pr + 128], ident[:])
        l.then_inc(S("p_ktr"), 1)
        pe.wait_ge(S("p_klo"), 10)
        pe.wait_ge(S("p_maskb"), 1)

        def qk(v):
            i = v // UN
            if v % UN == 0:
                pe.wait_ge(S("pt_dve"), chunks_final_dve(q_last[i]))
            if v >= 2:
                pe.wait_ge(S("p_exp"), sm_count(v - 2))
            for s in softmaxes(v):
                _, b, h, k0, n, views, _ = s
                for a, (at, w) in enumerate(views):
                    o = psum[:, at:at + w]
                    keys = slice(128 * k0 + w * a, 128 * k0 + w * a + w)
                    k = KM[:, h, keys] if b == 3 else KCp[:, h // 4, :] if b == 2 else KS[:, b, h // 4, keys]
                    masks = []
                    if b == 2:
                        masks.append((o, M_CMP + 64 * i))
                    if b == 1 and i >= WIN // 128 and a == 0:
                        masks.append((o[:, 0:128], M_TAIL))
                    if b < 2 and a == len(views) - 1:
                        masks.append((o[:, w - 128:w], M_CAUSAL))
                    hq = h if b < 3 else 8 + h
                    nc.tensor.matmul(o, QA[i % 2][:, hq, :], k, start=True, stop=False)
                    l = nc.tensor.matmul(o, QB[i % 2][:, hq, :], k, start=False, stop=not masks)
                    for n_m, (om, m_at) in enumerate(masks):
                        l = nc.tensor.matmul(om, identb[:], maskb[:, m_at:m_at + om.shape[1]], start=False, stop=n_m == len(masks) - 1)
            l.then_inc(S("p_qk"), 1)

        def transposes(c):
            kind = p_chunks[c]
            if c >= 3:
                wait_chunk_read(pe, c - 3)
            o = bank(4 + c % 3)
            if kind[0] == "p":
                _, v, tiles = kind
                sms = softmaxes(v)
                pe.wait_ge(S("p_exp"), sm_count(v) - len(sms) + 1 + tiles[-1][0])
                for j, (a, k, w) in enumerate(tiles):
                    at = sms[a][6] + 128 * k
                    l = nc.tensor.transpose(o[0:w, 128 * j:128 * j + 128], P[v % 2][:, at:at + w], ident[:])
            elif kind[0] == "q":
                _, i, part = kind
                pe.wait_ge(S(f"p_q{i % 2}"), 64 * (i // 2 + 1))
                for j in range(4):
                    l = nc.tensor.transpose(o[:, 128 * j:128 * j + 128], qd[i % 2][:, 4 * part + j], ident[:])
            else:
                _, i, part = kind
                pe.wait_ge(S("p_mix"), i + 1)
                for j in range(4):
                    l = nc.tensor.transpose(o[:, 128 * j:128 * j + 128], mx[i % 2][:, 512 * part + 128 * j:512 * part + 128 * j + 128], ident[:])
            l.then_inc(S("p_tr"), 1)

        def pv(c):
            _, v, tiles = p_chunks[c]
            i, sms = v // UN, softmaxes(v)
            wait_chunk_read(pe, c)
            for j, (a, k, w) in enumerate(tiles):
                num, b, h, k0, keys = sms[a][0:5]
                g = NG * i + group(num)
                if k == 0 and num in GROUPS and g >= 1:
                    pe.wait_ge(S("p_norm"), g)
                at = 512 * 7 + HD * (num - GROUPS[group(num)])
                kv = HD * (h // 4)
                val = VM[:, k, HD * h:HD * h + HD] if b == 3 else VC[0:w, NDB, kv:kv + HD] if b == 2 else V[:, b, k0 + k, kv:kv + HD]
                l = nc.tensor.matmul(psum[:, at:at + HD], PTs[p_rank[c] % NPT][0:w, 128 * j:128 * j + 128], val, start=k == 0, stop=128 * (k + 1) >= keys)
            l.then_inc(S("p_pv"), 1)

        for what, n in p_steps:
            if what == "qk":
                qk(n)
            elif what == "t":
                transposes(n)
            elif what == "pv":
                pv(n)

    def sm_count(v):
        return SM * (v // UN) + softmaxes(v)[-1][0] + 1

    def chunks_final_dve(c):
        return c + 1 - chunks_before(c + 1, chunk_act)

    def pt_copy(eng, copy, c, sem):
        n, w = len(p_chunks[c][2]), max(t[2] for t in p_chunks[c][2])
        r = p_rank[c]
        eng.wait_ge(S("p_tr"), c + 1)
        if r >= NPT:
            eng.wait_ge(S("p_pv"), r - NPT + 1)
        copy(PTs[r % NPT][0:w, 0:128 * n], bank(4 + c % 3)[0:w, 0:128 * n]).then_inc(sem, 1)

    def split_dst(c, lo):
        kind, i, part = p_chunks[c]
        if kind == "q":
            return (QB if lo else QA)[i % 2][:, 4 * part:4 * part + 4, :]
        return (xlo if lo else xhi)[:, 4 * part:4 * part + 4, tile_col(i):tile_col(i) + 128]

    def act_prompt(act):
        for n in range(4):
            br, half = n // 2, n % 2
            act.wait_ge(S("p_ktr"), n + 1)
            for kv in range(2):
                rows = slice(64 * kv, 64 * kv + 64)
                nc.scalar.copy(KS[rows, br, kv, 512 * half:512 * half + 512], psum[rows, 512 * n:512 * n + 512]).then_inc(S("p_khi"), 1)
        act.wait_ge(S("p_ktr"), 5)
        for par in range(2):
            rows = slice(64 * par, 64 * par + 64)
            nc.scalar.copy(KM[rows, par::2, :], psum[rows, 2048:2560].rearrange("p (h m) -> p h m", h=2)).then_inc(S("p_khi"), 1)
        for what, n in p_steps:
            if what == "sm":
                v, i = n, n // UN
                if v >= 2:
                    act.wait_ge(S("p_tr"), last_chunk[v - 2] + 1)
                if v % UN == 0 and i >= 2:
                    act.wait_ge(S("p_norm"), NG * (i - 1))
                act.wait_ge(S("p_nb"), sm_count(v))
                for s in softmaxes(v):
                    g = SM * i + s[0]
                    dst = P[v % 2][:, s[6]:s[6] + s[4]]
                    if len(s[5]) == 2:
                        dst = dst.rearrange("p (a b) -> p a b", a=2)
                    nc.scalar.activation(dst, s_view(s), ACT.Exp, bias=nb[:, g % NNB:g % NNB + 1], scale=SCALE,
                                         accum_out=ssum[:, i % 2, s[0]:s[0] + 1]).then_inc(S("p_exp"), 1)
            elif what == "t":
                if p_chunks[n][0] != "p":
                    kind, i, part = p_chunks[n]
                    act.wait_ge(S("p_tr"), n + 1)
                    if kind == "q" and i >= 2:
                        act.wait_ge(S("p_qk"), UN * (i - 1))
                    nc.scalar.copy(split_dst(n, False), bank(4 + n % 3).rearrange("p (j c) -> p j c", j=4)).then_inc(S("p_shi"), 1)
                elif chunk_act(n):
                    pt_copy(act, nc.scalar.copy, n, S("pt_act"))

    def dve_prompt(dve):
        ch = Link(dve, S("p_dve"))
        for n in range(4):
            br, half = n // 2, n % 2
            for kv in range(2):
                rows, other = slice(64 * kv, 64 * kv + 64), slice(64 - 64 * kv, 128 - 64 * kv)
                ks = slice(512 * half, 512 * half + 512)
                dve.wait_ge(S("p_khi"), 2 * n + kv + 1)
                nc.vector.tensor_tensor(KS[other, br, kv, ks], psum[rows, 512 * n:512 * n + 512], KS[rows, br, kv, ks].bitcast(F32), ALU.subtract).then_inc(S("p_klo"), 1)
        for par in range(2):
            rows, other = slice(64 * par, 64 * par + 64), slice(64 - 64 * par, 128 - 64 * par)
            dve.wait_ge(S("p_khi"), 9 + par)
            nc.vector.tensor_tensor(KM[other, par::2, :], psum[rows, 2048:2560].rearrange("p (h m) -> p h m", h=2), KM[rows, par::2, :].bitcast(F32), ALU.subtract).then_inc(S("p_klo"), 1)
        nc.vector.tensor_copy(maskb[:], mraw[:]).then_inc(S("p_maskb"), 1)
        ch.step(nc.vector.memset(gw[:, :, 24:28], 1.0))
        for what, n in p_steps:
            if what == "sm":
                v, i = n, n // UN
                if v % UN == 0:
                    dve.wait_ge(S(f"p_g{i % 2}"), 16 * (i // 2 + 1))
                    g = gt[i % 2][:].rearrange("p (b h) -> p h b", b=3)
                    w = gw[:, i % 2, 0:24].rearrange("p (h b) -> p h b", b=3)
                    ch.do(nc.vector.tensor_copy(w[:, :, 0:2], g[:, :, 1:3]))
                    ch.do(nc.vector.tensor_copy(w[:, :, 2], g[:, :, 0]))
                    ch.wait()
                dve.wait_ge(S("p_qk"), v + 1)
                for s in softmaxes(v):
                    g = SM * i + s[0]
                    if g >= NNB:
                        dve.wait_ge(S("p_exp"), g - NNB + 1)
                    m = nb[:, NNB + g % NNB:NNB + g % NNB + 1]
                    ch.step(nc.vector.tensor_reduce(out=m, in_=s_view(s), op=ALU.max, axis=AX.X if len(s[5]) == 1 else AX.XY))
                    nc.vector.tensor_scalar(nb[:, g % NNB:g % NNB + 1], m, NEG / 10, -SCALE, ALU.max, ALU.mult).then_inc(S("p_nb"), 1)
            elif what == "t":
                if p_chunks[n][0] != "p":
                    dve.wait_ge(S("p_shi"), split_rank[n] + 1)
                    nc.vector.tensor_tensor(split_dst(n, True), bank(4 + n % 3).rearrange("p (j c) -> p j c", j=4), split_dst(n, False).bitcast(F32), ALU.subtract).then_inc(S("pt_dve"), 1)
                elif not chunk_act(n):
                    pt_copy(dve, nc.vector.tensor_copy, n, S("pt_dve"))
            elif what == "norm":
                i, g = n // NG, n % NG
                us, n_g = slice(GROUPS[g], GROUPS[g + 1]), GROUPS[g + 1] - GROUPS[g]
                w = rw[:, n % 2, 0:n_g]
                if n >= 2:
                    dve.wait_ge(S("p_norm"), n - 1)
                ch.step(nc.vector.tensor_scalar(w, ssum[:, i % 2, us], 1e-30, None, ALU.max))
                ch.step(nc.vector.reciprocal(w, w))
                ch.step(nc.vector.tensor_tensor(w, w, gw[:, i % 2, us], ALU.mult))
                dve.wait_ge(S("p_pv"), pv_done[n])
                if g == 0 and i >= 1:
                    dve.wait_ge(S("p_mix"), i)
                nc.vector.tensor_tensor(Oi[:, us, :], bank(7, n_g * HD).rearrange("p (u d) -> p u d", d=HD),
                                        w.rearrange("p (u o) -> p u o", o=1).to_broadcast([128, n_g, HD]), ALU.mult).then_inc(S("p_norm"), 1)

    def pool_mix(pool, ch, r, on, om, oc, z, m, done):
        mn = m[0:r, 0:512].rearrange("p (h d) -> p h d", d=HD)
        ch.do(pool.tensor_tensor(m[0:r, 512:768], oc, z[0:r, 512:768], ALU.mult))
        ch.do(pool.tensor_tensor(m[0:r, 768:1024].rearrange("p (h d) -> p h d", d=HD), om, z[0:r, 768:1024].rearrange("p (h d) -> p h d", d=HD), ALU.mult))
        ch.step(pool.tensor_tensor(mn, on[:, :, 0], on[:, :, 1], ALU.add))
        ch.step(pool.tensor_tensor(mn, mn, on[:, :, 2], ALU.add))
        pool.tensor_tensor(m[0:r, 0:512], m[0:r, 0:512], z[0:r, 0:512], ALU.mult).then_inc(S(done), 1)

    def pool_prompt(pool):
        ch = Link(pool, S("p_pool"))
        for i in range(QT):
            pool.wait_ge(S("p_norm"), NG * (i + 1))
            pool.wait_ge(S(f"p_z{i % 2}"), 48 * (i // 2 + 1))
            if i >= 2:
                pool.wait_ge(S("p_tr"), x_last[i - 2] + 1)
            pool_mix(pool, ch, 128, Oi[:, 0:24].rearrange("p (h b) d -> p h b d", b=3), Oi[:, 24:28], OC[:, i], zt[i % 2], mx[i % 2], "p_mix")

    NPAIR = NDB // 2
    T_NEWS, T_NEWW, T_CMP = 12, 13, 14
    S_CHUNKS = [[(0, 128), (1, 128), (2, 128), (3, 128)], [(4, 128), (5, 128), (6, 128), (7, 128)],
                [(8, 128), (9, 128), (10, 128), (11, 128)], [(T_NEWS, 64), (T_NEWW, 64), (T_CMP, 63)]]
    NSC = len(S_CHUNKS)
    P_DONE = NG * QT

    def sp_sample(sp):
        sp.wait_ge(S("p_mix"), QT)
        sp.wait_ge(S("p_tr"), len(p_chunks))
        sp.wait_ge(S("p_pv"), len(p_index))
        sp.wait_ge(S("p_norm"), P_DONE)
        rows = hD[T:T + NS_TOK, :]
        for kv in range(2):
            sp.dma_start(qs[:, :, kv, :], rows[:, 256 * kv:256 * kv + 256].rearrange("p (g d) -> p g d", g=4)).then_inc(S("s_const"), 16)
        sp.dma_start(qms[:], rows[:, C_QM:C_QM + 256]).then_inc(S("s_const"), 16)
        sp.dma_start(kvn[:], rows[:, C_KVS:C_KVS + 512]).then_inc(S("s_const"), 16)
        sp.dma_start(csum[:], io["c_sum"]).then_inc(S("s_const"), 16)
        sp.dma_start(cblk[:], io["c_blk"]).then_inc(S("s_const"), 16)
        for b in range(NDB):
            sp.dma_start(MK[b // 4][:, b % 4], io["cache_mem"][0, b].rearrange("(t p) a h d -> p t (a h d)", p=128)).then_inc(S(f"m_in{b // 4}"), 16)
        for n, (o, c, w) in enumerate(((0, C_ZN, 512), (512, C_ZR, 256), (768, C_ZM, 256))):
            sp.dma_start(zs[:, o:o + w], rows[:, c:c + w]).then_inc(S("s_z"), 16)
        sp.dma_start(gs[:], rows[:, C_G:C_G + 24]).then_inc(S("s_z"), 16)
        for p in range(NPAIR):
            if p < 2:
                sp.wait_ge(S("m_pv"), 2)
            else:
                sp.wait_ge(S("s_pv"), p - 1)
            for j in range(2 * NPG):
                page = sp.value_load(pt[0:1, 2 * NPG * p + j:2 * NPG * p + j + 1], min_val=0, max_val=NPOOL - 1)
                sp.dma_start(SG[p % 2][:, j // NPG, j % NPG, :], io["cache_nsa_slc"][0, bass.ds(page, 1)].rearrange("o t a k d -> (o t) (a k d)")).then_inc(S(f"s_in{p % 2}"), 16)
            for b in range(2):
                sp.dma_start(WG[p % 2][:, b], io["cache_nsa_win"][0, 2 * p + b].rearrange("(t p) a k d -> p t (a k d)", p=128)).then_inc(S(f"s_in{p % 2}"), 16)
            if p >= 1:
                store_pair(sp, p - 1)
            if p == 1:
                for g in range(2):
                    sp.wait_ge(S("m_o"), g + 1)
                    sp.dma_start(omD[128 * g:128 * g + 128, :], OMs[:, g, :]).then_inc(S("o_out"), 16)
        store_pair(sp, NPAIR - 1)
        sp.wait_ge(S("o_out"), 16 * (NPAIR + 2))
        for b in range(NDB):
            sp.dma_start(on_s[DS * b:DS * b + DS], oD[64 * b:64 * b + 64, :].rearrange("(h s) (r d) -> s h r d", s=DS, d=HD)).then_inc(S("on_in"), 16)
            sp.dma_start(om_s[DS * b:DS * b + DS], omD[32 * b:32 * b + 32, :].rearrange("(h s) d -> s h d", s=DS)).then_inc(S("on_in"), 16)

    def store_pair(sp, p):
        sp.wait_ge(S("s_o"), p + 1)
        sp.dma_start(oD[128 * p:128 * p + 128, :], OSp[p % 2][:].rearrange("p r d -> p (r d)")).then_inc(S("o_out"), 16)

    def pool_sample(pool):
        ch = Link(pool, S("s_pool"))
        pool.wait_ge(S("p_tr"), len(p_chunks))
        pool.wait_ge(S("p_pv"), len(p_index))
        pool.wait_ge(S("p_norm"), P_DONE)
        pool.wait_ge(S("p_mix"), QT)
        pool.memset(QP[:], 0.0).then_inc(S("s_zero"), 1)
        pool.memset(QM[:], 0.0).then_inc(S("s_zero"), 1)
        pool.memset(pp[:], 0.0).then_inc(S("s_zero"), 1)
        pool.memset(rs3[:], 1.0).then_inc(S("s_zero"), 1)
        pool.wait_ge(S("on_in"), 16 * 2 * NDB)
        pool.wait_ge(S("s_z"), 64)
        g = gs[:].rearrange("p (r h o) -> p h r o", r=3, o=1).to_broadcast([NS_TOK, 8, 3, HD])
        ch.step(pool.tensor_tensor(on_s[:], on_s[:], g, ALU.mult))
        pool_mix(pool, ch, NS_TOK, on_s, om_s[:], OC[0:NS_TOK, QT], zs, ms, "s_mix")

    def pe_sample(pe):
        pe.wait_ge(S("s_const"), 96)
        pe.wait_ge(S("pt_dve"), chunks_final_dve(len(p_chunks) - 1))
        pe.wait_ge(S("pt_act"), chunks_before(len(p_chunks), chunk_act))
        pe.wait_ge(S("p_exp"), SM * QT)
        pe.wait_ge(S("p_norm"), P_DONE)
        for g in range(4):
            l = nc.tensor.transpose(bank(0)[:, 64 * g:64 * g + 64], qs[:, g], ident[0:64, 0:64])
        for pr in range(2):
            l = nc.tensor.transpose(bank(1)[:, 64 * pr:64 * pr + 64], qms[:, 128 * pr:128 * pr + 128], ident[0:64, 0:64])
        for br in range(2):
            l = nc.tensor.transpose(bank(1)[:, 128 + 64 * br:192 + 64 * br], kvn[:, 256 * br:256 * br + 128], ident[0:64, 0:64])
        l.then_inc(S("s_qtr"), 1)

        def m_keys(b):
            pe.wait_ge(S(f"m_in{b // 4}"), 64)
            if b >= 2:
                pe.wait_ge(S("m_kt"), b - 1)
            for pr in range(2):
                for mt in range(2):
                    l = nc.tensor.transpose(bank(2 + b % 2)[:, 256 * pr + 128 * mt:256 * pr + 128 * mt + 128], MK[b // 4][:, b % 4, mt, 128 * pr:128 * pr + 128], ident[:])
            l.then_inc(S("m_ktr"), 1)

        for g in range(2):
            for b in range(4 * g, 4 * g + 4):
                m_keys(b)
            pe.wait_ge(S("s_q"), 1)
            pe.wait_ge(S("m_kt"), 4 * g + 4)
            for b in range(4 * g, 4 * g + 4):
                for pr in range(2):
                    l = nc.tensor.matmul(bank(4 + g, 256), QM[:, pr, b, :], KTm[:, b % 4, pr, :], start=b == 4 * g and pr == 0, stop=b == 4 * g + 3 and pr == 1)
            l.then_inc(S("m_qk"), 1)
            pe.wait_ge(S("m_exp"), g + 1)
            for mt in range(2):
                l = nc.tensor.transpose(bank(6)[:, 128 * mt:128 * mt + 128], PM[:, 128 * mt:128 * mt + 128], ident[:])
            l.then_inc(S("m_tr"), 1)
            pe.wait_ge(S("m_pt"), g + 1)
            if g == 1:
                pe.wait_ge(S("m_o"), 1)
            for b in range(4):
                for mt in range(2):
                    l = nc.tensor.matmul(psum[32 * b:32 * b + 32, 512 * 7:512 * 7 + 256], PTS[:, mt, 32 * b:32 * b + 32], MK[g][:, b, mt, 256:512], start=mt == 0, stop=mt == 1)
            l.then_inc(S("m_pv"), 1)
        pe.wait_ge(S("m_o"), 2)

        for p in range(NPAIR):
            pair = (2 * p, 2 * p + 1)
            if p >= 1:
                pe.wait_ge(S("s_o"), p)
                pe.wait_ge(S("s_exp"), 3 * p)
            c_out = psum[:, 512 * 7 + 384:512 * 7 + 447]
            for b in pair:
                l = nc.tensor.matmul(c_out, QP[:, b, :], KCs[:, b, 0:63], start=b == pair[0], stop=b == pair[1])
            l.then_inc(S("s_qk"), 1)
            pe.wait_ge(S(f"s_in{p % 2}"), 16 * (2 * NPG + 2) * (p // 2 + 1))
            for c in range(6):
                i = (6 + NSC) * p + c
                wait_ring(pe, i - 2)
                for j in range(4):
                    src = SG[p % 2][:, c // 2, 4 * (c % 2) + j, 0:128] if c < 4 else WG[p % 2][:, c - 4, j, 0:128]
                    l = nc.tensor.transpose(bank(5 + i % 2)[:, 128 * j:128 * j + 128], src, ident[:])
                l.then_inc(S("s_tr"), 1)
            wait_ring(pe, (6 + NSC) * p + 4)
            wait_ring(pe, (6 + NSC) * p + 5)
            for b in pair:
                nc.tensor.matmul(bank(3), QP[:, b, :], KTw[:, b % 2, :], start=b == pair[0], stop=False)
            nc.tensor.matmul(bank(3, 8), identb[:], maskb[:, M_WINH:M_WINH + 8], start=False, stop=True)
            for b in pair:
                nc.tensor.matmul(bank(4, 64), QP[:, b, :], KTn[:, 1, :], start=b == pair[0], stop=False)
            nc.tensor.matmul(bank(4, 64), identb[:], maskb[:, M_NEW + 64 * p:M_NEW + 64 * p + 64], start=False, stop=True).then_inc(S("s_qk"), 1)
            pe.wait_ge(S("s_pcn"), p + 1)
            nc.tensor.matmul(psum[:, 512 * 7 + 448:512 * 7 + 511], csum[:], PC[:, 0:63], start=True, stop=True).then_inc(S("s_imp"), 1)
            for a in range(2):
                for b in pair:
                    nc.tensor.matmul(bank(a), QP[:, b, :], KTs[:, b % 2, 512 * a:512 * a + 512], start=b == pair[0], stop=b == pair[1])
            for b in pair:
                nc.tensor.matmul(bank(2, 64), QP[:, b, :], KTn[:, 0, :], start=b == pair[0], stop=False)
            nc.tensor.matmul(bank(2, 64), identb[:], maskb[:, M_NEW + 64 * p:M_NEW + 64 * p + 64], start=False, stop=True).then_inc(S("s_qk"), 1)
            for n, c in enumerate((2, 3, 0, 1)):
                i = (6 + NSC) * p + 6 + n
                wait_ring(pe, i - 2)
                pe.wait_ge(S("s_exp"), 3 * p + (2 if n == 0 else 3))
                for j, (k, w) in enumerate(S_CHUNKS[c]):
                    l = nc.tensor.transpose(bank(5 + i % 2)[0:w, 128 * j:128 * j + 128], s_prob(k, w), ident[:])
                l.then_inc(S("s_tr"), 1)
            wait_ring(pe, (6 + NSC) * p + 8)
            wait_ring(pe, (6 + NSC) * p + 9)
            pe.wait_ge(S("s_sel"), p + 1)
            for b in range(2):
                rows = slice(64 * b, 64 * b + 64)
                o = lambda br: psum[rows, 512 * 7 + 128 * br:512 * 7 + 128 * br + 128]
                q = lambda k, w=128: PTS[0:w, k, rows]
                nc.tensor.matmul(o(0), q(T_CMP, 63), VC[0:63, pair[b], :], start=True, stop=True)
                for k in range(NPG):
                    nc.tensor.matmul(o(1), q(k), SG[p % 2][:, b, k, 128:256], start=k == 0, stop=False)
                nc.tensor.matmul(o(1), q(T_NEWS, 64), kvn[:, 128:256], start=False, stop=True)
                for k in range(4):
                    nc.tensor.matmul(o(2), q(8 + k), WG[p % 2][:, b, k, 128:256], start=k == 0, stop=False)
                l = nc.tensor.matmul(o(2), q(T_NEWW, 64), kvn[:, 384:512], start=False, stop=True)
            l.then_inc(S("s_pv"), 1)
        pe.wait_ge(S("s_mix"), 1)
        for g in range(2):
            for k in range(4):
                l = nc.tensor.transpose(bank(g)[:, 64 * k:64 * k + 64], ms[:, 128 * (4 * g + k):128 * (4 * g + k) + 128], ident[0:64, 0:64])
            l.then_inc(S("s_xtr"), 1)

    def wait_ring(eng, i):
        if i >= 0:
            eng.wait_ge(S("s_ring_dve") if i % 2 else S("s_ring_act"), i // 2 + 1)

    def s_prob(k, w):
        if k < 8:
            return PSl[:, 128 * k:128 * k + w]
        if k < 12:
            return PW[:, 128 * (k - 8):128 * (k - 8) + w]
        return {T_NEWS: PSl[:, 1024:1088], T_NEWW: PW[:, 512:576], T_CMP: PC[:, 0:63]}[k]

    def ring_copy(eng, copy, i, sem):
        p, c = i // (6 + NSC), i % (6 + NSC)
        eng.wait_ge(S("s_tr"), i + 1)
        src = bank(5 + i % 2)
        if c < 6:
            if p >= 1:
                eng.wait_ge(S("s_qk"), 3 * p)
            dst = KTs[:, c // 2, 512 * (c % 2):512 * (c % 2) + 512] if c < 4 else KTw[:, c - 4, :]
            copy(dst, src).then_inc(sem, 1)
            return
        if p >= 1:
            eng.wait_ge(S("s_pv"), p)
        part = S_CHUNKS[(2, 3, 0, 1)[c - 6]]
        w = part[-1][1] if part[-1][1] == 128 else 64
        if w == 128:
            copy(PTS[:, part[0][0]:part[0][0] + 4, :], src.rearrange("p (j c) -> p j c", j=4)).then_inc(sem, 1)
        else:
            i1 = copy(PTS[0:64, T_NEWS:T_NEWS + 2, :], src[0:64, 0:256].rearrange("p (j c) -> p j c", j=2))
            i1.then_inc(S("s_part"), 1)
            copy(PTS[0:63, T_CMP, :], src[0:63, 256:384]).then_inc(sem, 1)

    def s_scores(j):
        return [psum[:, 512 * 7 + 384:512 * 7 + 447], psum[:, 512 * 3:512 * 3 + 576], psum[:, 0:1088]][j]

    def act_sample(act):
        act.wait_ge(S("s_qtr"), 1)
        act.wait_ge(S("s_zero"), 4)
        for kv in range(2):
            rows = slice(64 * kv, 64 * kv + 64)
            for par in range(2):
                c0 = 64 * par + 32 * kv
                nc.scalar.copy(QP[rows, par::2, c0:c0 + 32].rearrange("p b (g s) -> p b g s", g=4),
                               psum[rows, 0:256].rearrange("p (g b s) -> p b g s", g=4, b=NDB)[:, par::2]).then_inc(S("s_qpart"), 1)
        for r in range(2):
            rows = slice(64 * r, 64 * r + 64)
            for pr in range(2):
                for c in range(4):
                    c0 = 32 * c + 8 * (2 * pr + r)
                    nc.scalar.copy(QM[rows, pr, c::4, c0:c0 + 8],
                                   psum[rows, 512 + 64 * pr:576 + 64 * pr].rearrange("p (b s) -> p b s", b=NDB)[:, c::4]).then_inc(S("s_qpart"), 1)
        nc.scalar.copy(KTn[:], psum[:, 640:768].rearrange("p (r c) -> p r c", r=2)).then_inc(S("s_q"), 1)
        for g in range(2):
            act.wait_ge(S("m_nb"), g + 1)
            if g == 1:
                act.wait_ge(S("m_tr"), 1)
            nc.scalar.activation(PM[:], bank(4 + g, 256), ACT.Exp, bias=snb[:, g:g + 1], scale=SCALE, accum_out=ssm[:, g:g + 1]).then_inc(S("m_exp"), 1)
            act.wait_ge(S("m_tr"), g + 1)
            if g == 1:
                act.wait_ge(S("m_pv"), 1)
            nc.scalar.copy(PTS[:, 0:2, :], bank(6, 256).rearrange("p (j c) -> p j c", j=2)).then_inc(S("m_pt"), 1)
        for p in range(NPAIR):
            base = (6 + NSC) * p

            def exp(j):
                act.wait_ge(S("s_nb"), 3 * p + j + 1)
                if p >= 1:
                    act.wait_ge(S("s_pv"), p)
                dst = (PC[:, 0:63], PW[:], PSl[:])[j]
                nc.scalar.activation(dst, s_scores(j), ACT.Exp, bias=snb[:, 4 + j:5 + j], scale=SCALE, accum_out=ssm[:, 4 + j:5 + j]).then_inc(S("s_exp"), 1)

            exp(0)
            for c in range(0, 6, 2):
                ring_copy(act, nc.scalar.copy, base + c, S("s_ring_act"))
            exp(1)
            exp(2)
            for c in range(6, 6 + NSC, 2):
                ring_copy(act, nc.scalar.copy, base + c, S("s_ring_act"))
        for g in range(2):
            act.wait_ge(S("s_xtr"), g + 1)
            nc.scalar.copy(xhi[:, 4 * g:4 * g + 4, T:T + NS_TOK], bank(g, 256).rearrange("p (k c) -> p k c", k=4)).then_inc(S("s_xhi"), 1)

    def dve_sample(dve):
        ch = Link(dve, S("s_dve"))
        dve.wait_ge(S("s_zero"), 4)
        for g in range(2):
            for b in range(4 * g, 4 * g + 4):
                dve.wait_ge(S("m_ktr"), b + 1)
                if g == 1:
                    dve.wait_ge(S("m_qk"), 1)
                nc.vector.tensor_copy(KTm[:, b % 4], bank(2 + b % 2).rearrange("p (r m) -> p r m", r=2)).then_inc(S("m_kt"), 1)
            dve.wait_ge(S("m_qk"), g + 1)
            ch.step(nc.vector.tensor_reduce(out=smx[:, g:g + 1], in_=bank(4 + g, 256), op=ALU.max, axis=AX.X))
            nc.vector.tensor_scalar(snb[:, g:g + 1], smx[:, g:g + 1], -SCALE, None, ALU.mult).then_inc(S("m_nb"), 1)
            dve.wait_ge(S("m_pv"), g + 1)
            ch.step(nc.vector.reciprocal(ssm[:, 2 + g:3 + g], ssm[:, g:g + 1]))
            o = bank(7, 256).rearrange("p (h d) -> p h d", h=4)
            t = OMs[:, g, :]
            ch.step(nc.vector.tensor_scalar(t, o[:, 0], colc[:, 6:7], None, ALU.mult))
            for h in range(1, 4):
                ch.step(nc.vector.scalar_tensor_tensor(out=t, in0=o[:, h], scalar=colc[:, 6 + h:7 + h], in1=t, op0=ALU.mult, op1=ALU.add))
            nc.vector.tensor_scalar(t, t, ssm[:, 2 + g:3 + g], None, ALU.mult).then_inc(S("m_o"), 1)
        for p in range(NPAIR):
            base = (6 + NSC) * p

            def top(j):
                dve.wait_ge(S("s_qk"), 3 * p + j + 1)
                ch.step(nc.vector.tensor_reduce(out=smx[:, 4 + j:5 + j], in_=s_scores(j), op=ALU.max, axis=AX.X))
                if p >= 1:
                    dve.wait_ge(S("s_exp"), 3 * p)
                nc.vector.tensor_scalar(snb[:, 4 + j:5 + j], smx[:, 4 + j:5 + j], -SCALE, None, ALU.mult).then_inc(S("s_nb"), 1)
                dve.wait_ge(S("s_nb"), 3 * p + j + 1)

            top(0)
            for c in range(1, 6, 2):
                ring_copy(dve, nc.vector.tensor_copy, base + c, S("s_ring_dve"))
            dve.wait_ge(S("s_exp"), 3 * p + 1)
            ch.step(nc.vector.reciprocal(ssm[:, 8:9], ssm[:, 4:5]))
            nc.vector.tensor_scalar(PC[:, 0:63], PC[:, 0:63], ssm[:, 8:9], None, ALU.mult).then_inc(S("s_pcn"), 1)
            top(1)
            dve.wait_ge(S("s_imp"), p + 1)
            ch.step(nc.vector.tensor_copy(pp[:, 1:64], psum[:, 512 * 7 + 448:512 * 7 + 511]))
            ch.step(nc.vector.tensor_reduce(out=sc[:, 0], in_=pp[:, 4:60].rearrange("p (n r) -> p n r", r=4), op=ALU.add, axis=AX.X))
            ch.step(nc.vector.tensor_tensor(sc[:, 0], sc[:, 0], pp[:, 8:64].rearrange("p (n r) -> p n r", r=4)[:, :, 0], ALU.add))
            ch.step(nc.vector.tensor_reduce(out=smx[:, 8:9], in_=sc[:, 0], op=ALU.min, axis=AX.X))
            ch.step(nc.vector.tensor_scalar(sc[:, 1], sc[:, 0], smx[:, 8:9], None, ALU.is_equal))
            ch.step(nc.vector.tensor_tensor(sc[:, 1], sc[:, 1], cblk[:], ALU.mult))
            ch.step(nc.vector.tensor_reduce(out=smx[:, 9:10], in_=sc[:, 1], op=ALU.max, axis=AX.X))
            nc.vector.tensor_scalar(sc[:, 2], cblk[:], smx[:, 9:10], NEG, ALU.is_equal, ALU.mult).then_inc(S("s_sel"), 1)
            dve.wait_ge(S("s_sel"), p + 1)
            dve.wait_ge(S("s_qk"), 3 * p + 3)
            blocks = psum[:, 64:960].rearrange("p (n c) -> p n c", c=64)
            ch.step(nc.vector.tensor_tensor(blocks, blocks, sc[:, 2].rearrange("p (n o) -> p n o", o=1).to_broadcast([128, 14, 64]), ALU.add))
            top(2)
            for c in range(7, 6 + NSC, 2):
                ring_copy(dve, nc.vector.tensor_copy, base + c, S("s_ring_dve"))
            dve.wait_ge(S("s_exp"), 3 * p + 3)
            ch.do(nc.vector.reciprocal(rs3[:, 1:2], ssm[:, 6:7]))
            ch.do(nc.vector.reciprocal(rs3[:, 2:3], ssm[:, 5:6]))
            ch.wait()
            dve.wait_ge(S("s_pv"), p + 1)
            if p >= 2:
                dve.wait_ge(S("o_out"), 16 * (p - 1) + 32)
            o = bank(7, 384).rearrange("p (r k d) -> p r k d", r=3, k=2)
            t = OSp[p % 2]
            ch.step(nc.vector.tensor_scalar(t[:], o[:, :, 0], colc[:, 4:5], None, ALU.mult))
            ch.step(nc.vector.scalar_tensor_tensor(out=t[:], in0=o[:, :, 1], scalar=colc[:, 5:6], in1=t[:], op0=ALU.mult, op1=ALU.add))
            nc.vector.tensor_tensor(t[:], t[:], rs3[:].rearrange("p (r o) -> p r o", o=1).to_broadcast([128, 3, HD]), ALU.mult).then_inc(S("s_o"), 1)
            dve.wait_ge(S("s_o"), p + 1)
        for g in range(2):
            dve.wait_ge(S("s_xhi"), g + 1)
            dst = (slice(None), slice(4 * g, 4 * g + 4), slice(T, T + NS_TOK))
            nc.vector.tensor_tensor(xlo[dst], bank(g, 256).rearrange("p (k c) -> p k c", k=4), xhi[dst].bitcast(F32), ALU.subtract).then_inc(S("s_xlo"), 1)

    OUT_W = (MEMJ + 1, MEMJ + 2)

    def sp_out(sp):
        sp.wait_ge(S("s_mix"), 1)
        sp.wait_ge(S("s_xlo"), 2)
        sp.dma_start(gf[:], io["ln_final"].rearrange("(o n) -> o n", o=1).to_broadcast([128, D])).then_inc(S("d_const"), 16)
        load_w(sp, OUT_W[0])
        for t in range(2):
            sp.dma_start(xr[t][0:tile_rows(t)], x_rows[t]).then_inc(S(f"d_x{t}"), 16)
        load_w(sp, OUT_W[1])
        for t in range(NT):
            r = tile_rows(t)
            sp.wait_ge(S("d_y"), t + 1)
            dst = io["y_prompt"][0, 128 * t:128 * t + 128, :] if t < QT else io["y_sample"].rearrange("b s d -> (b s) d")
            sp.dma_start(dst, yo[t % 2][0:r]).then_inc(S(f"y_out{t % 2}"), 16)
            if t + 2 < NT:
                sp.dma_start(xr[t % 2][0:tile_rows(t + 2)], x_rows[t + 2]).then_inc(S(f"d_x{t % 2}"), 16)
        for i in range(2):
            sp.wait_ge(S(f"y_out{i}"), 16 * len(range(i, NT, 2)))

    def pe_out(pe):
        pe.wait_ge(S("s_xlo"), 2)
        for jj, w in enumerate(OUT_W):
            pe.wait_ge(S("w_split"), 2 * w + 2)
        for t in range(NT):
            r = tile_rows(t)
            if t >= 4:
                pe.wait_ge(S("d_sum"), t - 3)
            for jj, w in enumerate(OUT_W):
                o = 512 * (2 * (t % 4) + jj)
                for k in range(KT):
                    l = mm3(psum[0:r, o:o + 512], w % 2, k, 512, tile_col(t), r, k == 0, k == KT - 1)
            l.then_inc(S("d_mm"), 1)

    def act_out(act):
        for w in OUT_W:
            split_w_hi(act, w)
        for t in range(NT):
            r = tile_rows(t)
            act.wait_ge(S("d_sum"), t + 1)
            if t >= 2:
                act.wait_ge(S(f"y_out{t % 2}"), 16 * (t // 2))
            nc.scalar.activation(yo[t % 2][0:r], yt[t % 2][0:r], ACT.Square, accum_out=small[0:r, t:t + 1]).then_inc(S("d_ss"), 1)
            act.wait_ge(S("d_ms"), t + 1)
            nc.scalar.activation(small[0:r, 32 + t:33 + t], small[0:r, 16 + t:17 + t], ACT.Sqrt).then_inc(S("d_sd"), 1)

    def dve_out(dve):
        ch = Link(dve, S("d_dve"))
        for w in OUT_W:
            split_w_lo(dve, w)
        dve.wait_ge(S("d_const"), 16)
        for t in range(NT):
            r = tile_rows(t)
            dve.wait_ge(S("d_mm"), t + 1)
            dve.wait_ge(S(f"d_x{t % 2}"), 16 * (t // 2 + 1))
            o = 1024 * (t % 4)
            nc.vector.tensor_tensor(yt[t % 2][0:r], psum[0:r, o:o + 1024], xr[t % 2][0:r], ALU.add).then_inc(S("d_sum"), 1)
            dve.wait_ge(S("d_ss"), t + 1)
            v = small[0:r, 16 + t:17 + t]
            nc.vector.tensor_scalar(v, small[0:r, t:t + 1], 1.0 / D, EPS, ALU.mult, ALU.add).then_inc(S("d_ms"), 1)
            dve.wait_ge(S("d_sd"), t + 1)
            y = small[0:r, 48 + t:49 + t]
            ch.step(nc.vector.reciprocal(y, small[0:r, 32 + t:33 + t]))
            rsqrt_polish(dve, ch, y, v, small[0:r, 64 + t:65 + t])
            nc.vector.scalar_tensor_tensor(out=yo[t % 2][0:r], in0=yt[t % 2][0:r], scalar=y, in1=gf[0:r], op0=ALU.mult, op1=ALU.mult).then_inc(S("d_y"), 1)
            dve.wait_ge(S("d_y"), t + 1)

    with nc.Block() as block:

        @block.sync
        def _(sp):
            n_c = 0
            for dst, src in ((ident[:], io["c_ident"]), (colc[:], io["c_col"]), (pt[:], io["page_table"].rearrange("b p -> (b p)").rearrange("(a n) -> a n", a=1)),
                             (gb[:, 0, :], io["ln_mix"].to_broadcast([128, D])), (gb[:, 1, :], io["ln_mem"].to_broadcast([128, D]))):
                sp.dma_start(dst, src).then_inc(S("const_in"), 16)
            load_w(sp, 0)
            for n in range(NT + 2):
                if n >= 2:
                    sp.wait_ge(S("x_scaled"), n - 1)
                sp.dma_start(xraw[n % 2][0:tile_rows(n), :], x_rows[n]).then_inc(S(f"x_in{n % 2}"), 16)
            if on("B"):
                for j in range(1, MEMJ + 1):
                    load_w(sp, j)
                    if j == 3:
                        sp.wait_ge(S("x_tr"), 2 * (NT + 2))
                        load_gather(sp, 0)
                load_w1(sp)
                sp.dma_start(io["new_win_s"][0, :, 0:WIN - DS].rearrange("b t a k d -> b (t a k d)"),
                             io["cache_nsa_win"][0, :, DS:WIN].rearrange("b t a k d -> b (t a k d)")).then_inc(S("out_done"), 16)
                wait_h(sp)
                kv = lambda c: hD[0:T, c:c + 256]
                kvs = lambda c: hD[T:T + NS_TOK, c:c + 256]
                fl = "t a k d -> t (a k d)"
                for dst, c in ((io["new_cmp_p"], C_KVC), (io["new_slc_p"], C_KVS)):
                    sp.dma_start(dst[0, 0].rearrange(fl), kv(c)).then_inc(S("out_done"), 16)
                sp.dma_start(io["new_win_p"][0, 0].rearrange(fl), kv(C_KVW)[T - WIN:T]).then_inc(S("out_done"), 16)
                for dst, c in ((io["new_cmp_s"], C_KVC), (io["new_slc_s"], C_KVS)):
                    sp.dma_start(dst[0].rearrange("b t a k d -> (b t) (a k d)"), kvs(c)).then_inc(S("out_done"), 16)
                sp.dma_start(io["new_win_s"][0, :, WIN - DS:WIN].rearrange("b t a k d -> b t (a k d)"),
                             kvs(C_KVW).rearrange("(b t) n -> b t n", b=NDB)).then_inc(S("out_done"), 16)
            n_out = 7 if on("B") else 0
            if on("R"):
                sp_compress_retention(sp)
                n_out += 2 + 4
            if on("P"):
                sp_prompt(sp)
            if on("S"):
                sp_sample(sp)
            if on("D"):
                sp_out(sp)
            sp.wait_ge(S("out_done"), 16 * n_out)

        @block.tensor
        def _(pe):
            pe.wait_ge(S("const_in"), 80)
            for n in range(NT + 2):
                r = tile_rows(n)
                pe.wait_ge(S("x_scaled"), n + 1)
                for g in range(2):
                    i = 2 * n + g
                    if i >= 4:
                        pe.wait_ge(S("x_lo"), i - 3)
                    for k in range(4):
                        l = nc.tensor.transpose(bank(i % 4)[:, 128 * k:128 * k + r], xs[0][0:r, 128 * (4 * g + k):128 * (4 * g + k) + 128], ident[0:r, 0:r])
                    l.then_inc(S("x_tr"), 1)
            if on("B"):
                pe.wait_ge(S("x_lo"), 2 * (NT + 2))
                for q, (j, t) in enumerate(proj_jobs):
                    if q == 0 or proj_jobs[q - 1][0] != j:
                        pe.wait_ge(S("w_split"), 2 * j + 2)
                    if q >= 8:
                        wait_evac(pe, q - 8)
                    r, n = tile_rows(t), w_n[j]
                    for k in range(KT):
                        l = mm3(psum[0:r, 512 * (q % 8):512 * (q % 8) + n], j % 2, k, n, tile_col(t), r, k == 0, k == KT - 1)
                    l.then_inc(S("h_mm"), 1)
            if on("R"):
                pe_compress_retention(pe)
            if on("P"):
                pe_prompt(pe)
            if on("S"):
                pe_sample(pe)
            if on("D"):
                pe_out(pe)

        @block.scalar
        def _(act):
            def hi(n):
                for g in range(2):
                    act.wait_ge(S("x_tr"), 2 * n + g + 1)
                    nc.scalar.copy(xhi[:, 4 * g:4 * g + 4, tile_col(n):tile_col(n) + tile_rows(n)], x_src(n, g)).then_inc(S("x_hi"), 1)

            split_done = 0
            for n in range(NT + 2):
                r = tile_rows(n)
                act.wait_ge(S(f"x_in{n % 2}"), 16 * (n // 2 + 1))
                if n >= 1:
                    act.wait_ge(S("x_tr"), 2 * n)
                nc.scalar.activation(xs[0][0:r, :], xraw[n % 2][0:r, :], ACT.Square, accum_out=small[0:r, n:n + 1]).then_inc(S("x_ss"), 1)
                act.wait_ge(S("x_ms"), n + 1)
                nc.scalar.activation(small[0:r, 32 + n:33 + n], small[0:r, 16 + n:17 + n], ACT.Sqrt).then_inc(S("x_sd"), 1)
                if n == 0:
                    split_w_hi(act, 0)
                if n >= 1:
                    hi(n - 1)
            hi(NT + 1)
            if on("B"):
                act.wait_ge(S("w_in0"), 16)
                split_w_hi(act, 1)
                for q, (j, t) in enumerate(proj_jobs):
                    if t == 2 and j >= 1 and j + 1 <= MEMJ:
                        split_w_hi(act, j + 1)
                    if not by_act(j):
                        continue
                    r = tile_rows(t)
                    act.wait_ge(S("h_mm"), q + 1)
                    if q >= HST:
                        act.wait_ge(S(f"h_out{q % HST}"), 16 * (q // HST))
                    src, dst = psum[0:r, 512 * (q % 8):512 * (q % 8) + 512], hst[q % HST][0:r]
                    if j == 2:
                        nc.scalar.copy(dst[:, 0:256], src[:, 0:256]).then_inc(S("h_part"), 1)
                        nc.scalar.activation(dst[:, 256:280], src[:, 256:280], ACT.Sigmoid).then_inc(S("h_evac_act"), 1)
                    elif j == 3:
                        nc.scalar.activation(dst, src, ACT.Silu).then_inc(S("h_evac_act"), 1)
                    else:
                        nc.scalar.copy(dst[:, 0:256], src[:, 0:256]).then_inc(S("h_part"), 1)
                        nc.scalar.activation(dst[:, 256:512], src[:, 256:512], ACT.Silu).then_inc(S("h_evac_act"), 1)
            if on("R"):
                act_compress_retention(act)
            if on("P"):
                act_prompt(act)
            if on("S"):
                act_sample(act)
            if on("D"):
                act_out(act)

        @block.vector
        def _(dve):
            def lo(n):
                for g in range(2):
                    dve.wait_ge(S("x_hi"), 2 * n + g + 1)
                    cs = slice(tile_col(n), tile_col(n) + tile_rows(n))
                    nc.vector.tensor_tensor(xlo[:, 4 * g:4 * g + 4, cs], x_src(n, g), xhi[:, 4 * g:4 * g + 4, cs].bitcast(F32), ALU.subtract).then_inc(S("x_lo"), 1)

            ch = Link(dve, S("x_dve"))
            dve.wait_ge(S("const_in"), 80)
            nc.vector.tensor_copy(identb[:], ident[:]).then_inc(S("identb"), 1)
            for n in range(NT + 2):
                r = tile_rows(n)
                dve.wait_ge(S("x_ss"), n + 1)
                nc.vector.tensor_scalar(small[0:r, 16 + n:17 + n], small[0:r, n:n + 1], 1.0 / D, EPS, ALU.mult, ALU.add).then_inc(S("x_ms"), 1)
                dve.wait_ge(S("x_sd"), n + 1)
                nc.vector.reciprocal(small[0:r, 48 + n:49 + n], small[0:r, 32 + n:33 + n]).then_inc(S("x_rs"), 1)
                dve.wait_ge(S("x_rs"), n + 1)
                rsqrt_polish(dve, ch, small[0:r, 48 + n:49 + n], small[0:r, 16 + n:17 + n], small[0:r, 64 + n:65 + n])
                nc.vector.scalar_tensor_tensor(out=xs[0][0:r, :], in0=xraw[n % 2][0:r, :], scalar=small[0:r, 48 + n:49 + n],
                                               in1=gb[0:r, int(n >= NT), :], op0=ALU.mult, op1=ALU.mult).then_inc(S("x_scaled"), 1)
                if n == 0:
                    split_w_lo(dve, 0)
                if n >= 1:
                    lo(n - 1)
            lo(NT + 1)
            if on("B"):
                split_w_lo(dve, 1)
                for q, (j, t) in enumerate(proj_jobs):
                    if t == 2 and j >= 1 and j + 1 <= MEMJ:
                        split_w_lo(dve, j + 1)
                    if by_act(j):
                        continue
                    r = tile_rows(t)
                    dve.wait_ge(S("h_mm"), q + 1)
                    if q >= HST:
                        dve.wait_ge(S(f"h_out{q % HST}"), 16 * (q // HST))
                    nc.vector.tensor_copy(hst[q % HST][0:r, :], psum[0:r, 512 * (q % 8):512 * (q % 8) + 512]).then_inc(S("h_evac_dve"), 1)
            if on("R"):
                dve_compress_retention(dve)
            if on("P"):
                dve_prompt(dve)
            if on("S"):
                dve_sample(dve)
            if on("D"):
                dve_out(dve)

        @block.gpsimd
        def _(pool):
            if on("B"):
                for q, (j, t) in enumerate(proj_jobs):
                    r, n = tile_rows(t), w_n[j]
                    wait_evac(pool, q)
                    if j == MEMJ:
                        dst = new_mem[128 * (t - NT):128 * (t - NT) + 128, :]
                    else:
                        dst = hD[128 * t:128 * t + r, CHUNKS[j][0]:CHUNKS[j][0] + n]
                    pool.dma_start(dst, hst[q % HST][0:r, 0:n]).then_inc(S(f"h_out{q % HST}"), 16)
            if on("R"):
                pool_compress_retention(pool)
            if on("P"):
                pool_prompt(pool)
            if on("S"):
                pool_sample(pool)



_OUTS = [("y_prompt", (1, T, D)), ("y_sample", (NDB, DS, D)),
         ("new_cmp_p", (1, 1, T, 2, 2, HD)), ("new_cmp_s", (1, NDB, DS, 2, 2, HD)),
         ("new_slc_p", (1, 1, T, 2, 2, HD)), ("new_slc_s", (1, NDB, DS, 2, 2, HD)),
         ("new_win_p", (1, 1, WIN, 2, 2, HD)), ("new_win_s", (1, NDB, WIN, 2, 2, HD)),
         ("new_ret_p", (1, 1, 4, HD, HD)), ("new_ret_s", (1, NDB, 4, HD, HD)),
         ("new_mem", (1, 1, NM, 2, 4, HD))]


def kernel(**inputs):
    import concourse.bacc as bacc
    from concourse.bass_utils import run_bass_kernel_spmd

    nc = bacc.Bacc("TRN2", target_bir_lowering=False, num_devices=1)
    arrays, io = {}, {}
    for name, a in {**inputs, **constants()}.items():
        a = np.ascontiguousarray(a)
        arrays[f"in_{name}"] = a
        io[name] = nc.dram_tensor(f"in_{name}", a.shape, mybir.dt.from_np(a.dtype), kind="ExternalInput").ap()
    for name, shape in _OUTS:
        io[name] = nc.dram_tensor(f"out_{name}", shape, F32, kind="ExternalOutput").ap()
    build(nc, io)
    r = run_bass_kernel_spmd(nc, [arrays], core_ids=[0])
    return tuple(r.results[0][f"out_{name}"] for name, _ in _OUTS)
```
